# Optimizing a Trainium2 kernel written in Bass

```python
import math
import jax
import jax.numpy as jnp
from jax import lax
import numpy as np
import jax, jax.numpy as jnp

D_MODEL = 1024
BATCH = 1
SEQ = 512
DEPTH = 2

N_MIXERS = 2
N_SUBLAYERS = 3
ATTN_HEADS = 8
ATTN_HEAD_DIM = D_MODEL // (2 * ATTN_HEADS)
ATTN_V_DIM = 2 * ATTN_HEAD_DIM
Q_BLOCK = 128
NUM_BUCKETS = 32
MAX_DISTANCE = 128
HGRN_EXPAND = 128
HGRN_HEADS = D_MODEL // HGRN_EXPAND
HGRN_FORGET_DIM = HGRN_HEADS * HGRN_EXPAND
HGRN_HEAD_V = D_MODEL // HGRN_HEADS
HGRN_CHUNK = 64
D_FF = 2816
N_ATTN_LAYERS = (DEPTH + 1) // 2
N_HGRN_LAYERS = DEPTH // 2
EPS = 1e-6


def rms_norm(h, gain):
    h32 = h.astype(jnp.float32)
    h32 = h32 * lax.rsqrt(jnp.mean(h32 * h32, axis=-1, keepdims=True) + EPS)
    return (h32 * gain.astype(jnp.float32)).astype(h.dtype)

def t5_causal_bucket(dist):
    max_exact = NUM_BUCKETS // 2
    d = jnp.maximum(dist, 0)
    d_f = jnp.maximum(d, 1).astype(jnp.float32)
    large = max_exact + (jnp.log(d_f / max_exact) / math.log(MAX_DISTANCE / max_exact)
                         * (NUM_BUCKETS - max_exact)).astype(jnp.int32)
    large = jnp.minimum(large, NUM_BUCKETS - 1)
    return jnp.where(d < max_exact, d, large)

def swiglu(h, w_in, w_down):
    a, b = jnp.split(h @ w_in, 2, axis=-1)
    return (jax.nn.silu(a) * b) @ w_down

def diff_attention(h, w_qkv, w_o, q_gain, k_gain, lam, subln_gain, rel_bias, layer_idx):
    B, S, _ = h.shape
    H, hd, dv = ATTN_HEADS, ATTN_HEAD_DIM, ATTN_V_DIM
    q, k, v = jnp.split(h @ w_qkv, 3, axis=-1)
    q = rms_norm(q.reshape(B, S, H, 2, hd), q_gain) * (hd ** -0.5)
    k = rms_norm(k.reshape(B, S, H, 2, hd), k_gain)
    v = v.reshape(B, S, H, dv)
    lambda_init = 0.8 - 0.6 * math.exp(-0.3 * layer_idx)
    lam32 = lam.astype(jnp.float32)
    lam_full = (jnp.exp(jnp.sum(lam32[0] * lam32[1])) - jnp.exp(jnp.sum(lam32[2] * lam32[3]))
                + lambda_init)
    kt = k.transpose(0, 2, 3, 1, 4)
    vt = v.transpose(0, 2, 1, 3)
    nb = S // Q_BLOCK
    qb = q.reshape(B, nb, Q_BLOCK, H, 2, hd).transpose(1, 0, 3, 4, 2, 5)
    k_pos = jnp.arange(S)

    def block(args):
        q_blk, blk = args
        q_pos = blk * Q_BLOCK + jnp.arange(Q_BLOCK)
        dist = q_pos[:, None] - k_pos[None, :]
        bias = rel_bias[t5_causal_bucket(dist)].astype(jnp.float32).transpose(2, 0, 1)
        s = jnp.einsum('bhcqd,bhckd->bhcqk', q_blk, kt).astype(jnp.float32) + bias[None, :, None]
        s = jnp.where(dist >= 0, s, -jnp.inf)
        p = jax.nn.softmax(s, axis=-1)
        a = p[:, :, 0] - lam_full * p[:, :, 1]
        return jnp.einsum('bhqk,bhkv->bhqv', a, vt)

    o = lax.map(block, (qb, jnp.arange(nb)))
    o = o.transpose(1, 0, 3, 2, 4).reshape(B, S, H, dv)
    o = rms_norm(o, subln_gain) * (1.0 - lambda_init)
    return o.reshape(B, S, H * dv).astype(h.dtype) @ w_o

def hgrn2(h, w_in, w_o, out_gain, lb):
    B, S, _ = h.shape
    H, dk, dv, C = HGRN_HEADS, HGRN_EXPAND, HGRN_HEAD_V, HGRN_CHUNK
    F = HGRN_FORGET_DIM
    q, f, i, g = jnp.split(h @ w_in, [F, 2 * F, 2 * F + D_MODEL], axis=-1)
    f32 = f.astype(jnp.float32)
    lb32 = lb.astype(jnp.float32)
    log_forget = jnp.logaddexp(jnp.log(lb32), jnp.log1p(-lb32) + jax.nn.log_sigmoid(f32))
    k = (1.0 - lb32) * jax.nn.sigmoid(-f32)
    nc = S // C

    def to_chunks(t, d):
        return t.astype(jnp.float32).reshape(B, nc, C, H, d).transpose(1, 0, 3, 2, 4)

    qs, ks, gs = to_chunks(q, dk), to_chunks(k, dk), to_chunks(log_forget, dk)
    vs = to_chunks(i, dv)
    causal = jnp.tril(jnp.ones((C, C), dtype=bool))[None, None, :, :, None]

    def step(state, inp):
        qc, kc, vc, gc = inp
        G = jnp.cumsum(gc, axis=2)
        o_inter = jnp.einsum('bhtk,bhkv->bhtv', qc * jnp.exp(G), state)
        diff = G[:, :, :, None, :] - G[:, :, None, :, :]
        decay = jnp.exp(jnp.where(causal, diff, -jnp.inf))
        scores = jnp.einsum('bhtk,bhsk,bhtsk->bhts', qc, kc, decay)
        o_intra = jnp.einsum('bhts,bhsv->bhtv', scores, vc)
        G_last = G[:, :, -1:, :]
        new_state = (jnp.exp(G_last[:, :, 0, :])[..., None] * state
                     + jnp.einsum('bhsk,bhsv->bhkv', kc * jnp.exp(G_last - G), vc))
        return new_state, o_inter + o_intra

    state0 = jnp.zeros((B, H, dk, dv), jnp.float32)
    _, o = lax.scan(step, state0, (qs, ks, vs, gs))
    o = o.transpose(1, 0, 3, 2, 4).reshape(B, S, H, dv)
    o = rms_norm(o, out_gain.reshape(H, dv)) * jax.nn.silu(g.astype(jnp.float32)).reshape(B, S, H, dv)
    return o.reshape(B, S, D_MODEL).astype(h.dtype) @ w_o

def _normal(key, shape, scale):
    return jax.random.normal(key, shape, jnp.float32) * scale

def first_inputs(seed: int = 0) -> dict:
    key = jax.random.key(seed)
    ks = jax.random.split(key, 20)
    D, F2 = D_MODEL, 2 * HGRN_FORGET_DIM + 2 * D_MODEL
    return {
        'x': _normal(ks[0], (BATCH, SEQ, D), 1.0),
        'c': _normal(ks[1], (BATCH, D), 1.0),
        'ada_w': _normal(ks[2], (DEPTH, D, N_SUBLAYERS * 3 * D), 0.5 * D ** -0.5),
        'ada_b': _normal(ks[3], (DEPTH, N_SUBLAYERS * 3 * D), 0.02),
        'norm_g': 1.0 + _normal(ks[4], (DEPTH, N_SUBLAYERS, D), 0.02),
        'ffn_w_in': _normal(ks[5], (DEPTH, 2, D, 2 * D_FF), D ** -0.5),
        'ffn_w_down': _normal(ks[6], (DEPTH, 2, D_FF, D), D_FF ** -0.5),
        'attn_w_qkv': _normal(ks[7], (N_ATTN_LAYERS, D, 3 * D), D ** -0.5),
        'attn_w_o': _normal(ks[8], (N_ATTN_LAYERS, D, D), D ** -0.5),
        'attn_q_gain': 1.0 + _normal(ks[9], (N_ATTN_LAYERS, ATTN_HEAD_DIM), 0.02),
        'attn_k_gain': 1.0 + _normal(ks[10], (N_ATTN_LAYERS, ATTN_HEAD_DIM), 0.02),
        'attn_lambda': _normal(ks[11], (N_ATTN_LAYERS, 4, ATTN_HEAD_DIM), 0.1),
        'attn_subln_gain': 1.0 + _normal(ks[12], (N_ATTN_LAYERS, ATTN_V_DIM), 0.02),
        'rel_bias': _normal(ks[13], (NUM_BUCKETS, ATTN_HEADS), 0.5),
        'hgrn_w_in': _normal(ks[14], (N_HGRN_LAYERS, D, F2), D ** -0.5),
        'hgrn_w_o': _normal(ks[15], (N_HGRN_LAYERS, D, D), D ** -0.5),
        'hgrn_out_gain': 1.0 + _normal(ks[16], (N_HGRN_LAYERS, D), 0.02),
        'hgrn_lb_logits': _normal(ks[17], (N_HGRN_LAYERS, HGRN_FORGET_DIM), 0.1),
    }

def first_block(x, c, ada_w, ada_b, norm_g, ffn_w_in, ffn_w_down, attn_w_qkv, attn_w_o,
              attn_q_gain, attn_k_gain, attn_lambda, attn_subln_gain, rel_bias,
              hgrn_w_in, hgrn_w_o, hgrn_out_gain, hgrn_lb_logits):
    B = x.shape[0]
    lb_all = jnp.cumsum(jax.nn.softmax(hgrn_lb_logits.astype(jnp.float32), axis=0), axis=0)
    lb_all = lb_all - lb_all[0:1]
    c_act = jax.nn.silu(c)
    for layer in range(DEPTH):
        mod = (c_act @ ada_w[layer] + ada_b[layer]).reshape(B, N_SUBLAYERS, 3, D_MODEL)
        shift = mod[:, :, 0][:, None]
        scale = mod[:, :, 1][:, None]
        gate = mod[:, :, 2][:, None]
        h = rms_norm(x, norm_g[layer, 0]) * (1.0 + scale[:, :, 0]) + shift[:, :, 0]
        x = x + 0.5 * gate[:, :, 0] * swiglu(h, ffn_w_in[layer, 0], ffn_w_down[layer, 0])
        h = rms_norm(x, norm_g[layer, 1]) * (1.0 + scale[:, :, 1]) + shift[:, :, 1]
        j = layer // N_MIXERS
        if layer % N_MIXERS == 0:
            y = diff_attention(h, attn_w_qkv[j], attn_w_o[j], attn_q_gain[j], attn_k_gain[j],
                               attn_lambda[j], attn_subln_gain[j], rel_bias, layer)
        else:
            y = hgrn2(h, hgrn_w_in[j], hgrn_w_o[j], hgrn_out_gain[j], lb_all[j])
        x = x + gate[:, :, 1] * y
        h = rms_norm(x, norm_g[layer, 2]) * (1.0 + scale[:, :, 2]) + shift[:, :, 2]
        x = x + 0.5 * gate[:, :, 2] * swiglu(h, ffn_w_in[layer, 1], ffn_w_down[layer, 1])
    return x


DEPTH_2 = 1

GLA_HEADS = 4
GLA_DK = 48
GLA_DV = 96
GLA_GATE_RANK = 16
GLA_GATE_NORM = 16.0
GLA_CHUNK = 64
DSA_HEADS = 6
DSA_DH = 64
IDX_HEADS = 4
IDX_DIM = 32
TOPK_MAX = 256
QUERY_BLOCK = 128
POOL_GROUPS = 4
POOL_GC = 64
POOL_WINDOWS = (2, 4, 8, 16)
REL_BUCKETS = 32
REL_MAX_DIST = 128

GLA_W = GLA_HEADS * GLA_DV
DSA_W = DSA_HEADS * DSA_DH
POOL_W = POOL_GROUPS * POOL_GC
D_MIX = GLA_W + DSA_W + POOL_W

IN_SIZES = (
    GLA_HEADS * GLA_DK,
    GLA_HEADS * GLA_DK,
    GLA_W,
    GLA_GATE_RANK,
    GLA_W,
    DSA_W,
    DSA_W,
    DSA_W,
    DSA_W,
    IDX_HEADS * IDX_DIM,
    IDX_DIM,
    IDX_HEADS,
    POOL_W,
    POOL_W,
)
IN_COLS = sum(IN_SIZES)


def split_cols(p):
    outs = []
    off = 0
    for s in IN_SIZES:
        outs.append(p[..., off:off + s])
        off += s
    return outs

def rmsnorm(x, g):
    xf = x.astype(jnp.float32)
    y = xf * lax.rsqrt(jnp.mean(xf * xf, axis=-1, keepdims=True) + EPS)
    return (y * g.astype(jnp.float32)).astype(x.dtype)

def t5_bucket(rel):
    rel = jnp.maximum(rel, 0)
    max_exact = REL_BUCKETS // 2
    relf = jnp.maximum(rel, 1).astype(jnp.float32)
    large = max_exact + (jnp.log(relf / max_exact) / math.log(REL_MAX_DIST / max_exact)
                         * (REL_BUCKETS - max_exact)).astype(jnp.int32)
    large = jnp.minimum(large, REL_BUCKETS - 1)
    return jnp.where(rel < max_exact, rel, large)

def gla_mixer(q, k, v, glog):
    B, T, H, dk = q.shape
    dv = v.shape[-1]
    N = T // GLA_CHUNK
    def chunk(a):
        return a.astype(jnp.float32).reshape(B, N, GLA_CHUNK, H, a.shape[-1])
    qf, kf, vf, gf = chunk(q), chunk(k), chunk(v), chunk(glog)
    b = jnp.cumsum(gf, axis=2)
    b_last = b[:, :, -1:]
    qe = qf * jnp.exp(b) * (dk ** -0.5)
    ke = kf * jnp.exp(-b)
    kd = kf * jnp.exp(b_last - b)
    A = jnp.einsum('bnihd,bnjhd->bnhij', qe, ke)
    tril = jnp.tril(jnp.ones((GLA_CHUNK, GLA_CHUNK), dtype=bool))
    A = jnp.where(tril, A, 0.0)
    o_intra = jnp.einsum('bnhij,bnjhv->bnihv', A, vf)
    U = jnp.einsum('bnjhd,bnjhv->bnhdv', kd, vf)
    decay = jnp.exp(b_last[:, :, 0])
    def step(S, inp):
        dec, u = inp
        return dec[..., None] * S + u, S
    S0 = jnp.zeros((B, H, dk, dv), jnp.float32)
    _, S_prev = lax.scan(step, S0, (jnp.moveaxis(decay, 1, 0), jnp.moveaxis(U, 1, 0)))
    S_prev = jnp.moveaxis(S_prev, 0, 1)
    o_inter = jnp.einsum('bnihd,bnhdv->bnihv', qe, S_prev)
    return (o_intra + o_inter).reshape(B, T, H, dv)

def dsa_mixer(q, k, v, q_idx, k_idx, w_idx, rel_bias):
    B, T, H, dh = q.shape
    topk = min(TOPK_MAX, T // 4)
    NB = T // QUERY_BLOCK
    def blk(a):
        return jnp.moveaxis(a.reshape(B, NB, QUERY_BLOCK, *a.shape[2:]), 1, 0)
    pos_blk = jnp.arange(T, dtype=jnp.int32).reshape(NB, QUERY_BLOCK)
    key_pos = jnp.arange(T, dtype=jnp.int32)
    kidx_f = k_idx.astype(jnp.float32)
    rb = rel_bias.astype(jnp.float32)

    def body(args):
        qb, qib, wb, tq = args
        s = jax.nn.relu(jnp.einsum('bqhd,bsd->bqhs', qib.astype(jnp.float32), kidx_f)
                        * (IDX_DIM ** -0.5))
        score = jnp.einsum('bqhs,bqh->bqs', s, wb.astype(jnp.float32) * (IDX_HEADS ** -0.5))
        visible = key_pos[None, :] <= tq[:, None]
        score = jnp.where(visible[None], score, -jnp.inf)
        _, idx = lax.top_k(score, topk)
        kg = jax.vmap(lambda kk, ii: kk[ii])(k, idx)
        vg = jax.vmap(lambda vv, ii: vv[ii])(v, idx)
        logits = jnp.einsum('bqhd,bqkhd->bhqk', qb.astype(jnp.float32),
                            kg.astype(jnp.float32)) * (dh ** -0.5)
        rel = tq[None, :, None] - idx
        bias = rb[t5_bucket(rel)]
        logits = logits + jnp.moveaxis(bias, -1, 1)
        logits = jnp.where((rel >= 0)[:, None], logits, -1e30)
        p = jax.nn.softmax(logits, axis=-1)
        o = jnp.einsum('bhqk,bqkhd->bqhd', p, vg.astype(jnp.float32))
        return o.astype(q.dtype)

    o = lax.map(body, (blk(q), blk(q_idx), blk(w_idx), pos_blk))
    return jnp.moveaxis(o, 0, 1).reshape(B, T, H * dh)

def pool_mixer(u, pool_w, pool_scale):
    B, T, _ = u.shape
    ug = u.astype(jnp.float32).reshape(B, T, POOL_GROUPS, POOL_GC)
    cs = jnp.cumsum(ug, axis=1)
    pos = jnp.arange(T, dtype=jnp.int32)
    outs = []
    for gi, w in enumerate(POOL_WINDOWS):
        c = cs[:, :, gi]
        lower = jnp.pad(c, ((0, 0), (w, 0), (0, 0)))[:, :T]
        cnt = jnp.minimum(pos + 1, w).astype(jnp.float32)[None, :, None]
        outs.append((c - lower) / cnt - ug[:, :, gi])
    pooled = jnp.stack(outs, axis=2)
    y = jnp.einsum('btgc,gcd->btgd', pooled, pool_w.astype(jnp.float32)).reshape(B, T, POOL_W)
    return (y * pool_scale.astype(jnp.float32)).astype(u.dtype)

def second_inputs(seed: int = 0) -> dict:
    key = jax.random.key(seed)
    ks = jax.random.split(key, 12)
    f = jnp.float32
    x = jax.random.normal(ks[0], (BATCH, SEQ, D_MODEL), f)
    norm_g = 1.0 + 0.05 * jax.random.normal(ks[1], (DEPTH_2, D_MODEL), f)
    w_in = jax.random.normal(ks[2], (DEPTH_2, D_MODEL, IN_COLS), f) * D_MODEL ** -0.5
    gla_gate_w2 = jax.random.normal(ks[3], (DEPTH_2, GLA_GATE_RANK, GLA_HEADS * GLA_DK), f) * GLA_GATE_RANK ** -0.5
    gla_gate_b = 0.1 * jax.random.normal(ks[4], (DEPTH_2, GLA_HEADS * GLA_DK), f)
    gla_norm_g = 1.0 + 0.05 * jax.random.normal(ks[5], (DEPTH_2, GLA_DV), f)
    rel_bias = 0.1 * jax.random.normal(ks[6], (REL_BUCKETS, DSA_HEADS), f)
    pool_w = jax.random.normal(ks[7], (DEPTH_2, POOL_GROUPS, POOL_GC, POOL_GC), f) * POOL_GC ** -0.5
    pool_scale = 1.0 + 0.1 * jax.random.normal(ks[8], (DEPTH_2, POOL_W), f)
    w_out = jax.random.normal(ks[9], (DEPTH_2, D_MIX, D_MODEL), f) * D_MIX ** -0.5
    final_norm_g = 1.0 + 0.05 * jax.random.normal(ks[10], (D_MODEL,), f)
    return {'x': x, 'norm_g': norm_g, 'w_in': w_in, 'gla_gate_w2': gla_gate_w2,
            'gla_gate_b': gla_gate_b, 'gla_norm_g': gla_norm_g, 'rel_bias': rel_bias,
            'pool_w': pool_w, 'pool_scale': pool_scale, 'w_out': w_out,
            'final_norm_g': final_norm_g}

def second_block(x, norm_g, w_in, gla_gate_w2, gla_gate_b, gla_norm_g, rel_bias,
              pool_w, pool_scale, w_out, final_norm_g):
    B, T, _ = x.shape
    for l in range(DEPTH_2):
        h = rmsnorm(x, norm_g[l])
        p = jnp.einsum('btd,dc->btc', h, w_in[l])
        (gq, gk, gv, gz, ggate, dq, dk, dv, dgate,
         qi, ki, wi, pu, pgate) = split_cols(p)
        glog = jax.nn.log_sigmoid((jnp.einsum('btr,rc->btc', gz, gla_gate_w2[l])
                                   + gla_gate_b[l]).astype(jnp.float32)) / GLA_GATE_NORM
        o_gla = gla_mixer(gq.reshape(B, T, GLA_HEADS, GLA_DK),
                          gk.reshape(B, T, GLA_HEADS, GLA_DK),
                          gv.reshape(B, T, GLA_HEADS, GLA_DV),
                          glog.reshape(B, T, GLA_HEADS, GLA_DK))
        o_gla = rmsnorm(o_gla, gla_norm_g[l]).reshape(B, T, GLA_W).astype(x.dtype)
        y_gla = o_gla * jax.nn.silu(ggate)
        o_dsa = dsa_mixer(dq.reshape(B, T, DSA_HEADS, DSA_DH),
                          dk.reshape(B, T, DSA_HEADS, DSA_DH),
                          dv.reshape(B, T, DSA_HEADS, DSA_DH),
                          qi.reshape(B, T, IDX_HEADS, IDX_DIM), ki, wi, rel_bias)
        y_dsa = o_dsa * jax.nn.silu(dgate)
        y_pool = pool_mixer(pu, pool_w[l], pool_scale[l]) * jax.nn.silu(pgate)
        y = jnp.concatenate([y_gla, y_dsa, y_pool], axis=-1)
        x = x + jnp.einsum('btc,cd->btd', y, w_out[l])
    return rmsnorm(x, final_norm_g)


def setup_inputs(seed=0):
    out = dict(first_inputs(seed))
    for name, value in second_inputs(seed + 1).items():
        if name != "x":
            out[name + "_2"] = value
    return out


def reference(
    x, c, ada_w, ada_b, norm_g, ffn_w_in, ffn_w_down, attn_w_qkv, attn_w_o, attn_q_gain,
    attn_k_gain, attn_lambda, attn_subln_gain, rel_bias, hgrn_w_in, hgrn_w_o, hgrn_out_gain,
    hgrn_lb_logits, norm_g_2, w_in_2, gla_gate_w2_2, gla_gate_b_2, gla_norm_g_2, rel_bias_2,
    pool_w_2, pool_scale_2, w_out_2, final_norm_g_2,
):
    x = first_block(
        x, c, ada_w, ada_b, norm_g, ffn_w_in, ffn_w_down, attn_w_qkv, attn_w_o, attn_q_gain,
        attn_k_gain, attn_lambda, attn_subln_gain, rel_bias, hgrn_w_in, hgrn_w_o, hgrn_out_gain,
        hgrn_lb_logits,
    )
    return second_block(
        x, norm_g_2, w_in_2, gla_gate_w2_2, gla_gate_b_2, gla_norm_g_2, rel_bias_2, pool_w_2,
        pool_scale_2, w_out_2, final_norm_g_2,
    )


_drawn_inputs = setup_inputs


def setup_inputs(seed=0):
    import zlib

    import numpy as np

    out = dict(_drawn_inputs(seed))
    spreads = {}
    factors = {'norm_g': 4.046,
     'attn_q_gain': 8.0,
     'attn_k_gain': 8.0,
     'attn_subln_gain': 8.0,
     'hgrn_out_gain': 25.08,
     'gla_gate_b_2': 18.137,
     'gla_norm_g_2': 22.685,
     'rel_bias_2': 64.0,
     'pool_scale_2': 18.654,
     'norm_g_2': 3.616,
     'gla_gate_w2_2': 3.954}
    for name, (base, spread) in spreads.items():
        noise = np.random.default_rng([zlib.crc32(name.encode()), seed]).standard_normal(out[name].shape)
        drawn = base * np.exp(spread * noise) if base else spread * noise
        out[name] = jnp.asarray(drawn.astype(out[name].dtype))
    for name, factor in factors.items():
        out[name] = (out[name] * factor).astype(out[name].dtype)
    return out
```

```python
from contextlib import ExitStack

import concourse.bass as bass
from concourse import mybir

P = 128
T = 512
D = 1024
KD = D // P
TT = T // P
FF = 2816
KF = FF // P
KH = KF // 2
SLOT = KH * P
EPS = 1e-6
HEADS = 8
HD = 64
LEVELS = 7
GH, GK, GV = 4, 48, 96
DH = 6
IH = 4
TOPK = 128
LAMBDA_INIT = 0.2
NEG = -1.0e30
LOW = -3.0e38

ALU = mybir.AluOpType
ACT = mybir.ActivationFunctionType
F32 = mybir.dt.float32
F32R = mybir.dt.float32r
AX_X = mybir.AxisListType.X

SIZES = (("gq", 192), ("gk", 192), ("gv", 384), ("gz", 16), ("ggate", 384), ("dq", 384), ("dk", 384),
         ("dv", 384), ("dgate", 384), ("qi", 128), ("ki", 32), ("wi", 4), ("pu", 256), ("pgate", 256))
COL, _at = {}, 0
for _n, _s in SIZES:
    COL[_n] = _at
    _at += _s


def second_blocks():
    out = [("qi", 0, [(COL["qi"], P, 0)]),
           ("ki", 0, [(COL["ki"], 32, 32 * r) for r in range(IH)]),
           ("wi", 0, [(COL["wi"], P, 0)]),
           ("gz", 0, [(COL["gz"], P, 0)])]
    for kind in ("gq", "gk"):
        for t in range(2):
            out.append((kind, t, [(COL[kind] + 2 * GK * t + GK * r, 64, 64 * r) for r in range(2)]))
    for kind, n in (("gv", 3), ("dq", 3), ("dk", 3), ("dv", 3), ("pu", 2)):
        for t in range(n):
            out.append((kind, t, [(COL[kind] + P * t, P, 0)]))
    for t in range(GH):
        out.append(("ggate", t, [(COL["ggate"] + GV * t, P, 0)]))
    for kind, n in (("dgate", 3), ("pgate", 2)):
        for t in range(n):
            out.append((kind, t, [(COL[kind] + P * t, P, 0)]))
    return out


SECOND = second_blocks()
NATURAL = ("wi", "gv", "dv")

UP, DOWN = 2 * KF, 2 * KD
FIRST = {}
_at = 0
for _name, _n in (("F0", UP + DOWN), ("QKV", 24), ("WO", KD), ("F1", UP + DOWN), ("F2", UP + DOWN), ("HIN", 32),
                  ("HO", KD), ("F3", UP + DOWN), ("P2", len(SECOND)), ("OUT", KD)):
    FIRST[_name] = _at
    _at += _n
BLOCKS = _at


def tiles_of(n):
    for f in ("F0", "F1", "F2", "F3"):
        if FIRST[f] + UP <= n < FIRST[f] + UP + DOWN:
            return KH
    return 9 if n >= FIRST["OUT"] else KD


class Line:

    def __init__(self, eng, own):
        self.eng, self.own, self.count, self.last, self.i, self.per = eng, own, {}, None, None, {}

    def __call__(self, ins, sem=None):
        sem = sem or self.own
        ins.then_inc(sem, 1)
        self.count[sem.name] = self.count.get(sem.name, 0) + 1
        self.last = sem
        return ins

    def value(self, sem):
        n = self.count.get(sem.name, 0)
        per = self.per.get(sem.name, 0)
        return self.i * per + n if self.i is not None and per else n

    def settle(self):
        if self.last is not None:
            self.eng.wait_ge(self.last, self.value(self.last))

    def loop(self, first, end, body, per):
        if end <= first:
            return
        self.settle()
        per = {s.name: k for s, k in per}
        start = dict(self.count)
        with self.eng.Fori(0, end - first) as i:
            self.i, self.per = i, per
            body(i)
            self.i, self.per = None, {}
        for name in set(self.count) | set(per):
            had = self.count.get(name, 0) - start.get(name, 0)
            assert had == per.get(name, 0), (name, had, per.get(name, 0))
            self.count[name] = start.get(name, 0) + (end - first) * had


def program(nc, x, c, ada_w, ada_b, norm_g, ffn_w_in, ffn_w_down, attn_w_qkv, attn_w_o, attn_q_gain,
            attn_k_gain, attn_lambda, attn_subln_gain, rel_bias, hgrn_w_in, hgrn_w_o, hgrn_out_gain,
            hgrn_lb_logits, norm_g_2, w_in_2, gla_gate_w2_2, gla_gate_b_2, gla_norm_g_2, rel_bias_2,
            pool_w_2, pool_scale_2, w_out_2, final_norm_g_2, bucket_rows, level_masks, pool_counts, out):
    ctx = ExitStack()
    with ctx:
        def sb(name, shape, dt=F32, where=ctx):
            return where.enter_context(nc.sbuf_tensor(name, shape, dt))

        def sem(name):
            return ctx.enter_context(nc.semaphore(name))

        xT = sb("xT", [P, KD, T])
        h_hi = sb("h_hi", [P, KD, T], F32R)
        h_lo = sb("h_lo", [P, KD, T], F32R)
        raw = sb("raw", [P, 4, SLOT])
        w_hi = sb("w_hi", [P, 2, SLOT], F32R)
        w_lo = sb("w_lo", [P, 2, SLOT], F32R)
        ada = sb("ada", [P, 4, D])
        ada_sum = sb("ada_sum", [P, D])
        ident = sb("ident", [P, P])
        ones = sb("ones", [P, P])
        halves = sb("halves", [P, P])
        rows = sb("rows", [P, 2, P])
        cols = sb("cols", [P, 2, P])
        mod = sb("mod", [P, 18 * KD])
        cact = sb("cact", [P, KD])
        scale_col = sb("scale_col", [P, KD])
        gate_col = sb("gate_col", [P, KD])
        small = sb("small", [P, 64])
        sumsq = sb("sumsq", [P, T])
        sq = sb("sq", [P, T])
        rstd = sb("rstd", [P, T])
        lnt = sb("lnt", [P, T])
        tmp = sb("tmp", [P, 4, T])
        eight = sb("eight", [P, 8])
        gend = sb("gend", [P, 2, 8])

        ph = ExitStack()
        g_hi = sb("g_hi", [P, KF, T], F32R, ph)
        g_lo = sb("g_lo", [P, KF, T], F32R, ph)
        ph.close()
        ph = ExitStack()
        x_rows = sb("x_rows", [P, TT, D], F32, ph)
        bias_row = sb("bias_row", [8, 2, 640], F32, ph)
        lamb = sb("lamb", [P, 4, HD], F32, ph)
        table = sb("table", [33, 640 + 16], F32, ph)
        ph.close()
        ph = ExitStack()
        aq = sb("aq", [P, HEADS, T], F32, ph)
        ak = sb("ak", [P, HEADS, T], F32, ph)
        av = sb("av", [P, TT, D], F32, ph)
        toep1 = sb("toep1", [P, HEADS, T], F32, ph)
        s1 = sb("s1", [P, 3, 2, T], F32, ph)
        at1 = sb("at1", [P, 2, T], F32, ph)
        o1 = sb("o1", [P, 2, T], F32, ph)
        ph.close()
        ph = ExitStack()
        hq = sb("hq", [P, HEADS, T], F32, ph)
        hk = sb("hk", [P, HEADS, T], F32, ph)
        hG = sb("hG", [P, HEADS, T], F32, ph)
        hg = sb("hg", [P, HEADS, T], F32, ph)
        hv = sb("hv", [P, TT, D], F32, ph)
        masks = sb("masks", [P, 8, P], F32, ph)
        hE, hqE, hkE, hP = (ada[:, i, :].rearrange("p (a n) -> p a n", n=T) for i in range(4))
        heG, hqG = tmp[:, 2, :], tmp[:, 3, :]
        hkd = sb("hkd", [P, T], F32, ph)
        hkn = sb("hkn", [P, T], F32, ph)
        hst = (rows[:, 0, :], rows[:, 1, :], hkn[:, 3 * P:4 * P])
        ho = ada_sum[:, 0:T]
        zero = ada_sum[:, T:2 * T]
        reset = ada_sum[:, 0:T]
        ph.close()
        ph = ExitStack()
        z = {}
        for kind, shape in (("qi", [P, T]), ("ki", [P, T]), ("gz", [P, T]), ("gv", [P, TT, 384]), ("dq", [P, 3, T]), ("dk", [P, 3, T]), ("dv", [P, TT, 384]),
                            ("pu", [P, 2, T]), ("ggate", [P, GH, T]), ("dgate", [P, 3, T]), ("pgate", [P, 2, T]),
                            ("wi", [P, TT, IH])):
            z[kind] = sb("z_" + kind, shape, F32, ph)
        toep2 = sb("toep2", [P, DH, T], F32, ph)
        z["gq"], z["gk"] = toep2[:, 0:2, :], toep2[:, 2:4, :]
        gst = toep2[:, 4:6, :].rearrange("p a n -> p (a n)")[:, 0:8 * GV].rearrange("p (c v) -> p c v", v=GV)
        chosen = sb("chosen", [P, TT, T], F32, ph)
        s2 = sb("s2", [P, 3, 1, T], F32, ph)
        spare = ada[:, :, :].rearrange("p a (b n) -> p (a b) n", n=T)
        work, at2 = spare[:, 0:6, :], spare[:, 6:8, :]
        o2 = ada_sum[:, :].rearrange("p (a n) -> p a n", n=T)
        gE = s2[:, :, 0, :]
        poolw = sb("poolw", [P, 2, P], F32, ph)
        poolc = sb("poolc", [P, 2, 16], F32, ph)
        w2 = sb("w2", [16, 2, P], F32, ph)
        zero2 = sb("zero2", [P, T], F32, ph)
        reset2 = chosen[:, TT - 1, :]
        y8_hi = sb("y8_hi", [P, T], F32R, ph)
        y8_lo = sb("y8_lo", [P, T], F32R, ph)
        ph.close()

        B = [ctx.enter_context(nc.psum_tensor(f"bank{i}", [P, T], F32)) for i in range(8)]
        bias_dram = nc.dram_tensor("bias_scratch", (2, 8, P, 640), F32)

        landed = [sem(f"landed{i}") for i in range(4)]
        ada_landed = [sem(f"ada_landed{i}") for i in range(4)]
        hi_ready = sem("hi_ready")
        lo_ready = sem("lo_ready")
        used = sem("used")
        ada_used = sem("ada_used")
        ada_done = sem("ada_done")
        setup = sem("setup")
        setup2 = sem("setup2")
        const_ready = sem("const_ready")
        turned = sem("turned")
        cols_ready = sem("cols_ready")
        x_turned = sem("x_turned")
        x_ready = sem("x_ready")
        sq_ready = sem("sq_ready")
        sum_ready = sem("sum_ready")
        rms_ps = sem("rms_ps")
        rstd_ready = sem("rstd_ready")
        t_ready = sem("t_ready")
        hhi_ready = sem("hhi_ready")
        h_ready = sem("h_ready")
        silu_ready = sem("silu_ready")
        g_ready = sem("g_ready")
        gt_ready = sem("gt_ready")
        ghi_ready = sem("ghi_ready")
        cact_ready = sem("cact_ready")
        act_own = sem("act_own")
        dve_own = sem("dve_own")
        pool_own = sem("pool_own")
        bias_ps = sem("bias_ps")
        bias_sb = sem("bias_sb")
        bias_out = sem("bias_out")
        toep_in = sem("toep_in")
        epi_free = sem("epi_free")
        headsq = sem("headsq")
        headss = sem("headss")
        headrs = sem("headrs")
        headn = sem("headn")
        S_ps = sem("S_ps")
        S_max = sem("S_max")
        p_ready = sem("p_ready")
        a_ready = sem("a_ready")
        aT_ps = sem("aT_ps")
        aT_sb = sem("aT_sb")
        pv_done = sem("pv_done")
        o_sq = sem("o_sq")
        o_ss = sem("o_ss")
        o_rs = sem("o_rs")
        y_t = sem("y_t")
        y_hi = sem("y_hi")
        y_ready = sem("y_ready")
        f_min = sem("f_min")
        f_log = sem("f_log")
        f_arg = sem("f_arg")
        f_key = sem("f_key")
        f_done = sem("f_done")
        lv_D = sem("lv_D")
        lv_E = sem("lv_E")
        lv_q = sem("lv_q")
        lv_k = sem("lv_k")
        lv_S = sem("lv_S")
        lv_P = sem("lv_P")
        lv_O = sem("lv_O")
        st_E = sem("st_E")
        st_k = sem("st_k")
        st_T = sem("st_T")
        st_n = sem("st_n")
        st_U = sem("st_U")
        st_s = sem("st_s")
        ix_S = sem("ix_S")
        ix_r = sem("ix_r")
        ix_a = sem("ix_a")
        ix_c = sem("ix_c")
        ix_m = sem("ix_m")
        gl_z = sem("gl_z")
        gl_u = sem("gl_u")
        phase_const = sem("phase_const")
        small_in = sem("small_in")
        gl_l = sem("gl_l")
        gl_b = sem("gl_b")
        gl_e = sem("gl_e")
        gl_q = sem("gl_q")
        gl_A = sem("gl_A")
        gl_a = sem("gl_a")
        gl_m = sem("gl_m")
        gl_T = sem("gl_T")
        gl_n = sem("gl_n")
        gl_U = sem("gl_U")
        gl_s = sem("gl_s")
        gl_O = sem("gl_O")
        pl_d = sem("pl_d")
        pl_y = sem("pl_y")
        fin_t = sem("fin_t")
        fin_ps = sem("fin_ps")
        fin_sb = sem("fin_sb")
        out_done = [sem(f"out_done{i}") for i in range(2)]

        def norm_col(i, j):
            return cols[:, 0, 8 * i + j:8 * i + j + 1]
        C_C, C_HG, C_LB, C_SUB, C_PS, C_QG, C_KG, C_GB, C_GN, C_AB = 64, 72, 80, 88, 89, 91, 92, 93, 95, 96
        L_EPS, L_ONE, L_NLAM, L_ZERO = 0, 1, 2, 3
        eps_c, one_c, nlam_c = small[:, 0:1], small[:, 1:2], small[:, 2:3]
        lb_c, lb1_c = small[:, 8:16], small[:, 16:24]
        subg_c = small[:, 3:4]
        qg_c = small[:, 4:5]
        bank_of = [0, 0]

        ada_v = ada_w.rearrange("l (k p) n -> l k p n", p=P)
        up_v = ffn_w_in.rearrange("l s (k p) n -> l s p k n", p=P)
        down_v = ffn_w_down.rearrange("l s (u k p) n -> l s u p k n", p=P, k=KH)
        qkv_v = attn_w_qkv.rearrange("l (k p) n -> l p k n", p=P)
        wo_v = attn_w_o.rearrange("l (k p) n -> l p k n", p=P)
        hin_v = hgrn_w_in.rearrange("l (k p) n -> l p k n", p=P)
        ho_v = hgrn_w_o.rearrange("l (k p) n -> l p k n", p=P)
        in2_v = w_in_2.rearrange("l (k p) n -> l p k n", p=P)
        block = ctx.enter_context(nc.Block())

        def plus(i, per, base):
            return base if i is None else i * per + base

        HORDER = [("q", j) for j in range(8)] + [("v", j) for j in range(8)] + \
                 [("g", j) for j in range(8)] + [("f", j) for j in range(8)]
        HCOL = {"q": 0, "f": 1, "v": 2, "g": 3}

        FFN = (("F0", 0, 0, 3, 6), ("F1", 0, 1, 9, 9), ("F2", 1, 0, 0, 0), ("F3", 1, 1, 0, 0))

        def landings(n):
            total = 0
            for m in range(n % 4, n + 1, 4):
                if m >= FIRST["OUT"]:
                    total += 2
                elif m >= FIRST["P2"]:
                    total += len(SECOND[m - FIRST["P2"]][2])
                else:
                    total += 1
            return 16 * total

        def tmp_out(t):
            return tmp[:, 2 * (t % 2):2 * (t % 2) + 2, :]

        def hgrn_pool(pool, line):
            g = nc.gpsimd
            pool.wait_ge(used, FIRST["HIN"])
            line.settle()
            line(g.memset(zero[:, :], 0.0))
            line.settle()
            line(g.memset(reset[:, :], 1.0))
            line.settle()
            line(g.memset(reset[:, 0:T:P], 0.0), phase_const)
            for h in range(HEADS):
                for v in range(LEVELS):
                    n = h * LEVELS + v
                    pool.wait_ge(lv_E, n + 1)
                    if n >= 2:
                        pool.wait_ge(lv_S, level_at(n - 2))
                    line.settle()
                    line(g.tensor_tensor(hkE[:, n % 2, :], hk[:, h, :], hE[:, n % 2, :], ALU.mult), lv_k)
                    if v == 2:
                        pool.wait_ge(st_E, h + 1)
                        if h:
                            pool.wait_ge(st_T, h)
                            pool.wait_ge(pv_done, pv_h(h))
                        line.settle()
                        line(g.tensor_tensor(hqG[:, :], hq[:, h, :], heG[:, :], ALU.mult), st_k)
                        line.settle()
                        line(g.tensor_tensor(hkd[:, :], hk[:, h, :], hkd[:, :], ALU.mult), st_k)

        def level_at(n):
            return n // LEVELS * (LEVELS + 1) + n % LEVELS + 1

        def pv_h(h):
            return HEADS * TT + h

        def bias_tiles(act, dst, m, heads):
            src = bass.AP(tensor=bias_dram, offset=m * 8 * P * 640 + P - 1, ap=[[639, P], [P * 640, heads], [1, T]])
            act.dma_start(dst, src).then_inc(toep_in, 16)

        def split_hi(act, line, n, i=None):
            if n >= BLOCKS:
                return
            k = tiles_of(n)
            base = landings(n)
            act.wait_ge(landed[n % 4], plus(i, 16, base))
            if n >= 2:
                act.wait_ge(used, plus(i, 4, n - 1))
            if k == 9:
                line(nc.scalar.activation(w_hi[0:GV, n % 2, 0:GH * P], raw[0:GV, n % 4, 0:GH * P], ACT.Copy))
                line(nc.scalar.activation(w_hi[:, n % 2, GH * P:9 * P], raw[:, n % 4, GH * P:9 * P], ACT.Copy), hi_ready)
            else:
                line(nc.scalar.activation(w_hi[:, n % 2, 0:k * P], raw[:, n % 4, 0:k * P], ACT.Copy), hi_ready)

        def split_lo(dve, line, n, i=None):
            if n >= BLOCKS:
                return
            k = tiles_of(n)
            dve.wait_ge(hi_ready, plus(i, 4, n + 1))
            if k == 9:
                line(nc.vector.tensor_tensor(w_lo[0:GV, n % 2, 0:GH * P], raw[0:GV, n % 4, 0:GH * P],
                                             w_hi[0:GV, n % 2, 0:GH * P].bitcast(F32), ALU.subtract))
                line(nc.vector.tensor_tensor(w_lo[:, n % 2, GH * P:9 * P], raw[:, n % 4, GH * P:9 * P],
                                             w_hi[:, n % 2, GH * P:9 * P].bitcast(F32), ALU.subtract), lo_ready)
            else:
                line(nc.vector.tensor_tensor(w_lo[:, n % 2, 0:k * P], raw[:, n % 4, 0:k * P],
                                             w_hi[:, n % 2, 0:k * P].bitcast(F32), ALU.subtract), lo_ready)

        def residual_dve(dve, line, n, j, i=None):
            jj = plus(i, 2, j)
            dve.wait_ge(used, plus(i, 4, n + 1))
            bank = B[j % 2]
            xj = xT[:, bass.ds(jj, 1), :].rearrange("p a n -> p (a n)") if i is not None else xT[:, j, :]
            gc = gate_col[:, bass.ds(jj, 1)] if i is not None else gate_col[:, j:j + 1]
            line(nc.vector.scalar_tensor_tensor(out=xj, in0=bank[:, :], scalar=gc, in1=xj,
                                                op0=ALU.mult, op1=ALU.add), x_ready)
            dve.wait_ge(sq_ready, line.value(x_ready))
            line(nc.vector.tensor_tensor(sumsq[:, :], sumsq[:, :], sq[:, :], ALU.add), sum_ready)

        def residual_act(act, line, count, j, i=None):
            jj = plus(i, 2, j)
            act.wait_ge(x_ready, plus(i, 2, count))
            xj = xT[:, bass.ds(jj, 1), :].rearrange("p a n -> p (a n)") if i is not None else xT[:, j, :]
            line(nc.scalar.activation(sq[:, :], xj, ACT.Square), sq_ready)

        def product(pe, n, out_ap, xs, i=None, waits=None, rows_of=None):
            pe.wait_ge(lo_ready, plus(i, 4, n + 1))
            last = None
            for k, (xh, xl) in enumerate(xs):
                if waits:
                    pe.wait_ge(waits[0], waits[1] + k)
                r = rows_of[k] if rows_of else P
                wh = w_hi[0:r, n % 2, k * P:(k + 1) * P]
                wl = w_lo[0:r, n % 2, k * P:(k + 1) * P]
                end = k == len(xs) - 1
                nc.tensor.matmul(out_ap, wh, xh, start=(k == 0), stop=False)
                nc.tensor.matmul(out_ap, wh, xl, start=False, stop=False)
                last = nc.tensor.matmul(out_ap, wl, xh, start=False, stop=end)
            last.then_inc(used, 1)

        def product_rows(pe, n, bank, width=P, waits=None):
            pe.wait_ge(lo_ready, n + 1)
            last = None
            for t in range(TT):
                o = bank[:, t * width:(t + 1) * width]
                for k in range(KD):
                    xh, xl = h_hi[:, k, t * P:(t + 1) * P], h_lo[:, k, t * P:(t + 1) * P]
                    wh = w_hi[:, n % 2, k * P:k * P + width]
                    wl = w_lo[:, n % 2, k * P:k * P + width]
                    nc.tensor.matmul(o, xh, wh, start=(k == 0), stop=False)
                    nc.tensor.matmul(o, xl, wh, start=False, stop=False)
                    last = nc.tensor.matmul(o, xh, wl, start=False, stop=(k == KD - 1))
            last.then_inc(used, 1)

        H_TILES = [(h_hi[:, k, :], h_lo[:, k, :]) for k in range(KD)]

        def norm_pe(pe, m):
            pe.wait_ge(sum_ready, KD * (m + 1))
            nc.tensor.matmul(B[5][:, :], ones[:, :], sumsq[:, :], start=True, stop=True).then_inc(rms_ps, 1)

        def norm_act(act, line, m, after):
            nc.scalar.preload_act_table_set("natural_log_exp_and_others")
            act.wait_ge(rms_ps, m + 1)
            line(nc.scalar.activation(lnt[:, :], B[5][:, :], ACT.Ln, bias=eps_c, scale=1.0 / D))
            line.settle()
            line(nc.scalar.activation(rstd[:, :], lnt[:, :], ACT.Exp, scale=-0.5), rstd_ready)
            if after:
                nc.scalar.preload_act_table(after)
            if m == 7:
                return
            for j in range(KD):
                act.wait_ge(t_ready, KD * m + j + 1)
                shift = mod[:, 24 * m + j:24 * m + j + 1] if m < 6 else small[:, 7:8]
                line(nc.scalar.activation(h_hi[:, j, :], tmp[:, j % 4, :], ACT.Identity, bias=shift), hhi_ready)

        def norm_dve(dve, line, m):
            if m < 6:
                line(nc.vector.tensor_scalar(scale_col[:, :], mod[:, 24 * m + 8:24 * m + 16], 1.0, None, ALU.add))
                line(nc.vector.tensor_scalar(gate_col[:, :], mod[:, 24 * m + 16:24 * m + 24],
                                             1.0 if m % 3 == 1 else 0.5, None, ALU.mult))
                line.settle()
                line(nc.vector.tensor_tensor(scale_col[:, :], scale_col[:, :], cols[:, 0, 8 * m:8 * m + 8], ALU.mult))
            else:
                line(nc.vector.tensor_copy(scale_col[:, :], cols[:, 0, 8 * m:8 * m + 8]))
                line(nc.vector.memset(gate_col[:, :], 1.0))
            dve.wait_ge(rstd_ready, m + 1)
            line(nc.vector.memset(sumsq[:, :], 0.0))
            line.settle()
            if m == 7:
                return

            def lower(j):
                dve.wait_ge(hhi_ready, KD * m + j + 1)
                shift = mod[:, 24 * m + j:24 * m + j + 1] if m < 6 else small[:, 7:8]
                line(nc.vector.scalar_tensor_tensor(out=h_lo[:, j, :], in0=tmp[:, j % 4, :], scalar=shift,
                                                    in1=h_hi[:, j, :].bitcast(F32), op0=ALU.add,
                                                    op1=ALU.subtract), h_ready)
            for j in range(KD):
                if j >= 4:
                    dve.wait_ge(h_ready, KD * m + j - 3)
                line(nc.vector.scalar_tensor_tensor(out=tmp[:, j % 4, :], in0=xT[:, j, :],
                                                    scalar=scale_col[:, j:j + 1], in1=rstd[:, :],
                                                    op0=ALU.mult, op1=ALU.mult), t_ready)
                if j:
                    lower(j - 1)
            lower(KD - 1)

        NORM_OF = {"F0": 0, "QKV": 1, "F1": 2, "F2": 3, "HIN": 4, "F3": 5, "P2": 6}
        RES_OF = {"F0": 1, "WO": 2, "F1": 3, "F2": 4, "HO": 5, "F3": 6, "OUT": 7}

        def ffn_pe(pe, name, fidx, q0, parts):
            n0 = FIRST[name]
            hb = KD * NORM_OF[name]

            def up(n, i, m, with_ada):
                for s in range(2):
                    pe.wait_ge(g_ready, plus(i, 2, 1 + KF * fidx + 2 * m + s))
                    for b in range(2):
                        product(pe, n + 2 * s + b, B[2 * s + b][:, :], H_TILES, i,
                                (h_ready, hb + 1) if s == b == 0 else None)
                if with_ada:
                    ada_pe(pe, q0 + m, i)
            if parts:
                with pe.Fori(0, parts) as i:
                    up(n0, i, 0, True)
            with pe.Fori(0, KF // 2 - parts) as i:
                up(n0 + 4 * parts, i, parts, False)
            pe.wait_ge(g_ready, 2 + KF * (fidx + 1))
            xb = KD * RES_OF[name]
            with pe.Fori(0, KD // 2) as i:
                for s in range(2):
                    pe.wait_ge(x_ready, plus(i, 2, xb + s - 1))
                    bank = B[s][:, :]
                    for b in range(2):
                        n = n0 + UP + 2 * s + b
                        pe.wait_ge(lo_ready, plus(i, 4, n + 1))
                        for k in range(KH):
                            f = b * KH + k
                            wh, wl = w_hi[:, n % 2, k * P:(k + 1) * P], w_lo[:, n % 2, k * P:(k + 1) * P]
                            nc.tensor.matmul(bank, wh, g_hi[:, f, :], start=(f == 0), stop=False)
                            nc.tensor.matmul(bank, wh, g_lo[:, f, :], start=False, stop=False)
                            last = nc.tensor.matmul(bank, wl, g_hi[:, f, :], start=False, stop=(f == KF - 1))
                        last.then_inc(used, 1)

        def ada_pe(pe, q, i=None):
            pe.wait_ge(ada_used, plus(i, 8, 8 * q + 8))
            for j in range(KD):
                col = B[4][:, bass.ds(plus(i, 8, 8 * q + j), 1)] if i is not None else B[4][:, 8 * q + j:8 * q + j + 1]
                last = nc.tensor.matmul(col, ada_sum[:, j * P:(j + 1) * P], ones[:, 0:1], start=True, stop=True)
            last.then_inc(ada_done, 1)

        def ada_dve(dve, line, q, kk, i=None):
            dve.wait_ge(ada_landed[kk % 4], plus(i, 32, 16 * (2 * q + kk // 4 + 1)))
            if kk == 0:
                if q or i is not None:
                    dve.wait_ge(ada_done, plus(i, 1, q))
                line(nc.vector.tensor_scalar(ada_sum[:, :], ada[:, 0, :], cact[:, 0:1], None, ALU.mult), ada_used)
            else:
                dve.wait_ge(ada_used, plus(i, 8, 8 * q + kk))
                line(nc.vector.scalar_tensor_tensor(out=ada_sum[:, :], in0=ada[:, kk % 4, :],
                                                    scalar=cact[:, kk:kk + 1], in1=ada_sum[:, :],
                                                    op0=ALU.mult, op1=ALU.add), ada_used)

        def ada_take(dve, line, q0, parts):
            dve.wait_ge(ada_done, q0 + parts)
            a, b = 8 * q0, 8 * (q0 + parts)
            m = min(b, P)
            if a < m:
                line(nc.vector.tensor_tensor(mod[:, a:m], B[4][:, a:m], cols[:, 1, a:m], ALU.add))
            if b > P:
                line(nc.vector.tensor_tensor(mod[:, P:b], B[4][:, P:b], cols[:, 0, C_AB:C_AB + b - P], ALU.add))
            line.settle()

        def ffn_act(act, line, name, fidx, parts):
            n0 = FIRST[name]

            def up(n, i, m):
                for s in range(2):
                    split_hi(act, line, n + 2 * s + 1, i)
                    split_hi(act, line, n + 2 * s + 2, i)
                    f0 = KF * fidx + 2 * m + s
                    act.wait_ge(used, plus(i, 4, n + 2 * s + 2))
                    if f0:
                        act.wait_ge(gt_ready, plus(i, 2, f0))
                    line(nc.scalar.activation(sq[:, :], B[2 * s][:, :], ACT.Silu), silu_ready)
                    act.wait_ge(gt_ready, plus(i, 2, f0 + 1))
                    fi = g_hi[:, bass.ds(plus(i, 2, 2 * m + s), 1), :].rearrange("p a n -> p (a n)")
                    line(nc.scalar.activation(fi, tmp[:, s, :], ACT.Copy), ghi_ready)
            if n0 == 0:
                up(n0, None, 0)
            k = 1 if n0 == 0 else 0
            line.loop(k, KF // 2 - 1, lambda i: up(n0 + 4 * k, i, k), ((hi_ready, 4), (silu_ready, 2), (ghi_ready, 2)))
            up(n0 + 4 * (KF // 2 - 1), None, KF // 2 - 1)
            xb = KD * RES_OF[name]

            def down(n, i, m):
                for s in range(2):
                    split_hi(act, line, n + 2 * s + 1, i)
                    split_hi(act, line, n + 2 * s + 2, i)
                    residual_act(act, line, xb + 2 * m + s + 1, 2 * m + s, i)
            line.loop(0, KD // 2 - 1, lambda i: down(n0 + UP, i, 0), ((hi_ready, 4), (sq_ready, 2)))
            down(n0 + UP + 4 * (KD // 2 - 1), None, KD // 2 - 1)

        def ffn_dve(dve, line, name, fidx, q0, parts):
            n0 = FIRST[name]

            def up(n, i, m, with_ada):
                for s in range(2):
                    split_lo(dve, line, n + 2 * s + 1, i)
                    if with_ada:
                        for kk in range(4 * s, 4 * s + 2):
                            ada_dve(dve, line, q0 + m, kk, i)
                    split_lo(dve, line, n + 2 * s + 2, i)
                    f0 = KF * fidx + 2 * m + s
                    dve.wait_ge(silu_ready, plus(i, 2, f0 + 1))
                    dve.wait_ge(g_ready, plus(i, 2, f0 + 2))
                    line(nc.vector.tensor_tensor(tmp[:, s, :], sq[:, :], B[2 * s + 1][:, :], ALU.mult), gt_ready)
                    if with_ada:
                        for kk in range(4 * s + 2, 4 * s + 4):
                            ada_dve(dve, line, q0 + m, kk, i)
                    dve.wait_ge(ghi_ready, plus(i, 2, f0 + 1))
                    f = bass.ds(plus(i, 2, 2 * m + s), 1)
                    line(nc.vector.tensor_tensor(g_lo[:, f, :].rearrange("p a n -> p (a n)"), tmp[:, s, :],
                                                 g_hi[:, f, :].rearrange("p a n -> p (a n)").bitcast(F32),
                                                 ALU.subtract), g_ready)
            per = ((lo_ready, 4), (gt_ready, 2), (g_ready, 2))
            line.loop(0, parts, lambda i: up(n0, i, 0, True), per + ((ada_used, 8),))
            line.loop(parts, KF // 2 - 1, lambda i: up(n0 + 4 * parts, i, parts, False), per)
            up(n0 + 4 * (KF // 2 - 1), None, KF // 2 - 1, False)
            if parts:
                ada_take(dve, line, q0, parts)

            def down(n, i, m):
                for s in range(2):
                    split_lo(dve, line, n + 2 * s + 1, i)
                    split_lo(dve, line, n + 2 * s + 2, i)
                    residual_dve(dve, line, n + 2 * s + 1, 2 * m + s, i)
            line.loop(0, KD // 2 - 1, lambda i: down(n0 + UP, i, 0), ((lo_ready, 4), (x_ready, 2), (sum_ready, 2)))
            down(n0 + UP + 4 * (KD // 2 - 1), None, KD // 2 - 1)

        def back_pe(pe, name, ybase, tiles, rows_of=None):
            xb = KD * RES_OF[name]
            for j in range(KD):
                if j >= 2:
                    pe.wait_ge(x_ready, xb + j - 1)
                if j == 0:
                    pe.wait_ge(y_ready, ybase)
                xs = [tuple(half[0:(rows_of[k] if rows_of else P)] for half in y_pair(k)) for k in range(tiles)]
                product(pe, FIRST[name] + j, B[j % 2][:, :], xs, rows_of=rows_of)

        def back_act(act, line, name):
            for j in range(KD):
                split_hi(act, line, FIRST[name] + j + 1)
                residual_act(act, line, KD * RES_OF[name] + j + 1, j)

        def back_dve(dve, line, name):
            for j in range(KD):
                split_lo(dve, line, FIRST[name] + j + 1)
                residual_dve(dve, line, FIRST[name] + j, j)

        def rows_pe(pe, base, heads, comps, q_of, k_of, v_of, o_rows):
            units = [(h, i) for h in range(heads) for i in range(TT)]

            def scores(u):
                h, i = units[u]
                w = (i + 1) * P
                if u >= 2:
                    pe.wait_ge(S_max, base + u - 1)
                for cc in range(comps):
                    last = nc.tensor.matmul(B[2 * (u % 2) + cc][:, 0:w], q_of(h, cc)[:, i * P:(i + 1) * P],
                                            k_of(h, cc)[:, 0:w], start=True, stop=True)
                last.then_inc(S_ps, 1)

            def turn(u):
                h, i = units[u]
                pe.wait_ge(a_ready, base + u + 1)
                if u >= 2:
                    pe.wait_ge(aT_sb, base + u - 1)
                for k in range(i + 1):
                    last = nc.tensor.transpose(B[4 + u % 2][:, k * P:(k + 1) * P],
                                               a_of(comps)[:, u % 3, 0, k * P:(k + 1) * P], ident[:, :])
                last.then_inc(aT_ps, 1)

            def values(u):
                h, i = units[u]
                pe.wait_ge(aT_sb, base + u + 1)
                if i == 0:
                    finish_wait(pe, h)
                r = o_rows(h)
                for k in range(i + 1):
                    last = nc.tensor.matmul(B[6][r, i * P:(i + 1) * P], v_of(h, k),
                                            (at1 if comps == 2 else at2)[:, u % 2, k * P:(k + 1) * P],
                                            start=(k == 0), stop=(k == i))
                last.then_inc(pv_done, 1)

            def finish_wait(pe, h):
                if comps == 2 and h:
                    pe.wait_ge(o_sq, h)
                if comps == 1 and h and h % 2 == 0:
                    pe.wait_ge(o_sq, O2 + h // 2)

            def sums(h):
                pe.wait_ge(o_sq, h + 1)
                if h:
                    pe.wait_ge(o_rs, h)
                nc.tensor.matmul(B[7][:, :], ones[:, :], sq[:, :], start=True, stop=True).then_inc(o_ss, 1)

            n = len(units)
            for u in range(n + 3):
                if u < n:
                    scores(u)
                if 1 <= u < n + 1:
                    turn(u - 1)
                if 2 <= u < n + 2:
                    values(u - 2)
                if comps == 2 and u >= 3 and units[u - 3][1] == TT - 1:
                    sums(units[u - 3][0])

        def a_of(comps):
            return s1 if comps == 2 else s2

        def m_col(u, cc):
            return small[:, 24 + 2 * (u % 3) + cc:25 + 2 * (u % 3) + cc]

        def l_col(u, cc):
            return small[:, 32 + 2 * (u % 3) + cc:33 + 2 * (u % 3) + cc]

        def rows_dve(dve, line, base, heads, comps, after):
            units = [(h, i) for h in range(heads) for i in range(TT)]
            s_t = a_of(comps)
            toep = toep1 if comps == 2 else toep2

            def maxima(u):
                h, i = units[u]
                w = (i + 1) * P
                dve.wait_ge(S_ps, base + u + 1)
                if u >= 3:
                    dve.wait_ge(aT_ps, base + u - 2)
                for cc in range(comps):
                    bias = toep[:, h, T - w:T]
                    if comps == 2:
                        line(nc.vector.tensor_tensor_reduce(out=s_t[:, u % 3, cc, 0:w], in0=B[2 * (u % 2) + cc][:, 0:w],
                                                            in1=bias, scale=1.0, scalar=LOW, op0=ALU.add, op1=ALU.max,
                                                            accum_out=m_col(u, cc)))
                    else:
                        line(nc.vector.scalar_tensor_tensor(out=s_t[:, u % 3, 0, 0:w], in0=B[2 * (u % 2)][:, 0:w],
                                                            scalar=HD ** -0.5, in1=bias, op0=ALU.mult, op1=ALU.add))
                        line.settle()
                        line(nc.vector.tensor_tensor_reduce(out=s_t[:, u % 3, 0, 0:w], in0=s_t[:, u % 3, 0, 0:w],
                                                            in1=chosen[:, i, 0:w], scale=1.0, scalar=LOW, op0=ALU.add,
                                                            op1=ALU.max, accum_out=m_col(u, 0)))
                line.settle()
                c0 = 24 + 2 * (u % 3)
                line(nc.vector.tensor_scalar(small[:, c0:c0 + comps], small[:, c0:c0 + comps], -1.0, None, ALU.mult), S_max)

            def weights(u):
                h, i = units[u]
                w = (i + 1) * P
                dve.wait_ge(p_ready, base + u + 1)
                c0 = 32 + 2 * (u % 3)
                line(nc.vector.reciprocal(small[:, c0:c0 + comps], small[:, c0:c0 + comps]))
                line.settle()
                if comps == 1:
                    line(nc.vector.tensor_scalar(s_t[:, u % 3, 0, 0:w], s_t[:, u % 3, 0, 0:w], l_col(u, 0), None,
                                                 ALU.mult), a_ready)
                    return
                line(nc.vector.tensor_scalar(l_col(u, 1), l_col(u, 1), nlam_c, None, ALU.mult))
                line(nc.vector.tensor_scalar(s_t[:, u % 3, 0, 0:w], s_t[:, u % 3, 0, 0:w], l_col(u, 0), None, ALU.mult))
                line.settle()
                line(nc.vector.scalar_tensor_tensor(out=s_t[:, u % 3, 0, 0:w], in0=s_t[:, u % 3, 1, 0:w],
                                                    scalar=l_col(u, 1), in1=s_t[:, u % 3, 0, 0:w], op0=ALU.mult,
                                                    op1=ALU.add), a_ready)
            n = len(units)
            for u in range(n + 8):
                if u < n:
                    maxima(u)
                if 1 <= u < n + 1:
                    weights(u - 1)
                for lag, step in after:
                    if lag <= u < n + lag and units[u - lag][1] == TT - 1:
                        step(units[u - lag][0])

        def rows_act(act, line, base, pv_base, heads, comps, after):
            units = [(h, i) for h in range(heads) for i in range(TT)]
            s_t = a_of(comps)
            at = at1 if comps == 2 else at2

            def exps(u):
                h, i = units[u]
                w = (i + 1) * P
                act.wait_ge(S_max, base + u + 1)
                for cc in range(comps):
                    line(nc.scalar.activation(s_t[:, u % 3, cc, 0:w], s_t[:, u % 3, cc, 0:w], ACT.Exp,
                                              bias=m_col(u, cc), accum_out=l_col(u, cc)),
                         p_ready if cc == comps - 1 else None)

            def copies(u):
                h, i = units[u]
                w = (i + 1) * P
                act.wait_ge(aT_ps, base + u + 1)
                if u >= 2:
                    act.wait_ge(pv_done, pv_base + u - 1)
                line(nc.scalar.activation(at[:, u % 2, 0:w], B[4 + u % 2][:, 0:w], ACT.Copy), aT_sb)
            n = len(units)
            for u in range(n + 8):
                if u < n:
                    exps(u)
                if 1 <= u < n + 1:
                    copies(u - 1)
                for lag, step in after:
                    if lag <= u < n + lag and units[u - lag][1] == TT - 1:
                        step(units[u - lag][0])

        def head_out_act(act, line, m, osb, pv):
            act.wait_ge(pv_done, pv)
            if m:
                act.wait_ge(o_ss, m)
                act.wait_ge(y_t, m)
            line(nc.scalar.activation(osb, B[6][:, :], ACT.Copy))
            line(nc.scalar.activation(sq[:, :], B[6][:, :], ACT.Square), o_sq)

        def head_rs_act(act, line, m):
            act.wait_ge(o_ss, m + 1)
            if m:
                act.wait_ge(y_t, m)
            line(nc.scalar.activation(lnt[:, :], B[7][:, :], ACT.Ln, bias=eps_c, scale=1.0 / P))
            line.settle()
            line(nc.scalar.activation(rstd[:, :], lnt[:, :], ACT.Exp, scale=-0.5), o_rs)

        def head_hi_act(act, line, m, tile):
            act.wait_ge(y_t, m + 1)
            line(nc.scalar.activation(h_hi[:, tile, :], tmp[:, 0, :], ACT.Copy), y_hi)

        def head_out_dve(dve, line, m, osb, gain, gate=None):
            dve.wait_ge(o_rs, m + 1)
            dve.wait_ge(y_ready, m)
            if gate is None:
                line(nc.vector.scalar_tensor_tensor(out=tmp[:, 0, :], in0=osb, scalar=gain, in1=rstd[:, :],
                                                    op0=ALU.mult, op1=ALU.mult), y_t)
            else:
                line(nc.vector.scalar_tensor_tensor(out=tmp[:, 1, :], in0=osb, scalar=gain, in1=rstd[:, :],
                                                    op0=ALU.mult, op1=ALU.mult))
                line.settle()
                line(nc.vector.tensor_tensor(tmp[:, 0, :], tmp[:, 1, :], gate, ALU.mult), y_t)

        def head_lo_dve(dve, line, m, tile):
            dve.wait_ge(y_hi, m + 1)
            line(nc.vector.tensor_tensor(h_lo[:, tile, :], tmp[:, 0, :], h_hi[:, tile, :].bitcast(F32),
                                         ALU.subtract), y_ready)

        O2 = 2 * HEADS + GH

        def qkv_pe(pe):
            n0 = FIRST["QKV"]
            for b in range(24):
                n = n0 + b
                if 4 <= b < 20:
                    pe.wait_ge(headsq, b - 3)
                elif b >= 20:
                    pe.wait_ge(epi_free, b - 19)
                if b < 16:
                    product(pe, n, B[b % 4][:, :], H_TILES, waits=(h_ready, KD * 1 + 1) if b == 0 else None)
                else:
                    product_rows(pe, n, B[b % 4])
                if 1 <= b <= 16:
                    pe.wait_ge(headsq, b)
                    if b >= 2:
                        pe.wait_ge(headrs, b - 1)
                    nc.tensor.matmul(B[5][:, :], halves[:, :], sq[:, :], start=True, stop=True).then_inc(headss, 1)

        def qkv_act(act, line):
            n0 = FIRST["QKV"]
            for b in range(25):
                if b < 24:
                    split_hi(act, line, n0 + b + 1)
                if 1 <= b <= 16:
                    m = b - 1
                    act.wait_ge(headss, m + 1)
                    if m:
                        act.wait_ge(headn, m)
                    line(nc.scalar.activation(lnt[:, :], B[5][:, :], ACT.Ln, bias=eps_c, scale=1.0 / HD))
                    line.settle()
                    line(nc.scalar.activation(rstd[:, :], lnt[:, :], ACT.Exp, scale=-0.5), headrs)
                if b < 16:
                    dst = (aq if b < 8 else ak)[:, b % 8, :]
                    act.wait_ge(used, n0 + b + 1)
                    if b:
                        act.wait_ge(headss, b)
                    line(nc.scalar.activation(dst, B[b % 4][:, :], ACT.Copy))
                    line(nc.scalar.activation(sq[:, :], B[b % 4][:, :], ACT.Square), headsq)
                elif b < 24:
                    act.wait_ge(used, n0 + b + 1)
                    line(nc.scalar.activation(av[:, :, (b - 16) * P:(b - 15) * P],
                                              B[b % 4][:, :].rearrange("p (t n) -> p t n", n=P), ACT.Copy), epi_free)

        def qkv_dve(dve, line):
            n0 = FIRST["QKV"]
            for b in range(25):
                if b < 24:
                    split_lo(dve, line, n0 + b + 1)
                if 1 <= b <= 16:
                    m = b - 1
                    dst = (aq if m < 8 else ak)[:, m % 8, :]
                    gain = qg_c if m < 8 else cols[:, 0, C_KG:C_KG + 1]
                    dve.wait_ge(headrs, m + 1)
                    line(nc.vector.scalar_tensor_tensor(out=dst, in0=dst, scalar=gain, in1=rstd[:, :],
                                                        op0=ALU.mult, op1=ALU.mult), headn)

        def hin_pe(pe):
            n0 = FIRST["HIN"]
            for b, (kind, j) in enumerate(HORDER):
                if 4 <= b < 28:
                    pe.wait_ge(epi_free, 8 + b - 3)
                elif b >= 28:
                    pe.wait_ge(f_arg, b - 27)
                if kind == "v":
                    product_rows(pe, n0 + b, B[b % 4])
                else:
                    product(pe, n0 + b, B[b % 4][:, :], H_TILES, waits=(h_ready, KD * 4 + 1) if b == 0 else None)

        def hin_act(act, line):
            n0 = FIRST["HIN"]
            for b, (kind, j) in enumerate(HORDER):
                split_hi(act, line, n0 + b + 1)
                bank = B[b % 4]
                if kind == "f":
                    if j == 0:
                        nc.scalar.preload_act_table_set("natural_log_exp_and_others")
                    act.wait_ge(f_min, j + 1)
                    if j:
                        act.wait_ge(f_done, j)
                    line(nc.scalar.activation(tmp[:, 1, :], tmp[:, 0, :], ACT.Exp))
                    line.settle()
                    line(nc.scalar.activation(tmp[:, 2, :], tmp[:, 1, :], ACT.Ln, bias=one_c))
                    line(nc.scalar.activation(tmp[:, 3, :], tmp[:, 1, :], ACT.Ln, bias=one_c, scale=lb_c[:, j:j + 1]), f_log)
                    act.wait_ge(f_arg, j + 1)
                    line(nc.scalar.activation(tmp[:, 1, :], lnt[:, :], ACT.Exp), f_key)
                    continue
                act.wait_ge(used, n0 + b + 1)
                if kind == "q":
                    line(nc.scalar.activation(hq[:, j, :], bank[:, :], ACT.Copy), epi_free)
                elif kind == "g":
                    if j == 0:
                        nc.scalar.preload_act_table(ACT.Silu)
                    line(nc.scalar.activation(hg[:, j, :], bank[:, :], ACT.Silu), epi_free)
                else:
                    line(nc.scalar.activation(hv[:, :, j * P:(j + 1) * P],
                                              bank[:, :].rearrange("p (t n) -> p t n", n=P), ACT.Copy), epi_free)

        def hin_dve(dve, line):
            n0 = FIRST["HIN"]
            dve.wait_ge(phase_const, 1)
            for b, (kind, j) in enumerate(HORDER):
                split_lo(dve, line, n0 + b + 1)
                if kind != "f":
                    continue
                bank = B[b % 4]
                dve.wait_ge(used, n0 + b + 1)
                if j:
                    line.settle()
                line(nc.vector.tensor_scalar(tmp[:, 0, :], bank[:, :], -1.0, 40.0, ALU.mult, ALU.min), f_min)
                line(nc.vector.tensor_scalar(sumsq2[:, :], bank[:, :], -1.0, -40.0, ALU.mult, ALU.add))
                line.settle()
                dve.wait_ge(f_log, j + 1)
                line(nc.vector.scalar_tensor_tensor(out=tmp[:, 2, :], in0=sumsq2[:, :], scalar=0.0, in1=tmp[:, 2, :],
                                                    op0=ALU.max, op1=ALU.add))
                line.settle()
                line(nc.vector.scalar_tensor_tensor(out=lnt[:, :], in0=tmp[:, 2, :], scalar=-1.0, in1=bank[:, :],
                                                    op0=ALU.mult, op1=ALU.subtract), f_arg)
                line(nc.vector.tensor_tensor(tmp[:, 3, :], tmp[:, 3, :], tmp[:, 2, :], ALU.subtract))
                line.settle()
                line(nc.vector.tensor_tensor_scan(hG[:, j, :], reset[:, :], tmp[:, 3, :], 0.0, ALU.mult, ALU.add))
                dve.wait_ge(f_key, j + 1)
                line(nc.vector.tensor_scalar(hk[:, j, :], tmp[:, 1, :], lb1_c[:, j:j + 1], None, ALU.mult), f_done)

        sumsq2 = rstd

        def hgrn_pe(pe):
            nlev = LEVELS + 1
            pe.wait_ge(f_done, HEADS)
            pe.wait_ge(epi_free, 32)
            pe.wait_ge(phase_const, 1)

            def score(h, v):
                n = h * nlev + v
                if n >= 2:
                    pe.wait_ge(lv_P, n - 1)
                if v < LEVELS:
                    m = h * LEVELS + v
                    pe.wait_ge(lv_q, m + 1)
                    pe.wait_ge(lv_k, m + 1)
                    qs, ks = hqE[:, m % 2, :], hkE[:, m % 2, :]
                else:
                    qs, ks = hq[:, h, :], hk[:, h, :]
                for c_ in range(TT):
                    s = slice(c_ * P, (c_ + 1) * P)
                    last = nc.tensor.matmul(B[n % 2][:, s], ks[:, s], qs[:, s], start=True, stop=True)
                last.then_inc(lv_S, 1)

            def output(h, v):
                n = h * nlev + v
                if v == 0:
                    if h:
                        pe.wait_ge(o_sq, HEADS + h)
                    nc.tensor.matmul(B[6][:, :], ones[:, :], zero[:, :], start=True, stop=False, skip_group_check=True)
                pe.wait_ge(lv_P, n + 1)
                for c_ in range(TT):
                    s = slice(c_ * P, (c_ + 1) * P)
                    last = nc.tensor.matmul(B[6][:, s], hv[:, c_, h * P:(h + 1) * P], hP[:, n % 2, s],
                                            start=False, stop=False, skip_group_check=True)
                last.then_inc(lv_O, 1)

            for h in range(HEADS):
                for v in range(nlev):
                    score(h, v)
                    if v:
                        output(h, v - 1)
                    if v == 4:
                        pe.wait_ge(st_k, 2 * h + 2)
                        if h:
                            pe.wait_ge(st_n, h)
                        for c_ in range(TT - 1):
                            s = slice(c_ * P, (c_ + 1) * P)
                            last = nc.tensor.transpose(B[4][:, s], hkd[:, s], ident[:, :])
                        last.then_inc(st_T, 1)
                    if v == 6:
                        pe.wait_ge(st_n, h + 1)
                        if h:
                            pe.wait_ge(st_s, 3 * h)
                        for c_ in range(TT - 1):
                            s = slice(c_ * P, (c_ + 1) * P)
                            last = nc.tensor.matmul(B[5][:, s], hkn[:, s], hv[:, c_, h * P:(h + 1) * P],
                                                    start=True, stop=True)
                        last.then_inc(st_U, 1)
                output(h, nlev - 1)
                pe.wait_ge(st_s, 3 * h + 3)
                for c_ in range(1, TT):
                    s = slice(c_ * P, (c_ + 1) * P)
                    last = nc.tensor.matmul(B[6][:, s], hst[c_ - 1], hqG[:, s], start=False,
                                            stop=(c_ == TT - 1), skip_group_check=True)
                last.then_inc(pv_done, 1)
                pe.wait_ge(o_sq, HEADS + h + 1)
                if h:
                    pe.wait_ge(o_rs, HEADS + h)
                nc.tensor.matmul(B[7][:, :], ones[:, :], sq[:, :], start=True, stop=True).then_inc(o_ss, 1)

        def hgrn_act(act, line):
            def finish_a(h):
                head_out_act(act, line, HEADS + h, ho[:, :], pv_h(h) + 1)
                head_rs_act(act, line, HEADS + h)

            def finish_b(h):
                head_hi_act(act, line, HEADS + h, h)
            for h in range(HEADS):
                for v in range(LEVELS):
                    n = h * LEVELS + v
                    act.wait_ge(lv_D, n + 1)
                    line(nc.scalar.activation(hE[:, n % 2, :], hE[:, n % 2, :], ACT.Abs))
                    line.settle()
                    line(nc.scalar.activation(hE[:, n % 2, :], hE[:, n % 2, :], ACT.Exp, scale=-1.0), lv_E)
                    if v == 0:
                        if h:
                            act.wait_ge(st_k, 2 * h)
                            act.wait_ge(st_T, h)
                            act.wait_ge(st_s, 3 * h)
                        line(nc.scalar.activation(heG[:, :], hG[:, h, :], ACT.Exp))
                        for c_ in range(TT):
                            s = slice(c_ * P, (c_ + 1) * P)
                            line(nc.scalar.activation(hkd[:, s], hG[:, h, s], ACT.Exp, scale=-1.0,
                                                      bias=hG[:, h, (c_ + 1) * P - 1:(c_ + 1) * P]),
                                 st_E if c_ == TT - 1 else None)
                    if v == 1 and h:
                        finish_a(h - 1)
                    if v == 3 and h:
                        finish_b(h - 1)
                    if v == 5:
                        act.wait_ge(st_T, h + 1)
                        if h:
                            act.wait_ge(st_U, h)
                        line(nc.scalar.activation(hkn[:, 0:3 * P], B[4][:, 0:3 * P], ACT.Copy), st_n)
            finish_a(HEADS - 1)
            finish_b(HEADS - 1)

        def hgrn_dve(dve, line):
            nlev = LEVELS + 1
            dve.wait_ge(toep_in, 32)

            def dist(h, v):
                n = h * LEVELS + v
                if n >= 2:
                    dve.wait_ge(lv_k, n - 1)
                    dve.wait_ge(lv_q, n - 1)
                half = 1 << v
                Gv = hG[:, h, :].rearrange("p (b w) -> p b w", w=2 * half)
                ref = Gv[:, :, half - 1:half].broadcast_to((P, T // (2 * half), 2 * half))
                line(nc.vector.tensor_tensor(hE[:, n % 2, :].rearrange("p (b w) -> p b w", w=2 * half), Gv, ref,
                                             ALU.subtract), lv_D)

            def query(h, v):
                n = h * LEVELS + v
                dve.wait_ge(lv_E, n + 1)
                if n >= 2:
                    dve.wait_ge(lv_S, level_at(n - 2))
                line(nc.vector.tensor_tensor(hqE[:, n % 2, :], hq[:, h, :], hE[:, n % 2, :], ALU.mult), lv_q)

            def mask(h, v):
                n = h * nlev + v
                dve.wait_ge(lv_S, n + 1)
                if n >= 2:
                    dve.wait_ge(lv_O, n - 1)
                m = masks[:, v:v + 1, :].broadcast_to((P, TT, P))
                line(nc.vector.tensor_tensor(hP[:, n % 2, :].rearrange("p (c t) -> p c t", t=P),
                                             B[n % 2][:, :].rearrange("p (c t) -> p c t", t=P), m, ALU.mult), lv_P)

            def finish(h):
                head_out_dve(dve, line, HEADS + h, ho[:, :], cols[:, 0, C_HG + h:C_HG + h + 1], hg[:, h, :])
                head_lo_dve(dve, line, HEADS + h, h)
            for h in range(HEADS):
                if h == 0:
                    dist(0, 0)
                for v in range(nlev):
                    if v + 1 < LEVELS:
                        dist(h, v + 1)
                    elif v == LEVELS and h + 1 < HEADS:
                        dist(h + 1, 0)
                    if v < LEVELS:
                        query(h, v)
                    if v:
                        mask(h, v - 1)
                    if v == 3 and h:
                        finish(h - 1)
                mask(h, nlev - 1)
                dve.wait_ge(st_U, h + 1)
                if h:
                    dve.wait_ge(pv_done, pv_h(h))
                line(nc.vector.tensor_copy(hst[0], B[5][:, 0:P]), st_s)
                for c_ in range(1, TT - 1):
                    dve.wait_ge(st_s, 3 * h + c_)
                    line(nc.vector.scalar_tensor_tensor(out=hst[c_], in0=hst[c_ - 1],
                                                        scalar=heG[:, (c_ + 1) * P - 1:(c_ + 1) * P],
                                                        in1=B[5][:, c_ * P:(c_ + 1) * P], op0=ALU.mult, op1=ALU.add), st_s)
            finish(HEADS - 1)

        E2 = 32
        U2, PV2 = HEADS * TT, HEADS * TT + HEADS
        M2 = 2 * HEADS
        GATES = ("ggate", "dgate", "pgate")

        def second_pool(pool, line):
            g = nc.gpsimd
            line.settle()
            line(g.memset(w2[:, :, :], 0.0))
            line.settle()
            line(g.memset(poolw[:, :, :], 0.0))
            line.settle()
            line(g.memset(zero2[:, :], 0.0))
            line.settle()
            line(g.memset(reset2[:, :], 1.0))
            line.settle()
            line(g.memset(reset2[:, 0:T:64], 0.0), phase_const)
            for t in range(2):
                for m in range(2):
                    c0 = 2 * GK * t + GK * m
                    pool.dma_start(w2[:, t, 64 * m:64 * m + GK], gla_gate_w2_2[0, :, c0:c0 + GK]).then_inc(small_in, 16)
                    pool.dma_start(poolw[64 * m:64 * m + 64, t, 64 * m:64 * m + 64],
                                   pool_w_2[0, 2 * t + m, :, :]).then_inc(small_in, 16)
            pool.dma_start(poolc[:, :, :], pool_counts).then_inc(small_in, 16)
            for h in range(GH):
                pool.wait_ge(gl_a, h + 1)
                am = at2[:, h % 2, :].rearrange("p (t n) -> p t n", n=P)
                line.settle()
                line(g.affine_select(out=am, in_=am, compare_op=ALU.is_ge, fill=0.0, base=0,
                                     pattern=[[0, TT], [1, P]], channel_multiplier=-1))
                line.settle()
                line(g.memset(am[0:64, :, 64:P], 0.0), gl_m)
            for i in range(1, TT):
                pool.wait_ge(ix_a, IH * i)
                w = (i + 1) * P
                line.settle()
                line(g.affine_select(out=work[:, 4, 0:w], in_=work[:, 4, 0:w], compare_op=ALU.is_ge, fill=LOW,
                                     base=i * P, pattern=[[-1, w]], channel_multiplier=1), ix_c)

        def y_pair(k):
            return (h_hi[:, k, :], h_lo[:, k, :]) if k < KD else (y8_hi[:, :], y8_lo[:, :])

        def y_act(act, line, m, tile, r=P):
            act.wait_ge(y_t, m + 1)
            line(nc.scalar.activation(y_pair(tile)[0][0:r], tmp[0:r, 0, :], ACT.Copy), y_hi)

        def y_dve(dve, line, m, tile, r=P):
            dve.wait_ge(y_hi, m + 1)
            hi, lo = y_pair(tile)
            line(nc.vector.tensor_tensor(lo[0:r], tmp[0:r, 0, :], hi[0:r].bitcast(F32), ALU.subtract), y_ready)

        def second_pe(pe):
            t_ = nc.tensor
            n0 = FIRST["P2"]
            for b, (kind, t, _) in enumerate(SECOND):
                if b >= 4:
                    pe.wait_ge(epi_free, E2 + b - 3)
                if kind in NATURAL:
                    product_rows(pe, n0 + b, B[b % 4], IH if kind == "wi" else P)
                else:
                    product(pe, n0 + b, B[b % 4][:, :], H_TILES, waits=(h_ready, KD * 6 + 1) if b == 0 else None)
            pe.wait_ge(epi_free, E2 + len(SECOND))
            pe.wait_ge(small_in, 16 * 9)
            for t in range(2):
                last = t_.matmul(B[t][:, :], w2[:, t, :], z["gz"][0:16, :], start=True, stop=True)
            last.then_inc(gl_z, 1)
            for t in range(2):
                pe.wait_ge(gl_q, t + 1)
                for c_ in range(TT):
                    s = slice(c_ * P, (c_ + 1) * P)
                    last = t_.transpose(B[4][:, s], work[:, t, s], ident[:, :])
                last.then_inc(gl_T, 1)
                pe.wait_ge(gl_n, t + 1)
                if t:
                    pe.wait_ge(gl_s, t)
                for ch in range(7):
                    r0, bank = 64 * (ch % 2), B[5 + 2 * (ch % 2)]
                    for r in range(2):
                        h = 2 * t + r
                        last = t_.matmul(bank[64 * r:64 * r + 64, (ch // 2) * GV:(ch // 2 + 1) * GV],
                                         work[r0:r0 + 64, 2 + t, (ch // 2) * P + 64 * r:(ch // 2) * P + 64 * r + 64],
                                         z["gv"][r0:r0 + 64, ch // 2, h * GV:(h + 1) * GV], start=True, stop=True)
                last.then_inc(gl_U, 1)
                for r in range(2):
                    h = 2 * t + r
                    rows_ = slice(64 * r, 64 * r + GK)
                    if h >= 2:
                        pe.wait_ge(gl_a, h - 1)
                    for c_ in range(TT):
                        s = slice(c_ * P, (c_ + 1) * P)
                        last = t_.matmul(B[h % 2][:, s], z["gk"][rows_, t, s], z["gq"][rows_, t, s],
                                         start=True, stop=True)
                    last.then_inc(gl_A, 1)
                for r in range(2):
                    h = 2 * t + r
                    rows_ = slice(64 * r, 64 * r + GK)
                    pe.wait_ge(gl_m, h + 1)
                    pe.wait_ge(gl_s, t + 1)
                    if h:
                        pe.wait_ge(o_sq, M2 + h)
                    for c_ in range(TT):
                        s = slice(c_ * P, (c_ + 1) * P)
                        t_.matmul(B[6][0:GV, s], z["gv"][:, c_, h * GV:(h + 1) * GV], at2[:, h % 2, s],
                                  start=True, stop=False)
                        for ch in (2 * c_, 2 * c_ + 1):
                            if ch:
                                last = t_.matmul(B[6][0:GV, ch * 64:(ch + 1) * 64], gst[rows_, ch, :],
                                                 z["gq"][rows_, t, ch * 64:(ch + 1) * 64], start=False,
                                                 stop=(ch % 2 == 1))
                    last.then_inc(pv_done, 1)
                    pe.wait_ge(o_sq, M2 + h + 1)
                    if h:
                        pe.wait_ge(o_rs, M2 + h)
                    t_.matmul(B[3][:, :], ones[0:GV, :], sq[0:GV, :], start=True, stop=True).then_inc(o_ss, 1)
            for t in range(2):
                pe.wait_ge(pl_d, t + 1)
                t_.matmul(B[2][:, :] if t else B[5][:, :], poolw[:, t, :], work[:, 4 + t, :],
                          start=True, stop=True).then_inc(pl_y, 1)
            pe.wait_ge(y_ready, M2 + GH + 2)
            for i in range(1, TT):
                if i > 1:
                    pe.wait_ge(ix_r, IH * (i - 1))
                for h in range(IH):
                    r = slice(32 * h, 32 * h + 32)
                    last = t_.matmul(B[h][:, 0:(i + 1) * P], z["qi"][r, i * P:(i + 1) * P],
                                     z["ki"][r, 0:(i + 1) * P], start=True, stop=True, tile_position=(32 * h, 0))
                last.then_inc(ix_S, 1)
            pe.wait_ge(ix_r, IH * (TT - 1))
            rows_pe(pe, U2, DH, 1,
                    lambda h, cc: z["dq"][64 * (h % 2):64 * (h % 2) + 64, h // 2, :],
                    lambda h, cc: z["dk"][64 * (h % 2):64 * (h % 2) + 64, h // 2, :],
                    lambda h, k: z["dv"][:, k, h * HD:(h + 1) * HD],
                    lambda h: slice(64 * (h % 2), 64 * (h % 2) + 64))

        def second_act(act, line):
            s_ = nc.scalar
            n0 = FIRST["P2"]
            for b, (kind, t, _) in enumerate(SECOND):
                split_hi(act, line, n0 + b + 1)
                act.wait_ge(used, n0 + b + 1)
                bank = B[b % 4]
                if kind == "ggate" and t == 0:
                    nc.scalar.preload_act_table(ACT.Silu)
                if kind == "wi":
                    line(s_.activation(z["wi"][:, :, :], bank[:, 0:TT * IH].rearrange("p (t n) -> p t n", n=IH),
                                       ACT.Copy, scale=IH ** -0.5), epi_free)
                elif kind in NATURAL:
                    line(s_.activation(z[kind][:, :, t * P:(t + 1) * P],
                                       bank[:, :].rearrange("p (t n) -> p t n", n=P), ACT.Copy), epi_free)
                else:
                    dst = z[kind][:, :] if kind in ("qi", "ki", "gz") else z[kind][:, t, :]
                    line(s_.activation(dst, bank[:, :], ACT.Silu if kind in GATES else ACT.Copy), epi_free)
            nc.scalar.preload_act_table_set("natural_log_exp_and_others")
            for t in range(2):
                act.wait_ge(gl_u, t + 1)
                line(s_.activation(tmp[:, 2 + t, :], tmp[:, 2 + t, :], ACT.Exp))
                line.settle()
                line(s_.activation(tmp[:, 2 + t, :], tmp[:, 2 + t, :], ACT.Ln, bias=one_c), gl_l)
            for t in range(2):
                act.wait_ge(gl_b, t + 1)
                if t:
                    act.wait_ge(gl_s, t)
                    act.wait_ge(gl_q, t)
                bt = tmp[:, t, :]
                line(s_.activation(gE[:, 0, :], bt, ACT.Exp, scale=-1.0 / 16))
                line(s_.activation(gE[:, 1, :], bt, ACT.Exp, scale=1.0 / 16))
                for ch in range(8):
                    s = slice(64 * ch, 64 * ch + 64)
                    line(s_.activation(gE[:, 2, s], tmp[:, t, s], ACT.Exp, scale=1.0 / 16,
                                       bias=gend[:, t, ch:ch + 1]), gl_e if ch == 7 else None)
                act.wait_ge(gl_T, t + 1)
                line(s_.activation(work[:, 2 + t, :], B[4][:, :], ACT.Copy), gl_n)
                for r in range(2):
                    h = 2 * t + r
                    act.wait_ge(gl_A, h + 1)
                    if h >= 2:
                        act.wait_ge(pv_done, PV2 + h - 1)
                    line(s_.activation(at2[:, h % 2, :], B[h % 2][:, :], ACT.Copy), gl_a)
                for r in range(2):
                    h = 2 * t + r
                    m = M2 + h
                    act.wait_ge(pv_done, PV2 + h + 1)
                    act.wait_ge(o_ss, m)
                    act.wait_ge(y_t, m)
                    line(s_.activation(o2[0:GV, 0, :], B[6][0:GV, :], ACT.Copy))
                    line(s_.activation(sq[0:GV, :], B[6][0:GV, :], ACT.Square), o_sq)
                    act.wait_ge(o_ss, m + 1)
                    line(s_.activation(lnt[0:GV, :], B[3][0:GV, :], ACT.Ln, bias=eps_c[0:GV], scale=1.0 / GV))
                    line.settle()
                    line(s_.activation(rstd[0:GV, :], lnt[0:GV, :], ACT.Exp, scale=-0.5), o_rs)
                    y_act(act, line, m, h, GV)
            bias_tiles(act, toep2[:, :, :], 1, DH)
            for t in range(2):
                y_act(act, line, M2 + GH + t, 7 + t)
            for i in range(1, TT):
                act.wait_ge(ix_S, i)
                if i > 1:
                    act.wait_ge(ix_a, IH * (i - 1))
                for h in range(IH):
                    line(s_.activation(work[:, h, 0:(i + 1) * P], B[h][:, 0:(i + 1) * P], ACT.Relu,
                                       scale=32.0 ** -0.5), ix_r)

            def out_pair(h):
                if h % 2 == 0:
                    return
                act.wait_ge(pv_done, PV2 + GH + TT * (h + 1))
                act.wait_ge(y_t, M2 + GH + 2 + h // 2)
                line(s_.activation(o2[:, (h // 2) % 2, :], B[6][:, :], ACT.Copy), o_sq)

            def hi_pair(h):
                if h % 2:
                    y_act(act, line, M2 + GH + 2 + h // 2, 4 + h // 2)
            rows_act(act, line, U2, PV2 + GH, DH, 1, ((3, out_pair), (6, hi_pair)))

        def second_dve(dve, line):
            v_ = nc.vector
            n0 = FIRST["P2"]
            for b in range(len(SECOND)):
                split_lo(dve, line, n0 + b + 1)
            dve.wait_ge(gl_z, 1)
            dve.wait_ge(phase_const, 2)
            line.settle()
            for t in range(2):
                gb = cols[:, 0, C_GB + t:C_GB + t + 1]
                line(v_.tensor_scalar(tmp[:, t, :], B[t][:, :], gb, -1.0, ALU.add, ALU.mult))
                line.settle()
                line(v_.tensor_scalar(tmp[:, 2 + t, :], tmp[:, t, :], 40.0, None, ALU.min), gl_u)
            for t in range(2):
                line.settle()
                line(v_.tensor_scalar(work[:, t, :], tmp[:, t, :], -40.0, 0.0, ALU.add, ALU.max))
                line.settle()
                dve.wait_ge(gl_l, t + 1)
                line(v_.tensor_tensor(work[:, t, :], work[:, t, :], tmp[:, 2 + t, :], ALU.add))
                line.settle()
                line(v_.tensor_tensor_scan(tmp[:, t, :], reset2[:, :], work[:, t, :], 0.0, ALU.mult, ALU.add))
                line.settle()
                line(v_.tensor_scalar(gend[:, t, :], tmp[:, t, 63:T:64], -1.0 / 16, None, ALU.mult), gl_b)
            for t in range(2):
                dve.wait_ge(gl_e, t + 1)
                line(v_.scalar_tensor_tensor(out=z["gq"][:, t, :], in0=z["gq"][:, t, :], scalar=GK ** -0.5,
                                             in1=gE[:, 0, :], op0=ALU.mult, op1=ALU.mult))
                line(v_.tensor_tensor(work[:, t, :], z["gk"][:, t, :], gE[:, 2, :], ALU.mult))
                line.settle()
                line(v_.tensor_tensor(z["gk"][:, t, :], z["gk"][:, t, :], gE[:, 1, :], ALU.mult), gl_q)
                dve.wait_ge(gl_U, t + 1)
                if t:
                    dve.wait_ge(pv_done, PV2 + 2)
                line(v_.tensor_copy(gst[:, 1, :], B[5][:, 0:GV]))
                for ch in range(1, 7):
                    line.settle()
                    line(v_.scalar_tensor_tensor(out=gst[:, ch + 1, :], in0=gst[:, ch, :],
                                                 scalar=gE[:, 0, 64 * ch + 63:64 * ch + 64],
                                                 in1=B[5 + 2 * (ch % 2)][:, (ch // 2) * GV:(ch // 2 + 1) * GV],
                                                 op0=ALU.mult, op1=ALU.add), gl_s if ch == 6 else None)
                for r in range(2):
                    h = 2 * t + r
                    m = M2 + h
                    dve.wait_ge(o_rs, m + 1)
                    dve.wait_ge(y_ready, m)
                    gain = cols[0:GV, 0, C_GN:C_GN + 1]
                    line(v_.scalar_tensor_tensor(out=sumsq[0:GV, :], in0=o2[0:GV, 0, :], scalar=gain,
                                                 in1=rstd[0:GV, :], op0=ALU.mult, op1=ALU.mult))
                    line.settle()
                    line(v_.tensor_tensor(tmp[0:GV, 0, :], sumsq[0:GV, :], z["ggate"][0:GV, h, :], ALU.mult), y_t)
                    y_dve(dve, line, m, h, GV)
            for t in range(2):
                u = z["pu"][:, t, :]
                at, src, size = 0, u, 1
                sums = []
                line.settle()
                for _ in range(2 if t == 0 else 4):
                    dst = gE[:, at % 3, :] if at < 3 else o2[:, 1, :]
                    line(v_.tensor_copy(dst[:, 0:size], src[:, 0:size]))
                    line(v_.tensor_tensor(dst[:, size:T], src[:, size:T], src[:, 0:T - size], ALU.add))
                    line.settle()
                    src, size, at = dst, 2 * size, at + 1
                    sums.append((dst, size))
                for r in range(2):
                    s_w, w = sums[-2 + r]
                    p = slice(64 * r, 64 * r + 64)
                    line(v_.scalar_tensor_tensor(out=work[p, 4 + t, 16:T], in0=s_w[p, 16:T], scalar=1.0 / w,
                                                 in1=u[p, 16:T], op0=ALU.mult, op1=ALU.subtract))
                    line(v_.tensor_tensor(work[p, 4 + t, 0:16], s_w[p, 0:16], poolc[p, t, :], ALU.mult))
                    line.settle()
                    line(v_.tensor_tensor(work[p, 4 + t, 0:16], work[p, 4 + t, 0:16], u[p, 0:16], ALU.subtract),
                         pl_d if r else None)
            for t in range(2):
                m = M2 + GH + t
                dve.wait_ge(pl_y, t + 1)
                dve.wait_ge(y_ready, m)
                line(v_.scalar_tensor_tensor(out=tmp[:, 0, :], in0=B[2][:, :] if t else B[5][:, :],
                                             scalar=cols[:, 0, C_PS + t:C_PS + t + 1], in1=z["pgate"][:, t, :],
                                             op0=ALU.mult, op1=ALU.mult), y_t)
                y_dve(dve, line, m, 7 + t)
            line(v_.memset(chosen[:, 0, 0:P], 0.0))
            for i in range(1, TT):
                w = (i + 1) * P
                score = work[:, 4, 0:w]
                for h in range(IH):
                    dve.wait_ge(ix_r, IH * (i - 1) + h + 1)
                    wc = z["wi"][:, i, h:h + 1]
                    line.settle()
                    if h == 0:
                        line(v_.tensor_scalar(score, work[:, 0, 0:w], wc, None, ALU.mult), ix_a)
                    else:
                        line(v_.scalar_tensor_tensor(out=score, in0=work[:, h, 0:w], scalar=wc, in1=score,
                                                     op0=ALU.mult, op1=ALU.add), ix_a)
                dve.wait_ge(ix_c, i)
                src = score
                for r in range(TOPK // 8):
                    line.settle()
                    line(v_.max(eight[:, :], src))
                    if r < TOPK // 8 - 1:
                        line.settle()
                        line(v_.match_replace(work[:, 5, 0:w], eight[:, :], src, -3.3e38))
                        src = work[:, 5, 0:w]
                line.settle()
                line(v_.tensor_scalar(tmp[:, 0, 0:w], score, eight[:, 7:8], None, ALU.is_gt))
                line(v_.tensor_scalar(tmp[:, 1, 0:w], score, eight[:, 7:8], None, ALU.is_equal))
                line.settle()
                line(v_.tensor_reduce(small[:, 57:58], tmp[:, 0, 0:w], AX_X, ALU.add))
                line(v_.tensor_tensor_scan(tmp[:, 2, 0:w], tmp[:, 1, 0:w], zero2[:, 0:w], 0.0, ALU.add, ALU.add))
                line.settle()
                line(v_.tensor_scalar(small[:, 58:59], small[:, 57:58], -1.0, float(TOPK), ALU.mult, ALU.add))
                line.settle()
                line(v_.scalar_tensor_tensor(out=tmp[:, 3, 0:w], in0=tmp[:, 2, 0:w], scalar=small[:, 58:59],
                                             in1=tmp[:, 1, 0:w], op0=ALU.is_le, op1=ALU.mult))
                line.settle()
                line(v_.tensor_tensor(tmp[:, 3, 0:w], tmp[:, 3, 0:w], tmp[:, 0, 0:w], ALU.add))
                line.settle()
                line(v_.tensor_scalar(chosen[:, i, 0:w], tmp[:, 3, 0:w], 1.0, -NEG, ALU.subtract, ALU.mult))
            dve.wait_ge(toep_in, 48)
            line.settle()

            def gate_pair(h):
                if h % 2 == 0:
                    return
                m = M2 + GH + 2 + h // 2
                dve.wait_ge(o_sq, O2 + h // 2 + 1)
                dve.wait_ge(y_ready, m)
                line(v_.tensor_tensor(tmp[:, 0, :], o2[:, (h // 2) % 2, :], z["dgate"][:, h // 2, :], ALU.mult), y_t)

            def lo_pair(h):
                if h % 2:
                    y_dve(dve, line, M2 + GH + 2 + h // 2, 4 + h // 2)
            rows_dve(dve, line, U2, DH, 1, ((5, gate_pair), (7, lo_pair)))

        @block.sync
        def _(sp):
            sp.dma_start(x_rows[:, :, :], x[0].rearrange("(t p) d -> p t d", p=P)).then_inc(setup2, 16)

            def slot(n, k):
                return raw[:, n % 4, 0:k * P].rearrange("p (k n) -> p k n", n=P)

            def load(n, src, i=None, k=KD):
                if n >= 4 or i is not None:
                    sp.wait_ge(lo_ready, plus(i, 4, n - 3))
                sp.dma_start(slot(n, k), src).then_inc(landed[n % 4], 16)

            def load_ada(q, kk, l, col, i=None, first=False):
                if not first:
                    sp.wait_ge(ada_used, plus(i, 8, 8 * q + kk - 3))
                sp.dma_start(ada[:, kk % 4, :], ada_v[l, kk, :, col]).then_inc(ada_landed[kk % 4], 16)

            for q in range(3):
                for kk in range(8):
                    load_ada(q, kk, 0, slice(q * D, (q + 1) * D), None, q == 0 and kk < 4)

            def feed_forward(name, l, s, q0, parts):
                n0 = FIRST[name]

                def up(n, i, m, with_ada):
                    for b in range(4):
                        col = bass.ds(plus(i, 2 * P, m * 2 * P + (b // 2) * P + (b % 2) * FF), P)
                        load(n + b, up_v[l, s, :, :, col], i)
                        if with_ada:
                            for kk in (2 * b, 2 * b + 1):
                                load_ada(q0 + m, kk, (q0 // 9), bass.ds(plus(i, D, (q0 % 9 + m) * D), D), i)

                k = 0
                if n0 == 0:
                    up(0, None, 0, True)
                    k = 1
                if parts > k:
                    with sp.Fori(0, parts - k) as i:
                        up(n0 + 4 * k, i, k, True)
                    k = parts
                with sp.Fori(0, KF // 2 - k) as i:
                    up(n0 + 4 * k, i, k, False)
                with sp.Fori(0, KD // 2) as i:
                    for b in range(4):
                        load(n0 + UP + b, down_v[l, s, b % 2, :, :, bass.ds(plus(i, 2 * P, (b // 2) * P), P)], i, KH)

            def plain(name, view, count, width=None):
                with sp.Fori(0, count // 4) as i:
                    for b in range(4):
                        load(FIRST[name] + b, view[:, :, bass.ds(plus(i, 4 * P, b * P), P)], i)

            feed_forward(*FFN[0])
            plain("QKV", qkv_v[0], 24)
            plain("WO", wo_v[0], KD)
            feed_forward(*FFN[1])
            feed_forward(*FFN[2])
            for b, (kind, j) in enumerate(HORDER):
                col = HCOL[kind] * D + j * P
                load(FIRST["HIN"] + b, hin_v[0][:, :, col:col + P])
            plain("HO", ho_v[0], KD)
            feed_forward(*FFN[3])
            extra = 0
            for b, (kind, t, pieces) in enumerate(SECOND):
                n = FIRST["P2"] + b
                sp.wait_ge(lo_ready, n - 3)
                for m, (col, width, at) in enumerate(pieces):
                    sp.dma_start(slot(n, KD)[:, :, at:at + width],
                                 in2_v[0][:, :, col:col + width]).then_inc(landed[n % 4], 16)
            for j in range(KD):
                n = FIRST["OUT"] + j
                sp.wait_ge(lo_ready, n - 3)
                sp.dma_start(slot(n, 9)[0:GV, 0:GH, :],
                             w_out_2[0, 0:GH * GV, j * P:(j + 1) * P].rearrange("(k p) n -> p k n", p=GV))\
                    .then_inc(landed[n % 4], 16)
                sp.dma_start(slot(n, 9)[:, GH:9, :],
                             w_out_2[0, GH * GV:, j * P:(j + 1) * P].rearrange("(k p) n -> p k n", p=P))\
                    .then_inc(landed[n % 4], 16)
            for t in range(TT):
                sp.wait_ge(fin_sb, 2 * (t + 1))
                sp.dma_start(out[0, t * P:(t + 1) * P, :], tmp_out(t)).then_inc(out_done[t % 2], 16)
            for i in range(2):
                sp.wait_ge(out_done[i], 16 * TT // 2)

        @block.gpsimd
        def _(pool):
            line = Line(pool, pool_own)
            g = nc.gpsimd
            line.settle()
            line(g.memset(rows[:, :, :], 0.0))
            line.settle()
            line(g.memset(table[:, :], NEG))
            line.settle()
            line(g.memset(ident[:, :], 0.0))
            line.settle()
            line(g.memset(ones[:, :], 1.0))
            line.settle()
            line(g.memset(halves[:, :], 0.0))
            line.settle()
            line(g.memset(sumsq[:, :], 0.0))
            line.settle()
            line(g.memset(small[:, :], 0.0))
            line.settle()
            line(g.affine_select(out=ident[:, :], in_=ident[:, :], compare_op=ALU.not_equal, fill=1.0, base=0,
                                 pattern=[[-1, P]], channel_multiplier=1))
            line.settle()
            line(g.memset(halves[0:HD, 0:HD], 1.0))
            line.settle()
            line(g.memset(halves[HD:P, HD:P], 1.0))
            line.settle()
            line(g.memset(small[:, 0:1], EPS))
            line.settle()
            line(g.memset(small[:, 1:2], 1.0))
            line.settle()
            line(g.memset(small[:, 7:8], 0.0), const_ready)
            line.settle()
            r = rows[:, 0, :]

            def small_load(dst, src):
                pool.dma_start(dst, src).then_inc(setup, 16)

            small_load(r[0:48, :], norm_g.rearrange("l s (k p) -> (l s k) p", p=P))
            small_load(r[48:56, :], norm_g_2.rearrange("l (k p) -> (l k) p", p=P))
            small_load(r[56:64, :], final_norm_g_2.rearrange("(k p) -> k p", p=P))
            small_load(r[64:72, :], c.rearrange("b (k p) -> (b k) p", p=P))
            small_load(r[72:80, :], hgrn_out_gain.rearrange("b (k p) -> (b k) p", p=P))
            small_load(r[80:88, :], hgrn_lb_logits.rearrange("b (k p) -> (b k) p", p=P))
            small_load(r[88:89, :], attn_subln_gain)
            small_load(r[89:91, :], pool_scale_2.rearrange("b (k p) -> (b k) p", p=P))
            for m in range(2):
                small_load(r[91:92, HD * m:HD * m + HD], attn_q_gain)
                small_load(r[92:93, HD * m:HD * m + HD], attn_k_gain)
                for t in range(2):
                    small_load(r[93 + t:94 + t, 64 * m:64 * m + GK],
                               gla_gate_b_2[:, 2 * GK * t + GK * m:2 * GK * t + GK * m + GK])
            small_load(r[95:96, 0:GV], gla_norm_g_2)
            ada_b_rows = ada_b.rearrange("l (k p) -> (l k) p", p=P)
            small_load(r[96:112, :], ada_b_rows[128:144, :])
            small_load(rows[:, 1, :], ada_b_rows[0:128, :])
            small_load(table[:, 0:640], bucket_rows)
            small_load(table[0:32, 640:648], rel_bias)
            small_load(table[0:32, 648:654], rel_bias_2)
            small_load(lamb[:, :, :], attn_lambda[0].rearrange("(a r) d -> a r d", a=1).broadcast_to((P, 4, HD)))
            hgrn_pool(pool, line)
            pool.wait_ge(used, FIRST["P2"])
            second_pool(pool, line)

        @block.scalar
        def _(act):
            line = Line(act, act_own)
            s = nc.scalar
            act.wait_ge(const_ready, 1)
            act.wait_ge(cols_ready, 1)
            line(s.activation(cact[:, :], cols[:, 0, C_C:C_C + 8], ACT.Silu), cact_ready)
            act.wait_ge(cols_ready, 2)
            nc.scalar.preload_act_table_set("natural_log_exp_and_others")
            line(s.activation(small[:, 44:46], small[:, 42:44], ACT.Exp), cact_ready)
            line(s.activation(small[:, 48:56], small[:, 8:16], ACT.Exp), cact_ready)
            act.wait_ge(bias_sb, 4)
            for m, heads in ((0, HEADS), (1, DH)):
                act.dma_start(bias_dram.ap()[m, 0:heads, :, :],
                              bias_row[0:heads, m:m + 1, :].broadcast_to((heads, P, 640))).then_inc(bias_out, 16)
            for j in range(KD):
                act.wait_ge(x_ready, j + 1)
                line(s.activation(sq[:, :], xT[:, j, :], ACT.Square), sq_ready)
            norm_act(act, line, 0, ACT.Silu)
            split_hi(act, line, 0)
            act.wait_ge(bias_out, 32)
            ffn_act(act, line, "F0", 0, 6)
            norm_act(act, line, 1, None)
            bias_tiles(act, toep1[:, :, :], 0, HEADS)
            qkv_act(act, line)

            rows_act(act, line, 0, 0, HEADS, 2,
                     ((3, lambda h: head_out_act(act, line, h, o1[:, h % 2, :], TT * (h + 1))),
                      (4, lambda h: head_rs_act(act, line, h)), (6, lambda h: head_hi_act(act, line, h, h))))
            back_act(act, line, "WO")
            norm_act(act, line, 2, ACT.Silu)
            ffn_act(act, line, "F1", 1, 9)
            norm_act(act, line, 3, ACT.Silu)
            ffn_act(act, line, "F2", 2, 0)
            norm_act(act, line, 4, None)
            act.dma_start(masks[:, :, :], level_masks.rearrange("p (l t) -> p l t", t=P)).then_inc(toep_in, 16)
            hin_act(act, line)
            hgrn_act(act, line)
            back_act(act, line, "HO")
            norm_act(act, line, 5, ACT.Silu)
            ffn_act(act, line, "F3", 3, 0)
            norm_act(act, line, 6, None)
            second_act(act, line)
            back_act(act, line, "OUT")
            norm_act(act, line, 7, None)
            for t in range(TT):
                act.wait_ge(fin_ps, t + 1)
                if t >= 2:
                    act.wait_ge(out_done[t % 2], 16 * (t // 2))
                for hf in range(2):
                    line(s.activation(tmp[:, 2 * (t % 2) + hf, :], B[2 * (t % 2) + hf][:, :], ACT.Copy), fin_sb)

        @block.vector
        def _(dve):
            line = Line(dve, dve_own)
            v = nc.vector
            dve.wait_ge(turned, 1)
            line(v.tensor_copy(cols[:, :, :], B[7][:, 0:2 * P].rearrange("p (a n) -> p a n", n=P)), cols_ready)
            line.settle()
            for m in range(2):
                line(v.tensor_tensor(lnt[:, m * HD:(m + 1) * HD], lamb[:, 2 * m, :], lamb[:, 2 * m + 1, :], ALU.mult))
            line.settle()
            line(v.tensor_reduce(small[:, 42:44], lnt[:, 0:2 * HD].rearrange("p (a n) -> p a n", n=HD), AX_X, ALU.add))
            line(v.tensor_tensor(lb_c, cols[:, 0, C_LB:C_LB + 8], cols[:, 0, C_LB:C_LB + 8], ALU.subtract))
            line(v.tensor_scalar(qg_c, cols[:, 0, C_QG:C_QG + 1], HD ** -0.5, None, ALU.mult))
            line(v.tensor_scalar(subg_c, cols[:, 0, C_SUB:C_SUB + 1], 1.0 - LAMBDA_INIT, None, ALU.mult))
            for col in (41, 46):
                line(v.memset(small[:, col:col + 1], 0.0), g_ready)
            line.settle()
            line(v.memset(small[:, 47:48], 0.0), cols_ready)
            for m, heads in ((0, HEADS), (1, DH)):
                dve.wait_ge(bias_ps, 2 * m + 1)
                line(v.tensor_copy(bias_row[0:heads, m, 0:T], B[0 + m][0:heads, :]), bias_sb)
                dve.wait_ge(bias_ps, 2 * m + 2)
                line(v.tensor_copy(bias_row[0:heads, m, T:640], B[2 + m][0:heads, 0:P]), bias_sb)
            dve.wait_ge(cact_ready, 3)
            line(v.tensor_tensor(small[:, 56:57], small[:, 45:46], small[:, 44:45], ALU.subtract))
            line(v.reciprocal(small[:, 16:24], small[:, 48:56]))
            line.settle()
            line(v.tensor_scalar(nlam_c, small[:, 56:57], LAMBDA_INIT, None, ALU.subtract))
            line(v.tensor_tensor(small[:, 48:56], small[:, 48:56], small[:, 16:24], ALU.mult))
            line.settle()
            line(v.tensor_tensor(lb_c, small[:, 48:56], small[:, 48:56], ALU.subtract))
            line.settle()
            line(v.tensor_scalar(lb1_c, lb_c, -1.0, 1.0, ALU.mult, ALU.add))
            for j in range(KD):
                dve.wait_ge(x_turned, j + 1)
                line(v.tensor_copy(xT[:, j, :], B[j % 4][:, :]), x_ready)
                dve.wait_ge(sq_ready, j + 1)
                line(v.tensor_tensor(sumsq[:, :], sumsq[:, :], sq[:, :], ALU.add), sum_ready)
            for q in range(3):
                for kk in range(8):
                    ada_dve(dve, line, q, kk)
            ada_take(dve, line, 0, 3)
            norm_dve(dve, line, 0)
            split_lo(dve, line, 0)
            dve.wait_ge(bias_out, 32)
            ffn_dve(dve, line, "F0", 0, 3, 6)
            norm_dve(dve, line, 1)
            qkv_dve(dve, line)
            dve.wait_ge(toep_in, 16)

            rows_dve(dve, line, 0, HEADS, 2,
                     ((5, lambda h: head_out_dve(dve, line, h, o1[:, h % 2, :], subg_c)),
                      (7, lambda h: head_lo_dve(dve, line, h, h))))
            back_dve(dve, line, "WO")
            norm_dve(dve, line, 2)
            ffn_dve(dve, line, "F1", 1, 9, 9)
            norm_dve(dve, line, 3)
            ffn_dve(dve, line, "F2", 2, 0, 0)
            norm_dve(dve, line, 4)
            hin_dve(dve, line)
            hgrn_dve(dve, line)
            back_dve(dve, line, "HO")
            norm_dve(dve, line, 5)
            ffn_dve(dve, line, "F3", 3, 0, 0)
            norm_dve(dve, line, 6)
            second_dve(dve, line)
            back_dve(dve, line, "OUT")
            norm_dve(dve, line, 7)
            for j in range(KD):
                line(v.scalar_tensor_tensor(out=xT[:, j, :], in0=xT[:, j, :], scalar=scale_col[:, j:j + 1],
                                            in1=rstd[:, :], op0=ALU.mult, op1=ALU.mult), fin_t)

        @block.tensor
        def _(pe):
            t = nc.tensor
            pe.wait_ge(const_ready, 1)
            pe.wait_ge(setup, 16 * 23)
            t.transpose(B[7][:, 0:P], rows[:, 0, :], ident[:, :])
            t.transpose(B[7][:, P:2 * P], rows[:, 1, :], ident[:, :]).then_inc(turned, 1)
            for m, heads in ((0, HEADS), (1, DH)):
                rb = table[:, 640 + 8 * m:640 + 8 * m + heads]
                t.matmul(B[0 + m][0:heads, :], rb, table[:, 0:T], start=True, stop=True).then_inc(bias_ps, 1)
                t.matmul(B[2 + m][0:heads, 0:P], rb, table[:, T:640], start=True, stop=True).then_inc(bias_ps, 1)
            pe.wait_ge(bias_sb, 4)
            pe.wait_ge(setup2, 16)
            for j in range(KD):
                if j >= 4:
                    pe.wait_ge(x_ready, j - 3)
                for tt in range(TT):
                    last = t.transpose(B[j % 4][:, tt * P:(tt + 1) * P], x_rows[:, tt, j * P:(j + 1) * P], ident[:, :])
                last.then_inc(x_turned, 1)
            for q in range(3):
                ada_pe(pe, q)
            norm_pe(pe, 0)
            ffn_pe(pe, "F0", 0, 3, 6)
            norm_pe(pe, 1)
            qkv_pe(pe)
            pe.wait_ge(headn, 16)
            pe.wait_ge(epi_free, 8)
            rows_pe(pe, 0, HEADS, 2,
                    lambda h, cc: aq[HD * cc:HD * cc + HD, h, :], lambda h, cc: ak[HD * cc:HD * cc + HD, h, :],
                    lambda h, k: av[:, k, h * P:(h + 1) * P], lambda h: slice(0, P))
            back_pe(pe, "WO", HEADS, KD)
            norm_pe(pe, 2)
            ffn_pe(pe, "F1", 1, 9, 9)
            norm_pe(pe, 3)
            ffn_pe(pe, "F2", 2, 0, 0)
            norm_pe(pe, 4)
            hin_pe(pe)
            hgrn_pe(pe)
            back_pe(pe, "HO", 2 * HEADS, KD)
            norm_pe(pe, 5)
            ffn_pe(pe, "F3", 3, 0, 0)
            norm_pe(pe, 6)
            second_pe(pe)
            back_pe(pe, "OUT", 2 * HEADS + 9, 9, [GV] * GH + [P] * 5)
            norm_pe(pe, 7)
            pe.wait_ge(fin_t, KD)
            for tt in range(TT):
                if tt >= 2:
                    pe.wait_ge(fin_sb, 2 * (tt - 1))
                for j in range(KD):
                    last = t.transpose(B[2 * (tt % 2) + j // 4][:, (j % 4) * P:(j % 4 + 1) * P],
                                       xT[:, j, tt * P:(tt + 1) * P], ident[:, :])
                last.then_inc(fin_ps, 1)


def bucket_table():
    import math
    import numpy as np
    dist = 511 - np.arange(640)
    d = np.maximum(dist, 0)
    large = 16 + (np.log(np.maximum(d, 1).astype(np.float32) / 16) / math.log(128 / 16) * 16).astype(np.int32)
    bucket = np.where(d < 16, d, np.minimum(large, 31))
    bucket = np.where(dist < 0, 32, bucket)
    return (np.arange(33)[:, None] == bucket[None, :]).astype(np.float32)


def halving_masks():
    import numpy as np
    s, t = np.arange(128)[:, None], np.arange(128)[None, :]
    m = np.zeros((128, 8, 128), np.float32)
    for v in range(7):
        half = 1 << v
        m[:, v, :] = (s // (2 * half) == t // (2 * half)) & (s % (2 * half) < half) & (t % (2 * half) >= half)
    m[:, 7, :] = s == t
    return m.reshape(128, 1024)


def window_counts():
    import numpy as np
    w = np.array([[2, 4], [8, 16]], np.float32)
    out = np.zeros((128, 2, 16), np.float32)
    for t in range(2):
        for g in range(2):
            out[64 * g:64 * g + 64, t, :] = 1.0 / np.minimum(np.arange(16) + 1, w[t, g])
    return out


_INS = ['x', 'c', 'ada_w', 'ada_b', 'norm_g', 'ffn_w_in', 'ffn_w_down', 'attn_w_qkv', 'attn_w_o', 'attn_q_gain',
        'attn_k_gain', 'attn_lambda', 'attn_subln_gain', 'rel_bias', 'hgrn_w_in', 'hgrn_w_o', 'hgrn_out_gain',
        'hgrn_lb_logits', 'norm_g_2', 'w_in_2', 'gla_gate_w2_2', 'gla_gate_b_2', 'gla_norm_g_2', 'rel_bias_2',
        'pool_w_2', 'pool_scale_2', 'w_out_2', 'final_norm_g_2']


def kernel(**inputs):
    import numpy as _np
    import concourse.bacc as _bacc
    from concourse import mybir as _mybir
    from concourse.bass_utils import run_bass_kernel_spmd as _run

    nc = _bacc.Bacc("TRN2", target_bir_lowering=False, num_devices=1, dynamic_dma_scratch_size=2048)
    arrays, args = {}, []
    feeds = [(name, _np.ascontiguousarray(inputs[name])) for name in _INS]
    feeds += [("bucket_rows", bucket_table()), ("level_masks", halving_masks()), ("pool_counts", window_counts())]
    for name, a in feeds:
        arrays[f"in_{name}"] = a
        args.append(nc.dram_tensor(f"in_{name}", a.shape, _mybir.dt.from_np(a.dtype), kind="ExternalInput").ap())
    args.append(nc.dram_tensor("out_0", (1, T, D), F32, kind="ExternalOutput").ap())
    program(nc, *args)
    r = _run(nc, [arrays], core_ids=[0])
    return r.results[0]["out_0"]
```

```python
from contextlib import ExitStack

import concourse.bass as bass
from concourse import mybir

P = 128
T = 512
D = 1024
KD = D // P
TT = T // P
FF = 2816
KF = FF // P
KH = KF // 2
SLOT = KH * P
EPS = 1e-6
HEADS = 8
HD = 64
LEVELS = 7
GH, GK, GV = 4, 48, 96
DH = 6
IH = 4
TOPK = 128
LAMBDA_INIT = 0.2
NEG = -1.0e30
LOW = -3.0e38

ALU = mybir.AluOpType
ACT = mybir.ActivationFunctionType
F32 = mybir.dt.float32
F32R = mybir.dt.float32r
AX_X = mybir.AxisListType.X

SIZES = (("gq", 192), ("gk", 192), ("gv", 384), ("gz", 16), ("ggate", 384), ("dq", 384), ("dk", 384),
         ("dv", 384), ("dgate", 384), ("qi", 128), ("ki", 32), ("wi", 4), ("pu", 256), ("pgate", 256))
COL, _at = {}, 0
for _n, _s in SIZES:
    COL[_n] = _at
    _at += _s


def second_blocks():
    out = [("qi", 0, [(COL["qi"], P, 0)]),
           ("ki", 0, [(COL["ki"], 32, 32 * r) for r in range(IH)]),
           ("wi", 0, [(COL["wi"], P, 0)]),
           ("gz", 0, [(COL["gz"], P, 0)])]
    for kind in ("gq", "gk"):
        for t in range(2):
            out.append((kind, t, [(COL[kind] + 2 * GK * t + GK * r, 64, 64 * r) for r in range(2)]))
    for kind, n in (("gv", 3), ("dq", 3), ("dk", 3), ("dv", 3), ("pu", 2)):
        for t in range(n):
            out.append((kind, t, [(COL[kind] + P * t, P, 0)]))
    for t in range(GH):
        out.append(("ggate", t, [(COL["ggate"] + GV * t, P, 0)]))
    for kind, n in (("dgate", 3), ("pgate", 2)):
        for t in range(n):
            out.append((kind, t, [(COL[kind] + P * t, P, 0)]))
    return out


SECOND = second_blocks()
NATURAL = ("gv", "dv")

UP, DOWN = 2 * KF, 2 * KD
FIRST = {}
_at = 0
for _name, _n in (("F0", UP + DOWN), ("QKV", 24), ("WO", KD), ("F1", UP + DOWN), ("F2", UP + DOWN), ("HIN", 32),
                  ("HO", KD), ("F3", UP + DOWN), ("P2", len(SECOND)), ("OUT", KD)):
    FIRST[_name] = _at
    _at += _n
BLOCKS = _at


def tiles_of(n):
    for f in ("F0", "F1", "F2", "F3"):
        if FIRST[f] + UP <= n < FIRST[f] + UP + DOWN:
            return KH
    return 9 if n >= FIRST["OUT"] else KD


class Line:

    def __init__(self, eng, own):
        self.eng, self.own, self.count, self.last, self.i, self.per = eng, own, {}, None, None, {}

    def __call__(self, ins, sem=None):
        sem = sem or self.own
        ins.then_inc(sem, 1)
        self.count[sem.name] = self.count.get(sem.name, 0) + 1
        self.last = sem
        return ins

    def value(self, sem):
        n = self.count.get(sem.name, 0)
        per = self.per.get(sem.name, 0)
        return self.i * per + n if self.i is not None and per else n

    def settle(self):
        if self.last is not None:
            self.eng.wait_ge(self.last, self.value(self.last))

    def loop(self, first, end, body, per):
        if end <= first:
            return
        self.settle()
        per = {s.name: k for s, k in per}
        start = dict(self.count)
        with self.eng.Fori(0, end - first) as i:
            self.i, self.per = i, per
            body(i)
            self.i, self.per = None, {}
        for name in set(self.count) | set(per):
            had = self.count.get(name, 0) - start.get(name, 0)
            assert had == per.get(name, 0), (name, had, per.get(name, 0))
            self.count[name] = start.get(name, 0) + (end - first) * had


def program(nc, x, c, ada_w, ada_b, norm_g, ffn_w_in, ffn_w_down, attn_w_qkv, attn_w_o, attn_q_gain,
            attn_k_gain, attn_lambda, attn_subln_gain, rel_bias, hgrn_w_in, hgrn_w_o, hgrn_out_gain,
            hgrn_lb_logits, norm_g_2, w_in_2, gla_gate_w2_2, gla_gate_b_2, gla_norm_g_2, rel_bias_2,
            pool_w_2, pool_scale_2, w_out_2, final_norm_g_2, bucket_rows, level_masks, pool_counts, out):
    ctx = ExitStack()
    with ctx:
        def sb(name, shape, dt=F32, where=ctx):
            return where.enter_context(nc.sbuf_tensor(name, shape, dt))

        def sem(name):
            return ctx.enter_context(nc.semaphore(name))

        xT = sb("xT", [P, KD, T])
        h_hi = sb("h_hi", [P, KD, T], F32R)
        h_lo = sb("h_lo", [P, KD, T], F32R)
        raw = sb("raw", [P, 4, SLOT])
        w_hi = sb("w_hi", [P, 2, SLOT], F32R)
        w_lo = sb("w_lo", [P, 2, SLOT], F32R)
        ada = sb("ada", [P, 4, D])
        ada_sum = sb("ada_sum", [P, D])
        ident = sb("ident", [P, P])
        ones = sb("ones", [P, P])
        halves = sb("halves", [P, P])
        rows = sb("rows", [P, 2, P])
        cols = sb("cols", [P, 2, P])
        mod = sb("mod", [P, 18 * KD])
        cact = sb("cact", [P, KD])
        scale_col = sb("scale_col", [P, KD])
        gate_col = sb("gate_col", [P, KD])
        small = sb("small", [P, 64])
        sumsq = sb("sumsq", [P, T])
        sq = sb("sq", [P, T])
        rstd = sb("rstd", [P, T])
        lnt = sb("lnt", [P, T])
        tmp = sb("tmp", [P, 4, T])
        eight = sb("eight", [P, 8])
        gend = sb("gend", [P, 2, 8])

        ph = ExitStack()
        g_hi = sb("g_hi", [P, KF, T], F32R, ph)
        g_lo = sb("g_lo", [P, KF, T], F32R, ph)
        ph.close()
        ph = ExitStack()
        x_rows = sb("x_rows", [P, TT, D], F32, ph)
        bias_row = sb("bias_row", [8, 2, 640], F32, ph)
        lamb = sb("lamb", [P, 4, HD], F32, ph)
        table = sb("table", [33, 640 + 16], F32, ph)
        ph.close()
        ph = ExitStack()
        aq = sb("aq", [P, 2, T], F32, ph)
        ak = sb("ak", [P, 2, T], F32, ph)
        av = sb("av", [P, 2, T], F32, ph)
        avT = sb("avT", [P, T], F32, ph)
        toep1 = sb("toep1", [P, HEADS, T], F32, ph)
        s1 = sb("s1", [P, 3, 2, T], F32, ph)
        at1 = sb("at1", [P, 2, T], F32, ph)
        o1 = sb("o1", [P, 2, T], F32, ph)
        y1_hi = sb("y1_hi", [P, KD, T], F32R, ph)
        y1_lo = sb("y1_lo", [P, KD, T], F32R, ph)
        osq1 = sb("osq1", [P, T], F32, ph)
        ors1 = sb("ors1", [P, T], F32, ph)
        ph.close()
        ph = ExitStack()
        hq = sb("hq", [P, HEADS, T], F32, ph)
        hk = sb("hk", [P, HEADS, T], F32, ph)
        hG = sb("hG", [P, HEADS, T], F32, ph)
        hg = sb("hg", [P, HEADS, T], F32, ph)
        hv = sb("hv", [P, TT, D], F32, ph)
        masks = sb("masks", [P, 8, P], F32, ph)
        hE, hqE, hkE, hP = (ada[:, i, :].rearrange("p (a n) -> p a n", n=T) for i in range(4))
        heG, hqG = tmp[:, 2, :], tmp[:, 3, :]
        hkd = sb("hkd", [P, T], F32, ph)
        hkn = sb("hkn", [P, T], F32, ph)
        hst = (rows[:, 0, :], rows[:, 1, :], hkn[:, 3 * P:4 * P])
        ho = ada_sum[:, 0:T]
        zero = ada_sum[:, T:2 * T]
        reset = ada_sum[:, 0:T]
        ph.close()
        ph = ExitStack()
        z = {}
        for kind, shape in (("qi", [P, T]), ("ki", [P, T]), ("gz", [P, T]), ("gv", [P, TT, 384]), ("dq", [P, 3, T]), ("dk", [P, 3, T]), ("dv", [P, TT, 384]),
                            ("pu", [P, 2, T]), ("ggate", [P, GH, T]), ("dgate", [P, 3, T]), ("pgate", [P, 2, T]),
                            ("wi", [P, TT, IH])):
            z[kind] = sb("z_" + kind, shape, F32, ph)
        toep2 = sb("toep2", [P, DH, T], F32, ph)
        z["gq"], z["gk"] = toep2[:, 0:2, :], toep2[:, 2:4, :]
        gst = toep2[:, 4:6, :].rearrange("p a n -> p (a n)")[:, 0:8 * GV].rearrange("p (c v) -> p c v", v=GV)
        chosen = sb("chosen", [P, TT, T], F32, ph)
        s2 = sb("s2", [P, 3, 1, T], F32, ph)
        spare = ada[:, :, :].rearrange("p a (b n) -> p (a b) n", n=T)
        work, at2 = spare[:, 0:6, :], spare[:, 6:8, :]
        o2 = ada_sum[:, :].rearrange("p (a n) -> p a n", n=T)
        gE = s2[:, :, 0, :]
        poolw = sb("poolw", [P, 2, P], F32, ph)
        poolc = sb("poolc", [P, 2, 16], F32, ph)
        w2 = sb("w2", [16, 2, P], F32, ph)
        zero2 = sb("zero2", [P, T], F32, ph)
        reset2 = chosen[:, TT - 1, :]
        y8_hi = sb("y8_hi", [P, T], F32R, ph)
        y8_lo = sb("y8_lo", [P, T], F32R, ph)
        ph.close()

        B = [ctx.enter_context(nc.psum_tensor(f"bank{i}", [P, T], F32)) for i in range(8)]
        bias_dram = nc.dram_tensor("bias_scratch", (2, 8, P, 640), F32)

        landed = [sem(f"landed{i}") for i in range(4)]
        ada_landed = [sem(f"ada_landed{i}") for i in range(4)]
        ada_landed_sw = [sem(f"ada_landed_sw{i}") for i in range(4)]
        hi_ready = sem("hi_ready")
        lo_ready = sem("lo_ready")
        used = sem("used")
        ada_used = sem("ada_used")
        ada_done = sem("ada_done")
        setup = sem("setup")
        setup2 = sem("setup2")
        const_ready = sem("const_ready")
        turned = sem("turned")
        cols_ready = sem("cols_ready")
        x_turned = sem("x_turned")
        x_ready = sem("x_ready")
        sq_ready = sem("sq_ready")
        sum_ready = sem("sum_ready")
        rms_ps = sem("rms_ps")
        rstd_ready = sem("rstd_ready")
        t_ready = sem("t_ready")
        hhi_ready = sem("hhi_ready")
        h_ready = sem("h_ready")
        silu_ready = sem("silu_ready")
        g_ready = sem("g_ready")
        gt_ready = sem("gt_ready")
        ghi_ready = sem("ghi_ready")
        cact_ready = sem("cact_ready")
        act_own = sem("act_own")
        dve_own = sem("dve_own")
        pool_own = sem("pool_own")
        bias_ps = sem("bias_ps")
        bias_sb = sem("bias_sb")
        bias_out = sem("bias_out")
        toep_in = sem("toep_in")
        vt_ps = sem("vt_ps")
        vt_out = sem("vt_out")
        epi_free = sem("epi_free")
        headsq = sem("headsq")
        headss = sem("headss")
        headrs = sem("headrs")
        headn = sem("headn")
        S_ps = sem("S_ps")
        S_max = sem("S_max")
        p_ready = sem("p_ready")
        a_ready = sem("a_ready")
        aT_ps = sem("aT_ps")
        aT_sb = sem("aT_sb")
        pv_done = sem("pv_done")
        o_sq = sem("o_sq")
        o_ss = sem("o_ss")
        o_rs = sem("o_rs")
        y_t = sem("y_t")
        y_hi = sem("y_hi")
        y_ready = sem("y_ready")
        f_min = sem("f_min")
        f_log = sem("f_log")
        f_arg = sem("f_arg")
        f_key = sem("f_key")
        f_done = sem("f_done")
        lv_D = sem("lv_D")
        lv_E = sem("lv_E")
        lv_q = sem("lv_q")
        lv_k = sem("lv_k")
        lv_S = sem("lv_S")
        lv_P = sem("lv_P")
        lv_O = sem("lv_O")
        st_E = sem("st_E")
        st_k = sem("st_k")
        st_T = sem("st_T")
        st_n = sem("st_n")
        st_U = sem("st_U")
        st_s = sem("st_s")
        ix_S = sem("ix_S")
        ix_r = sem("ix_r")
        ix_a = sem("ix_a")
        ix_c = sem("ix_c")
        ix_m = sem("ix_m")
        gl_z = sem("gl_z")
        gl_u = sem("gl_u")
        phase_const = sem("phase_const")
        small_in = sem("small_in")
        gl_l = sem("gl_l")
        gl_b = sem("gl_b")
        gl_e = sem("gl_e")
        gl_q = sem("gl_q")
        gl_A = sem("gl_A")
        gl_a = sem("gl_a")
        gl_m = sem("gl_m")
        gl_T = sem("gl_T")
        gl_n = sem("gl_n")
        gl_U = sem("gl_U")
        gl_s = sem("gl_s")
        gl_O = sem("gl_O")
        pl_d = sem("pl_d")
        pl_y = sem("pl_y")
        fin_t = sem("fin_t")
        fin_ps = sem("fin_ps")
        fin_sb = sem("fin_sb")
        out_done = [sem(f"out_done{i}") for i in range(2)]

        def norm_col(i, j):
            return cols[:, 0, 8 * i + j:8 * i + j + 1]
        C_C, C_HG, C_LB, C_SUB, C_PS, C_QG, C_KG, C_GB, C_GN, C_AB = 64, 72, 80, 88, 89, 91, 92, 93, 95, 96
        L_EPS, L_ONE, L_NLAM, L_ZERO = 0, 1, 2, 3
        eps_c, one_c, nlam_c = small[:, 0:1], small[:, 1:2], small[:, 2:3]
        lb_c, lb1_c = small[:, 8:16], small[:, 16:24]
        subg_c = small[:, 3:4]
        qg_c = small[:, 4:5]
        bank_of = [0, 0]

        ada_v = ada_w.rearrange("l (k p) n -> l k p n", p=P)
        up_v = ffn_w_in.rearrange("l s (k p) n -> l s p k n", p=P)
        down_v = ffn_w_down.rearrange("l s (u k p) n -> l s u p k n", p=P, k=KH)
        qkv_v = attn_w_qkv.rearrange("l (k p) n -> l p k n", p=P)
        wo_v = attn_w_o.rearrange("l (k p) n -> l p k n", p=P)
        hin_v = hgrn_w_in.rearrange("l (k p) n -> l p k n", p=P)
        ho_v = hgrn_w_o.rearrange("l (k p) n -> l p k n", p=P)
        in2_v = w_in_2.rearrange("l (k p) n -> l p k n", p=P)
        block = ctx.enter_context(nc.Block())

        def plus(i, per, base):
            return base if i is None else i * per + base

        HORDER = [("q", j) for j in range(8)] + [("v", j) for j in range(8)] + \
                 [("g", j) for j in range(8)] + [("f", j) for j in range(8)]
        HCOL = {"q": 0, "f": 1, "v": 2, "g": 3}

        FFN = (("F0", 0, 0, 3, 6), ("F1", 0, 1, 9, 9), ("F2", 1, 0, 0, 0), ("F3", 1, 1, 0, 0))

        def landings(n):
            total = 0
            for m in range(n % 4, n + 1, 4):
                if m >= FIRST["OUT"]:
                    total += 2
                elif m >= FIRST["P2"]:
                    total += len(SECOND[m - FIRST["P2"]][2])
                else:
                    total += 1
            return 16 * total

        def tmp_out(t):
            return tmp[:, 2 * (t % 2):2 * (t % 2) + 2, :]

        def load_ada(pool, q, kk, l, col, i=None):
            if q or kk >= 4:
                pool.wait_ge(ada_used, plus(i, 8, 8 * q + kk - 3))
            pool.dma_start(ada[:, kk % 4, :], ada_v[l, kk, :, col])\
                .then_inc((ada_landed if q < 3 else ada_landed_sw)[kk % 4], 16)

        def ada_loads(pool, q0, parts):
            with pool.Fori(0, parts) as i:
                for kk in range(8):
                    load_ada(pool, q0, kk, q0 // 9, bass.ds(plus(i, D, (q0 % 9) * D), D), i)

        def hgrn_pool(pool, line):
            g = nc.gpsimd
            pool.wait_ge(used, FIRST["HIN"])
            line.settle()
            line(g.memset(zero[:, :], 0.0))
            line.settle()
            line(g.memset(reset[:, :], 1.0))
            line.settle()
            line(g.memset(reset[:, 0:T:P], 0.0), phase_const)
            for h in range(HEADS):
                for v in range(LEVELS):
                    n = h * LEVELS + v
                    pool.wait_ge(lv_E, n + 1)
                    if n >= 2:
                        pool.wait_ge(lv_S, level_at(n - 2))
                    line.settle()
                    line(g.tensor_tensor(hkE[:, n % 2, :], hk[:, h, :], hE[:, n % 2, :], ALU.mult), lv_k)
                    if v == 2:
                        pool.wait_ge(st_E, h + 1)
                        if h:
                            pool.wait_ge(st_T, h)
                            pool.wait_ge(pv_done, pv_h(h))
                        line.settle()
                        line(g.tensor_tensor(hqG[:, :], hq[:, h, :], heG[:, :], ALU.mult), st_k)
                        line.settle()
                        line(g.tensor_tensor(hkd[:, :], hk[:, h, :], hkd[:, :], ALU.mult), st_k)

        def level_at(n):
            return n // LEVELS * (LEVELS + 1) + n % LEVELS + 1

        def pv_h(h):
            return HEADS * TT + h

        def bias_tiles(act, dst, m, heads):
            src = bass.AP(tensor=bias_dram, offset=m * 8 * P * 640 + P - 1, ap=[[639, P], [P * 640, heads], [1, T]])
            act.dma_start(dst, src).then_inc(toep_in, 16)

        def split_hi(act, line, n, i=None):
            if n >= BLOCKS:
                return
            k = tiles_of(n)
            base = landings(n)
            act.wait_ge(landed[n % 4], plus(i, 16, base))
            if n >= 2:
                act.wait_ge(used, plus(i, 4, n - 1))
            if k == 9:
                line(nc.scalar.activation(w_hi[0:GV, n % 2, 0:GH * P], raw[0:GV, n % 4, 0:GH * P], ACT.Copy))
                line(nc.scalar.activation(w_hi[:, n % 2, GH * P:9 * P], raw[:, n % 4, GH * P:9 * P], ACT.Copy), hi_ready)
            else:
                line(nc.scalar.activation(w_hi[:, n % 2, 0:k * P], raw[:, n % 4, 0:k * P], ACT.Copy), hi_ready)

        def split_lo(dve, line, n, i=None):
            if n >= BLOCKS:
                return
            k = tiles_of(n)
            dve.wait_ge(hi_ready, plus(i, 4, n + 1))
            if k == 9:
                line(nc.vector.tensor_tensor(w_lo[0:GV, n % 2, 0:GH * P], raw[0:GV, n % 4, 0:GH * P],
                                             w_hi[0:GV, n % 2, 0:GH * P].bitcast(F32), ALU.subtract))
                line(nc.vector.tensor_tensor(w_lo[:, n % 2, GH * P:9 * P], raw[:, n % 4, GH * P:9 * P],
                                             w_hi[:, n % 2, GH * P:9 * P].bitcast(F32), ALU.subtract), lo_ready)
            else:
                line(nc.vector.tensor_tensor(w_lo[:, n % 2, 0:k * P], raw[:, n % 4, 0:k * P],
                                             w_hi[:, n % 2, 0:k * P].bitcast(F32), ALU.subtract), lo_ready)

        def residual_dve(dve, line, n, j, i=None):
            jj = plus(i, 2, j)
            dve.wait_ge(used, plus(i, 4, n + 1))
            bank = B[j % 2]
            xj = xT[:, bass.ds(jj, 1), :].rearrange("p a n -> p (a n)") if i is not None else xT[:, j, :]
            gc = gate_col[:, bass.ds(jj, 1)] if i is not None else gate_col[:, j:j + 1]
            line(nc.vector.scalar_tensor_tensor(out=xj, in0=bank[:, :], scalar=gc, in1=xj,
                                                op0=ALU.mult, op1=ALU.add), x_ready)
            dve.wait_ge(sq_ready, line.value(x_ready))
            line(nc.vector.tensor_tensor(sumsq[:, :], sumsq[:, :], sq[:, :], ALU.add), sum_ready)

        def residual_act(act, line, count, j, i=None):
            jj = plus(i, 2, j)
            act.wait_ge(x_ready, plus(i, 2, count))
            xj = xT[:, bass.ds(jj, 1), :].rearrange("p a n -> p (a n)") if i is not None else xT[:, j, :]
            line(nc.scalar.activation(sq[:, :], xj, ACT.Square), sq_ready)

        def product(pe, n, out_ap, xs, i=None, waits=None, rows_of=None):
            pe.wait_ge(lo_ready, plus(i, 4, n + 1))
            last = None
            for k, (xh, xl) in enumerate(xs):
                if waits:
                    pe.wait_ge(waits[0], waits[1] + k)
                r = rows_of[k] if rows_of else P
                wh = w_hi[0:r, n % 2, k * P:(k + 1) * P]
                wl = w_lo[0:r, n % 2, k * P:(k + 1) * P]
                end = k == len(xs) - 1
                nc.tensor.matmul(out_ap, wh, xh, start=(k == 0), stop=False)
                nc.tensor.matmul(out_ap, wh, xl, start=False, stop=False)
                last = nc.tensor.matmul(out_ap, wl, xh, start=False, stop=end)
            last.then_inc(used, 1)

        H_TILES = [(h_hi[:, k, :], h_lo[:, k, :]) for k in range(KD)]

        def product_part(pe, n, bank, part, waits=None):
            if part == 0:
                pe.wait_ge(lo_ready, n + 1)
            for k in range(4 * part, 4 * part + 4):
                if waits:
                    pe.wait_ge(waits[0], waits[1] + k)
                xh, xl = H_TILES[k]
                wh, wl = w_hi[:, n % 2, k * P:(k + 1) * P], w_lo[:, n % 2, k * P:(k + 1) * P]
                nc.tensor.matmul(bank[:, :], wh, xh, start=(k == 0), stop=False)
                nc.tensor.matmul(bank[:, :], wh, xl, start=False, stop=False)
                last = nc.tensor.matmul(bank[:, :], wl, xh, start=False, stop=(k == KD - 1))
            if part == 1:
                last.then_inc(used, 1)

        def product_rows(pe, n, bank, width=P, waits=None):
            pe.wait_ge(lo_ready, n + 1)
            last = None
            for t in range(TT):
                o = bank[:, t * width:(t + 1) * width]
                for k in range(KD):
                    xh, xl = h_hi[:, k, t * P:(t + 1) * P], h_lo[:, k, t * P:(t + 1) * P]
                    wh = w_hi[:, n % 2, k * P:k * P + width]
                    wl = w_lo[:, n % 2, k * P:k * P + width]
                    nc.tensor.matmul(o, xh, wh, start=(k == 0), stop=False)
                    nc.tensor.matmul(o, xl, wh, start=False, stop=False)
                    last = nc.tensor.matmul(o, xh, wl, start=False, stop=(k == KD - 1))
            last.then_inc(used, 1)


        def norm_pe(pe, m):
            pe.wait_ge(sum_ready, KD * (m + 1))
            nc.tensor.matmul(B[5][:, :], ones[:, :], sumsq[:, :], start=True, stop=True).then_inc(rms_ps, 1)

        def norm_act(act, line, m, after):
            nc.scalar.preload_act_table_set("natural_log_exp_and_others")
            act.wait_ge(rms_ps, m + 1)
            line(nc.scalar.activation(lnt[:, :], B[5][:, :], ACT.Ln, bias=eps_c, scale=1.0 / D))
            line.settle()
            line(nc.scalar.activation(rstd[:, :], lnt[:, :], ACT.Exp, scale=-0.5), rstd_ready)
            if after:
                nc.scalar.preload_act_table(after)
            if m == 7:
                return
            for j in range(KD):
                act.wait_ge(t_ready, KD * m + j + 1)
                shift = mod[:, 24 * m + j:24 * m + j + 1] if m < 6 else small[:, 7:8]
                line(nc.scalar.activation(h_hi[:, j, :], tmp[:, j % 4, :], ACT.Identity, bias=shift), hhi_ready)

        def norm_dve(dve, line, m):
            if m < 6:
                line(nc.vector.tensor_scalar(scale_col[:, :], mod[:, 24 * m + 8:24 * m + 16], 1.0, None, ALU.add))
                line(nc.vector.tensor_scalar(gate_col[:, :], mod[:, 24 * m + 16:24 * m + 24],
                                             1.0 if m % 3 == 1 else 0.5, None, ALU.mult))
                line.settle()
                line(nc.vector.tensor_tensor(scale_col[:, :], scale_col[:, :], cols[:, 0, 8 * m:8 * m + 8], ALU.mult))
            else:
                line(nc.vector.tensor_copy(scale_col[:, :], cols[:, 0, 8 * m:8 * m + 8]))
                line(nc.vector.memset(gate_col[:, :], 1.0))
            dve.wait_ge(rms_ps, m + 1)
            line(nc.vector.memset(sumsq[:, :], 0.0))
            line.settle()
            dve.wait_ge(rstd_ready, m + 1)
            if m == 7:
                return

            def lower(j):
                dve.wait_ge(hhi_ready, KD * m + j + 1)
                shift = mod[:, 24 * m + j:24 * m + j + 1] if m < 6 else small[:, 7:8]
                line(nc.vector.scalar_tensor_tensor(out=h_lo[:, j, :], in0=tmp[:, j % 4, :], scalar=shift,
                                                    in1=h_hi[:, j, :].bitcast(F32), op0=ALU.add,
                                                    op1=ALU.subtract), h_ready)
            for j in range(KD):
                if j >= 4:
                    dve.wait_ge(h_ready, KD * m + j - 3)
                line(nc.vector.scalar_tensor_tensor(out=tmp[:, j % 4, :], in0=xT[:, j, :],
                                                    scalar=scale_col[:, j:j + 1], in1=rstd[:, :],
                                                    op0=ALU.mult, op1=ALU.mult), t_ready)
                if j:
                    lower(j - 1)
            lower(KD - 1)

        NORM_OF = {"F0": 0, "QKV": 1, "F1": 2, "F2": 3, "HIN": 4, "F3": 5, "P2": 6}
        RES_OF = {"F0": 1, "WO": 2, "F1": 3, "F2": 4, "HO": 5, "F3": 6, "OUT": 7}

        def ffn_pe(pe, name, fidx, q0, parts):
            n0 = FIRST[name]
            hb = KD * NORM_OF[name]

            def up(n, i, m, with_ada):
                for s in range(2):
                    pe.wait_ge(g_ready, plus(i, 2, 1 + KF * fidx + 2 * m + s))
                    for b in range(2):
                        product(pe, n + 2 * s + b, B[2 * s + b][:, :], H_TILES, i,
                                (h_ready, hb + 1) if s == b == 0 else None)
                if with_ada:
                    ada_pe(pe, q0 + m, i)
            if parts:
                with pe.Fori(0, parts) as i:
                    up(n0, i, 0, True)
            with pe.Fori(0, KF // 2 - parts) as i:
                up(n0 + 4 * parts, i, parts, False)
            pe.wait_ge(g_ready, 2 + KF * (fidx + 1))
            xb = KD * RES_OF[name]
            with pe.Fori(0, KD // 2) as i:
                for s in range(2):
                    pe.wait_ge(x_ready, plus(i, 2, xb + s - 1))
                    bank = B[s][:, :]
                    for b in range(2):
                        n = n0 + UP + 2 * s + b
                        pe.wait_ge(lo_ready, plus(i, 4, n + 1))
                        for k in range(KH):
                            f = b * KH + k
                            wh, wl = w_hi[:, n % 2, k * P:(k + 1) * P], w_lo[:, n % 2, k * P:(k + 1) * P]
                            nc.tensor.matmul(bank, wh, g_hi[:, f, :], start=(f == 0), stop=False)
                            nc.tensor.matmul(bank, wh, g_lo[:, f, :], start=False, stop=False)
                            last = nc.tensor.matmul(bank, wl, g_hi[:, f, :], start=False, stop=(f == KF - 1))
                        last.then_inc(used, 1)

        def ada_pe(pe, q, i=None):
            pe.wait_ge(ada_used, plus(i, 8, 8 * q + 8))
            for j in range(KD):
                col = B[4][:, bass.ds(plus(i, 8, 8 * q + j), 1)] if i is not None else B[4][:, 8 * q + j:8 * q + j + 1]
                last = nc.tensor.matmul(col, ada_total(q)[:, j * P:(j + 1) * P], ones[:, 0:1], start=True, stop=True)
            last.then_inc(ada_done, 1)

        def ada_total(q):
            return tmp[:, 0:2, :].rearrange("p a n -> p (a n)") if q == 1 else ada_sum[:, :]

        def ada_dve(dve, line, q, kk, i=None):
            total = ada_total(q)
            if q < 3:
                dve.wait_ge(ada_landed[kk % 4], 16 * (2 * q + kk // 4 + 1))
            else:
                dve.wait_ge(ada_landed_sw[kk % 4], plus(i, 32, 16 * (2 * (q - 3) + kk // 4 + 1)))
            if kk == 0:
                if q == 2:
                    dve.wait_ge(ada_done, 1)
                elif q > 2:
                    dve.wait_ge(ada_done, plus(i, 1, q))
                line(nc.vector.tensor_scalar(total, ada[:, 0, :], cact[:, 0:1], None, ALU.mult), ada_used)
            else:
                dve.wait_ge(ada_used, plus(i, 8, 8 * q + kk))
                line(nc.vector.scalar_tensor_tensor(out=total, in0=ada[:, kk % 4, :],
                                                    scalar=cact[:, kk:kk + 1], in1=total,
                                                    op0=ALU.mult, op1=ALU.add), ada_used)

        def ada_take(dve, line, q0, parts):
            dve.wait_ge(ada_done, q0 + parts)
            a, b = 8 * q0, 8 * (q0 + parts)
            m = min(b, P)
            if a < m:
                line(nc.vector.tensor_tensor(mod[:, a:m], B[4][:, a:m], cols[:, 1, a:m], ALU.add))
            if b > P:
                line(nc.vector.tensor_tensor(mod[:, P:b], B[4][:, P:b], cols[:, 0, C_AB:C_AB + b - P], ALU.add))
            line.settle()

        def ffn_act(act, line, name, fidx, parts):
            n0 = FIRST[name]

            def up(n, i, m):
                for s in range(2):
                    split_hi(act, line, n + 2 * s + 1, i)
                    split_hi(act, line, n + 2 * s + 2, i)
                    f0 = KF * fidx + 2 * m + s
                    act.wait_ge(used, plus(i, 4, n + 2 * s + 2))
                    if f0:
                        act.wait_ge(gt_ready, plus(i, 2, f0))
                    line(nc.scalar.activation(sq[:, :], B[2 * s][:, :], ACT.Silu), silu_ready)
                    act.wait_ge(gt_ready, plus(i, 2, f0 + 1))
                    fi = g_hi[:, bass.ds(plus(i, 2, 2 * m + s), 1), :].rearrange("p a n -> p (a n)")
                    line(nc.scalar.activation(fi, tmp[:, s, :], ACT.Copy), ghi_ready)
            if n0 == 0:
                up(n0, None, 0)
            k = 1 if n0 == 0 else 0
            line.loop(k, KF // 2 - 1, lambda i: up(n0 + 4 * k, i, k), ((hi_ready, 4), (silu_ready, 2), (ghi_ready, 2)))
            up(n0 + 4 * (KF // 2 - 1), None, KF // 2 - 1)
            xb = KD * RES_OF[name]

            def down(n, i, m):
                for s in range(2):
                    split_hi(act, line, n + 2 * s + 1, i)
                    split_hi(act, line, n + 2 * s + 2, i)
                    residual_act(act, line, xb + 2 * m + s + 1, 2 * m + s, i)
            line.loop(0, KD // 2 - 1, lambda i: down(n0 + UP, i, 0), ((hi_ready, 4), (sq_ready, 2)))
            down(n0 + UP + 4 * (KD // 2 - 1), None, KD // 2 - 1)

        def ffn_dve(dve, line, name, fidx, q0, parts):
            n0 = FIRST[name]

            def up(n, i, m, with_ada):
                for s in range(2):
                    split_lo(dve, line, n + 2 * s + 1, i)
                    if with_ada:
                        for kk in ((0, 1, 2), (5, 6, 7))[s]:
                            ada_dve(dve, line, q0 + m, kk, i)
                    split_lo(dve, line, n + 2 * s + 2, i)
                    f0 = KF * fidx + 2 * m + s
                    dve.wait_ge(silu_ready, plus(i, 2, f0 + 1))
                    dve.wait_ge(g_ready, plus(i, 2, f0 + 2))
                    line(nc.vector.tensor_tensor(tmp[:, s, :], sq[:, :], B[2 * s + 1][:, :], ALU.mult), gt_ready)
                    if with_ada:
                        for kk in ((3, 4), ())[s]:
                            ada_dve(dve, line, q0 + m, kk, i)
                    dve.wait_ge(ghi_ready, plus(i, 2, f0 + 1))
                    f = bass.ds(plus(i, 2, 2 * m + s), 1)
                    line(nc.vector.tensor_tensor(g_lo[:, f, :].rearrange("p a n -> p (a n)"), tmp[:, s, :],
                                                 g_hi[:, f, :].rearrange("p a n -> p (a n)").bitcast(F32),
                                                 ALU.subtract), g_ready)
            per = ((lo_ready, 4), (gt_ready, 2), (g_ready, 2))
            line.loop(0, parts, lambda i: up(n0, i, 0, True), per + ((ada_used, 8),))
            line.loop(parts, KF // 2 - 1, lambda i: up(n0 + 4 * parts, i, parts, False), per)
            up(n0 + 4 * (KF // 2 - 1), None, KF // 2 - 1, False)
            if parts:
                ada_take(dve, line, q0, parts)

            def down(n, i, m):
                for s in range(2):
                    split_lo(dve, line, n + 2 * s + 1, i)
                    split_lo(dve, line, n + 2 * s + 2, i)
                    residual_dve(dve, line, n + 2 * s + 1, 2 * m + s, i)
            line.loop(0, KD // 2 - 1, lambda i: down(n0 + UP, i, 0), ((lo_ready, 4), (x_ready, 2), (sum_ready, 2)))
            down(n0 + UP + 4 * (KD // 2 - 1), None, KD // 2 - 1)

        def back_pe(pe, name, ybase, tiles, rows_of=None, pair=None):
            xb = KD * RES_OF[name]
            for j in range(KD):
                if j >= 2:
                    pe.wait_ge(x_ready, xb + j - 1)
                if j == 0:
                    pe.wait_ge(y_ready, ybase)
                xs = [tuple(half[0:(rows_of[k] if rows_of else P)] for half in (pair or y_pair)(k)) for k in range(tiles)]
                product(pe, FIRST[name] + j, B[j % 2][:, :], xs, rows_of=rows_of)

        def back_act(act, line, name):
            for j in range(KD):
                split_hi(act, line, FIRST[name] + j + 1)
                residual_act(act, line, KD * RES_OF[name] + j + 1, j)

        def back_dve(dve, line, name):
            for j in range(KD):
                split_lo(dve, line, FIRST[name] + j + 1)
                residual_dve(dve, line, FIRST[name] + j, j)

        def score_bank(u, comps, cc):
            return B[3 + (cc if comps == 2 else u % 2)]

        def rows_pe(pe, base, heads, comps, q_of, k_of, v_of, o_rows, ready, extra):
            n = heads * TT
            at = at1 if comps == 2 else at2

            def step(u):
                if u < n:
                    h, i = divmod(u, TT)
                    w = (i + 1) * P
                    if i == 0:
                        ready(pe, h)
                    free = u - (1 if comps == 2 else 2)
                    if free >= 0:
                        pe.wait_ge(S_max, base + free + 1)
                    for cc in range(comps):
                        last = nc.tensor.matmul(score_bank(u, comps, cc)[:, 0:w], q_of(h, cc)[:, i * P:(i + 1) * P],
                                                k_of(h, cc)[:, 0:w], start=True, stop=True)
                    last.then_inc(S_ps, 1)
                if 2 <= u < n + 2:
                    m = u - 2
                    h, i = divmod(m, TT)
                    pe.wait_ge(a_ready, base + m + 1)
                    if m:
                        pe.wait_ge(aT_sb, base + m)
                    for k in range(i + 1):
                        last = nc.tensor.transpose(B[5][:, k * P:(k + 1) * P],
                                                   a_of(comps)[:, m % 3, 0, k * P:(k + 1) * P], ident[:, :])
                    last.then_inc(aT_ps, 1)
                if 3 <= u < n + 3:
                    m = u - 3
                    h, i = divmod(m, TT)
                    pe.wait_ge(aT_sb, base + m + 1)
                    if i == 0:
                        if comps == 2 and h:
                            pe.wait_ge(o_sq, h)
                        if comps == 1 and h and h % 2 == 0:
                            pe.wait_ge(o_sq, O2 + h // 2)
                    r = o_rows(h)
                    for k in range(i + 1):
                        last = nc.tensor.matmul(B[6][r, i * P:(i + 1) * P], v_of(h, k), at[:, m % 2, k * P:(k + 1) * P],
                                                start=(k == 0), stop=(k == i))
                    last.then_inc(pv_done, 1)
                for lag, f in extra:
                    if u >= lag and u - lag < n and (u - lag) % TT == TT - 1:
                        f((u - lag) // TT)
            return step

        def a_of(comps):
            return s1 if comps == 2 else s2

        def m_col(u, cc):
            return small[:, 24 + 2 * (u % 3) + cc:25 + 2 * (u % 3) + cc]

        def l_col(u, cc):
            return small[:, 32 + 2 * (u % 3) + cc:33 + 2 * (u % 3) + cc]

        def rows_dve(dve, line, base, heads, comps, extra):
            s_t = a_of(comps)
            toep = toep1 if comps == 2 else toep2
            n = heads * TT

            def maxima(u):
                h, i = divmod(u, TT)
                w = (i + 1) * P
                dve.wait_ge(S_ps, base + u + 1)
                if u >= 3:
                    dve.wait_ge(aT_ps, base + u - 2)
                for cc in range(comps):
                    bias = toep[:, h, T - w:T]
                    if comps == 2:
                        line(nc.vector.tensor_tensor_reduce(out=s_t[:, u % 3, cc, 0:w],
                                                            in0=score_bank(u, comps, cc)[:, 0:w],
                                                            in1=bias, scale=1.0, scalar=LOW, op0=ALU.add, op1=ALU.max,
                                                            accum_out=m_col(u, cc)))
                    else:
                        line(nc.vector.scalar_tensor_tensor(out=s_t[:, u % 3, 0, 0:w],
                                                            in0=score_bank(u, comps, cc)[:, 0:w],
                                                            scalar=HD ** -0.5, in1=bias, op0=ALU.mult, op1=ALU.add))
                        line.settle()
                        line(nc.vector.tensor_tensor_reduce(out=s_t[:, u % 3, 0, 0:w], in0=s_t[:, u % 3, 0, 0:w],
                                                            in1=chosen[:, i, 0:w], scale=1.0, scalar=LOW, op0=ALU.add,
                                                            op1=ALU.max, accum_out=m_col(u, 0)))
                line.settle()
                c0 = 24 + 2 * (u % 3)
                line(nc.vector.tensor_scalar(small[:, c0:c0 + comps], small[:, c0:c0 + comps], -1.0, None,
                                             ALU.mult), S_max)

            def weights(u):
                h, i = divmod(u, TT)
                w = (i + 1) * P
                dve.wait_ge(p_ready, base + u + 1)
                c0 = 32 + 2 * (u % 3)
                line(nc.vector.reciprocal(small[:, c0:c0 + comps], small[:, c0:c0 + comps]))
                line.settle()
                if comps == 1:
                    line(nc.vector.tensor_scalar(s_t[:, u % 3, 0, 0:w], s_t[:, u % 3, 0, 0:w], l_col(u, 0), None,
                                                 ALU.mult), a_ready)
                    return
                line(nc.vector.tensor_scalar(l_col(u, 1), l_col(u, 1), nlam_c, None, ALU.mult))
                line(nc.vector.tensor_scalar(s_t[:, u % 3, 0, 0:w], s_t[:, u % 3, 0, 0:w], l_col(u, 0), None, ALU.mult))
                line.settle()
                line(nc.vector.scalar_tensor_tensor(out=s_t[:, u % 3, 0, 0:w], in0=s_t[:, u % 3, 1, 0:w],
                                                    scalar=l_col(u, 1), in1=s_t[:, u % 3, 0, 0:w], op0=ALU.mult,
                                                    op1=ALU.add), a_ready)

            def step(u):
                if u < n:
                    maxima(u)
                if 1 <= u < n + 1:
                    weights(u - 1)
                for lag, f in extra:
                    if u >= lag and u - lag < n and (u - lag) % TT == TT - 1:
                        f((u - lag) // TT)
            return step

        def rows_act(act, line, base, pv_base, heads, comps, extra):
            s_t = a_of(comps)
            at = at1 if comps == 2 else at2
            n = heads * TT

            def step(u):
                if u < n:
                    h, i = divmod(u, TT)
                    w = (i + 1) * P
                    act.wait_ge(S_max, base + u + 1)
                    for cc in range(comps):
                        line(nc.scalar.activation(s_t[:, u % 3, cc, 0:w], s_t[:, u % 3, cc, 0:w], ACT.Exp,
                                                  bias=m_col(u, cc), accum_out=l_col(u, cc)),
                             p_ready if cc == comps - 1 else None)
                if 2 <= u < n + 2:
                    m = u - 2
                    w = (m % TT + 1) * P
                    act.wait_ge(aT_ps, base + m + 1)
                    if m >= 2:
                        act.wait_ge(pv_done, pv_base + m - 1)
                    line(nc.scalar.activation(at[:, m % 2, 0:w], B[5][:, 0:w], ACT.Copy), aT_sb)
                for lag, f in extra:
                    if u >= lag and u - lag < n and (u - lag) % TT == TT - 1:
                        f((u - lag) // TT)
            return step

        DRAIN = 10

        def head_out_act(act, line, m, osb, osq, pv):
            act.wait_ge(pv_done, pv)
            if m:
                act.wait_ge(o_ss, m)
                act.wait_ge(y_t, m)
            line(nc.scalar.activation(osb, B[6][:, :], ACT.Copy))
            line(nc.scalar.activation(osq, B[6][:, :], ACT.Square), o_sq)

        def head_rs_act(act, line, m, bank, ors):
            act.wait_ge(o_ss, m + 1)
            if m:
                act.wait_ge(y_t, m)
            line(nc.scalar.activation(ors, bank[:, :], ACT.Ln, bias=eps_c, scale=1.0 / P))
            line.settle()
            line(nc.scalar.activation(ors, ors, ACT.Exp, scale=-0.5), o_rs)

        def head_hi_act(act, line, m, hi, y):
            act.wait_ge(y_t, m + 1)
            line(nc.scalar.activation(hi, y, ACT.Copy), y_hi)

        def head_out_dve(dve, line, m, osb, gain, ors, y, gate=None, y1=None):
            dve.wait_ge(o_rs, m + 1)
            dve.wait_ge(y_ready, m)
            if gate is None:
                line(nc.vector.scalar_tensor_tensor(out=y, in0=osb, scalar=gain, in1=ors,
                                                    op0=ALU.mult, op1=ALU.mult), y_t)
            else:
                line(nc.vector.scalar_tensor_tensor(out=y1, in0=osb, scalar=gain, in1=ors,
                                                    op0=ALU.mult, op1=ALU.mult))
                line.settle()
                line(nc.vector.tensor_tensor(y, y1, gate, ALU.mult), y_t)

        def head_lo_dve(dve, line, m, hi, lo, y):
            dve.wait_ge(y_hi, m + 1)
            line(nc.vector.tensor_tensor(lo, y, hi.bitcast(F32), ALU.subtract), y_ready)

        O2 = 2 * HEADS + GH

        STEP_AT = (0, 1, 3, 4)

        def passes(heads, blocks, steps_at):
            out, u = [], 0
            for g in range(heads + 1):
                for half in range(2 * blocks):
                    b = g * blocks + half // 2 if g < heads else None
                    st = None
                    if g and half in steps_at:
                        st, u = u, u + 1
                    out.append((b, half % 2, st))
            return out

        def attention_pe(pe):
            n0 = FIRST["QKV"]

            def sums(h):
                pe.wait_ge(o_sq, h + 1)
                if h:
                    pe.wait_ge(o_rs, h)
                nc.tensor.matmul(B[7][:, :], ones[:, :], osq1[:, :], start=True, stop=True).then_inc(o_ss, 1)

            def aux(b):
                pe.wait_ge(headsq, b + 1)
                if b:
                    pe.wait_ge(headrs, b)
                if b % 3 < 2:
                    nc.tensor.matmul(B[2][:, :], halves[:, :], sq[:, :], start=True, stop=True).then_inc(headss, 1)
                else:
                    for c_ in range(TT):
                        s = slice(c_ * P, (c_ + 1) * P)
                        last = nc.tensor.transpose(B[2][:, s], avT[:, s], ident[:, :])
                    last.then_inc(headss, 1)

            def ready(pe, h):
                pe.wait_ge(headn, 2 * h + 2)
                pe.wait_ge(headrs, 3 * h + 3)
            step = rows_pe(pe, 0, HEADS, 2, lambda h, cc: aq[HD * cc:HD * cc + HD, h % 2, :],
                           lambda h, cc: ak[HD * cc:HD * cc + HD, h % 2, :],
                           lambda h, k: av[:, h % 2, k * P:(k + 1) * P], lambda h: slice(0, P), ready, ((5, sums),))
            for b, half, st in passes(HEADS, 3, STEP_AT):
                if b is not None:
                    if half == 0 and b >= 2:
                        pe.wait_ge(headsq, b - 1)
                    product_part(pe, n0 + b, B[b % 2], half, (h_ready, KD + 1) if b == 0 else None)
                    if half == 0 and b:
                        aux(b - 1)
                if b is None and st == TT * (HEADS - 1):
                    aux(3 * HEADS - 1)
                if st is not None:
                    step(st)
            for u in range(HEADS * TT, HEADS * TT + DRAIN):
                step(u)

        def attention_act(act, line):
            n0 = FIRST["QKV"]

            def aux(b):
                act.wait_ge(headss, b + 1)
                if b % 3 < 2:
                    m = 2 * (b // 3) + b % 3
                    if m:
                        act.wait_ge(headn, m)
                    line(nc.scalar.activation(lnt[:, :], B[2][:, :], ACT.Ln, bias=eps_c, scale=1.0 / HD))
                    line.settle()
                    line(nc.scalar.activation(rstd[:, :], lnt[:, :], ACT.Exp, scale=-0.5), headrs)
                else:
                    if b >= 6:
                        act.wait_ge(pv_done, TT * (b // 3 - 1))
                    line(nc.scalar.activation(av[:, (b // 3) % 2, :], B[2][:, :], ACT.Copy), headrs)

            def copy(b):
                h = b // 3
                act.wait_ge(used, n0 + b + 1)
                if b:
                    act.wait_ge(headss, b)
                if h >= 2:
                    act.wait_ge(S_ps, TT * (h - 1))
                if b % 3 < 2:
                    line(nc.scalar.activation((aq, ak)[b % 3][:, h % 2, :], B[b % 2][:, :], ACT.Copy))
                    line(nc.scalar.activation(sq[:, :], B[b % 2][:, :], ACT.Square), headsq)
                else:
                    line(nc.scalar.activation(avT[:, :], B[b % 2][:, :], ACT.Copy), headsq)
            step = rows_act(act, line, 0, 0, HEADS, 2,
                            ((4, lambda h: head_out_act(act, line, h, o1[:, h % 2, :], osq1[:, :], TT * (h + 1))),
                             (6, lambda h: head_rs_act(act, line, h, B[7], ors1[:, :])),
                             (8, lambda h: head_hi_act(act, line, h, y1_hi[:, h, :], tmp[:, 0, :]))))
            for b, half, st in passes(HEADS, 3, STEP_AT):
                if b is not None and half == 0:
                    split_hi(act, line, n0 + b + 1)
                    if b:
                        aux(b - 1)
                if b is None and st == TT * (HEADS - 1):
                    aux(3 * HEADS - 1)
                if st is not None:
                    step(st)
                if b is not None and half == 1:
                    copy(b)
            for u in range(HEADS * TT, HEADS * TT + DRAIN):
                step(u)

        def attention_dve(dve, line):
            n0 = FIRST["QKV"]

            def norm(b):
                if b % 3 == 2:
                    return
                dst = (aq, ak)[b % 3][:, (b // 3) % 2, :]
                gain = qg_c if b % 3 == 0 else cols[:, 0, C_KG:C_KG + 1]
                dve.wait_ge(headrs, b + 1)
                line(nc.vector.scalar_tensor_tensor(out=dst, in0=dst, scalar=gain, in1=rstd[:, :],
                                                    op0=ALU.mult, op1=ALU.mult), headn)
            step = rows_dve(dve, line, 0, HEADS, 2,
                            ((7, lambda h: head_out_dve(dve, line, h, o1[:, h % 2, :], subg_c, ors1[:, :],
                                                        tmp[:, 0, :])),
                             (9, lambda h: head_lo_dve(dve, line, h, y1_hi[:, h, :], y1_lo[:, h, :], tmp[:, 0, :]))))
            for b, half, st in passes(HEADS, 3, STEP_AT):
                if b is not None and half == 0:
                    split_lo(dve, line, n0 + b + 1)
                    if b:
                        norm(b - 1)
                if b == 3 and half == 0:
                    dve.wait_ge(toep_in, 16)
                if st is not None:
                    step(st)
            for u in range(HEADS * TT, HEADS * TT + DRAIN):
                step(u)

        def value_in(act, line, m, bank):
            if m >= 2:
                act.wait_ge(vt_ps, m - 1)
            line(nc.scalar.activation(tmp[:, m % 2, :], bank[:, :], ACT.Copy), epi_free)

        def value_turn(pe, m, copied):
            pe.wait_ge(epi_free, copied)
            if m >= 2:
                pe.wait_ge(vt_out, m - 1)
            for c_ in range(TT):
                s = slice(c_ * P, (c_ + 1) * P)
                last = nc.tensor.transpose(B[6 + m % 2][:, s], tmp[:, m % 2, s], ident[:, :])
            last.then_inc(vt_ps, 1)

        def value_out(act, line, m, dst):
            act.wait_ge(vt_ps, m + 1)
            line(nc.scalar.activation(dst, B[6 + m % 2][:, :].rearrange("p (t n) -> p t n", n=P), ACT.Copy), vt_out)

        def hin_pe(pe):
            n0 = FIRST["HIN"]
            for b, (kind, j) in enumerate(HORDER):
                if 4 <= b < 28:
                    pe.wait_ge(epi_free, b - 3)
                elif b >= 28:
                    pe.wait_ge(f_arg, b - 27)
                product(pe, n0 + b, B[b % 4][:, :], H_TILES, waits=(h_ready, KD * 4 + 1) if b == 0 else None)
                if b and HORDER[b - 1][0] == "v":
                    value_turn(pe, HORDER[b - 1][1], b)

        def hin_act(act, line):
            n0 = FIRST["HIN"]
            for b, (kind, j) in enumerate(HORDER):
                split_hi(act, line, n0 + b + 1)
                if b >= 2 and HORDER[b - 2][0] == "v":
                    m = HORDER[b - 2][1]
                    value_out(act, line, m, hv[:, :, m * P:(m + 1) * P])
                bank = B[b % 4]
                if kind == "f":
                    if j == 0:
                        nc.scalar.preload_act_table_set("natural_log_exp_and_others")
                    act.wait_ge(f_min, j + 1)
                    if j:
                        act.wait_ge(f_done, j)
                    line(nc.scalar.activation(tmp[:, 1, :], tmp[:, 0, :], ACT.Exp))
                    line.settle()
                    line(nc.scalar.activation(tmp[:, 2, :], tmp[:, 1, :], ACT.Ln, bias=one_c))
                    line(nc.scalar.activation(tmp[:, 3, :], tmp[:, 1, :], ACT.Ln, bias=one_c, scale=lb_c[:, j:j + 1]), f_log)
                    act.wait_ge(f_arg, j + 1)
                    line(nc.scalar.activation(tmp[:, 1, :], lnt[:, :], ACT.Exp), f_key)
                    continue
                act.wait_ge(used, n0 + b + 1)
                if kind == "q":
                    line(nc.scalar.activation(hq[:, j, :], bank[:, :], ACT.Copy), epi_free)
                elif kind == "g":
                    if j == 0:
                        nc.scalar.preload_act_table(ACT.Silu)
                    line(nc.scalar.activation(hg[:, j, :], bank[:, :], ACT.Silu), epi_free)
                else:
                    value_in(act, line, j, bank)

        def hin_dve(dve, line):
            n0 = FIRST["HIN"]
            dve.wait_ge(phase_const, 1)
            for b, (kind, j) in enumerate(HORDER):
                split_lo(dve, line, n0 + b + 1)
                if kind != "f":
                    continue
                bank = B[b % 4]
                if j == 0:
                    dve.wait_ge(vt_ps, HEADS)
                dve.wait_ge(used, n0 + b + 1)
                if j:
                    line.settle()
                line(nc.vector.tensor_scalar(tmp[:, 0, :], bank[:, :], -1.0, 40.0, ALU.mult, ALU.min), f_min)
                line(nc.vector.tensor_scalar(sumsq2[:, :], bank[:, :], -1.0, -40.0, ALU.mult, ALU.add))
                line.settle()
                dve.wait_ge(f_log, j + 1)
                line(nc.vector.scalar_tensor_tensor(out=tmp[:, 2, :], in0=sumsq2[:, :], scalar=0.0, in1=tmp[:, 2, :],
                                                    op0=ALU.max, op1=ALU.add))
                line.settle()
                line(nc.vector.scalar_tensor_tensor(out=lnt[:, :], in0=tmp[:, 2, :], scalar=-1.0, in1=bank[:, :],
                                                    op0=ALU.mult, op1=ALU.subtract), f_arg)
                line(nc.vector.tensor_tensor(tmp[:, 3, :], tmp[:, 3, :], tmp[:, 2, :], ALU.subtract))
                line.settle()
                line(nc.vector.tensor_tensor_scan(hG[:, j, :], reset[:, :], tmp[:, 3, :], 0.0, ALU.mult, ALU.add))
                dve.wait_ge(f_key, j + 1)
                line(nc.vector.tensor_scalar(hk[:, j, :], tmp[:, 1, :], lb1_c[:, j:j + 1], None, ALU.mult), f_done)

        sumsq2 = rstd

        def hgrn_pe(pe):
            nlev = LEVELS + 1
            pe.wait_ge(f_done, HEADS)
            pe.wait_ge(epi_free, 24)
            pe.wait_ge(vt_out, HEADS)
            pe.wait_ge(phase_const, 1)

            def score(h, v):
                n = h * nlev + v
                if n >= 2:
                    pe.wait_ge(lv_P, n - 1)
                if v < LEVELS:
                    m = h * LEVELS + v
                    pe.wait_ge(lv_q, m + 1)
                    pe.wait_ge(lv_k, m + 1)
                    qs, ks = hqE[:, m % 2, :], hkE[:, m % 2, :]
                else:
                    qs, ks = hq[:, h, :], hk[:, h, :]
                for c_ in range(TT):
                    s = slice(c_ * P, (c_ + 1) * P)
                    last = nc.tensor.matmul(B[n % 2][:, s], ks[:, s], qs[:, s], start=True, stop=True)
                last.then_inc(lv_S, 1)

            def output(h, v):
                n = h * nlev + v
                if v == 0:
                    if h:
                        pe.wait_ge(o_sq, HEADS + h)
                    nc.tensor.matmul(B[6][:, :], ones[:, :], zero[:, :], start=True, stop=False, skip_group_check=True)
                pe.wait_ge(lv_P, n + 1)
                for c_ in range(TT):
                    s = slice(c_ * P, (c_ + 1) * P)
                    last = nc.tensor.matmul(B[6][:, s], hv[:, c_, h * P:(h + 1) * P], hP[:, n % 2, s],
                                            start=False, stop=False, skip_group_check=True)
                last.then_inc(lv_O, 1)

            for h in range(HEADS):
                for v in range(nlev):
                    score(h, v)
                    if v:
                        output(h, v - 1)
                    if v == 4:
                        pe.wait_ge(st_k, 2 * h + 2)
                        if h:
                            pe.wait_ge(st_n, h)
                        for c_ in range(TT - 1):
                            s = slice(c_ * P, (c_ + 1) * P)
                            last = nc.tensor.transpose(B[4][:, s], hkd[:, s], ident[:, :])
                        last.then_inc(st_T, 1)
                    if v == 6:
                        pe.wait_ge(st_n, h + 1)
                        if h:
                            pe.wait_ge(st_s, 3 * h)
                        for c_ in range(TT - 1):
                            s = slice(c_ * P, (c_ + 1) * P)
                            last = nc.tensor.matmul(B[5][:, s], hkn[:, s], hv[:, c_, h * P:(h + 1) * P],
                                                    start=True, stop=True)
                        last.then_inc(st_U, 1)
                output(h, nlev - 1)
                pe.wait_ge(st_s, 3 * h + 3)
                for c_ in range(1, TT):
                    s = slice(c_ * P, (c_ + 1) * P)
                    last = nc.tensor.matmul(B[6][:, s], hst[c_ - 1], hqG[:, s], start=False,
                                            stop=(c_ == TT - 1), skip_group_check=True)
                last.then_inc(pv_done, 1)
                pe.wait_ge(o_sq, HEADS + h + 1)
                if h:
                    pe.wait_ge(o_rs, HEADS + h)
                nc.tensor.matmul(B[7][:, :], ones[:, :], sq[:, :], start=True, stop=True).then_inc(o_ss, 1)

        def hgrn_act(act, line):
            def finish_a(h):
                head_out_act(act, line, HEADS + h, ho[:, :], sq[:, :], pv_h(h) + 1)
                head_rs_act(act, line, HEADS + h, B[7], rstd[:, :])

            def finish_b(h):
                head_hi_act(act, line, HEADS + h, h_hi[:, h, :], tmp[:, 0, :])
            for h in range(HEADS):
                for v in range(LEVELS):
                    n = h * LEVELS + v
                    act.wait_ge(lv_D, n + 1)
                    line(nc.scalar.activation(hE[:, n % 2, :], hE[:, n % 2, :], ACT.Abs))
                    line.settle()
                    line(nc.scalar.activation(hE[:, n % 2, :], hE[:, n % 2, :], ACT.Exp, scale=-1.0), lv_E)
                    if v == 0:
                        if h:
                            act.wait_ge(st_k, 2 * h)
                            act.wait_ge(st_T, h)
                            act.wait_ge(st_s, 3 * h)
                        line(nc.scalar.activation(heG[:, :], hG[:, h, :], ACT.Exp))
                        for c_ in range(TT):
                            s = slice(c_ * P, (c_ + 1) * P)
                            line(nc.scalar.activation(hkd[:, s], hG[:, h, s], ACT.Exp, scale=-1.0,
                                                      bias=hG[:, h, (c_ + 1) * P - 1:(c_ + 1) * P]),
                                 st_E if c_ == TT - 1 else None)
                    if v == 1 and h:
                        finish_a(h - 1)
                    if v == 3 and h:
                        finish_b(h - 1)
                    if v == 5:
                        act.wait_ge(st_T, h + 1)
                        if h:
                            act.wait_ge(st_U, h)
                        line(nc.scalar.activation(hkn[:, 0:3 * P], B[4][:, 0:3 * P], ACT.Copy), st_n)
            finish_a(HEADS - 1)
            finish_b(HEADS - 1)

        def hgrn_dve(dve, line):
            nlev = LEVELS + 1
            dve.wait_ge(toep_in, 32)

            def dist(h, v):
                n = h * LEVELS + v
                if n >= 2:
                    dve.wait_ge(lv_k, n - 1)
                    dve.wait_ge(lv_q, n - 1)
                half = 1 << v
                Gv = hG[:, h, :].rearrange("p (b w) -> p b w", w=2 * half)
                ref = Gv[:, :, half - 1:half].broadcast_to((P, T // (2 * half), 2 * half))
                line(nc.vector.tensor_tensor(hE[:, n % 2, :].rearrange("p (b w) -> p b w", w=2 * half), Gv, ref,
                                             ALU.subtract), lv_D)

            def query(h, v):
                n = h * LEVELS + v
                dve.wait_ge(lv_E, n + 1)
                if n >= 2:
                    dve.wait_ge(lv_S, level_at(n - 2))
                line(nc.vector.tensor_tensor(hqE[:, n % 2, :], hq[:, h, :], hE[:, n % 2, :], ALU.mult), lv_q)

            def mask(h, v):
                n = h * nlev + v
                dve.wait_ge(lv_S, n + 1)
                if n >= 2:
                    dve.wait_ge(lv_O, n - 1)
                m = masks[:, v:v + 1, :].broadcast_to((P, TT, P))
                line(nc.vector.tensor_tensor(hP[:, n % 2, :].rearrange("p (c t) -> p c t", t=P),
                                             B[n % 2][:, :].rearrange("p (c t) -> p c t", t=P), m, ALU.mult), lv_P)

            def finish(h):
                head_out_dve(dve, line, HEADS + h, ho[:, :], cols[:, 0, C_HG + h:C_HG + h + 1], rstd[:, :], tmp[:, 0, :],
                             hg[:, h, :], tmp[:, 1, :])
                head_lo_dve(dve, line, HEADS + h, h_hi[:, h, :], h_lo[:, h, :], tmp[:, 0, :])
            for h in range(HEADS):
                if h == 0:
                    dist(0, 0)
                for v in range(nlev):
                    if v + 1 < LEVELS:
                        dist(h, v + 1)
                    elif v == LEVELS and h + 1 < HEADS:
                        dist(h + 1, 0)
                    if v < LEVELS:
                        query(h, v)
                    if v:
                        mask(h, v - 1)
                    if v == 3 and h:
                        finish(h - 1)
                mask(h, nlev - 1)
                dve.wait_ge(st_U, h + 1)
                if h:
                    dve.wait_ge(pv_done, pv_h(h))
                line(nc.vector.tensor_copy(hst[0], B[5][:, 0:P]), st_s)
                for c_ in range(1, TT - 1):
                    dve.wait_ge(st_s, 3 * h + c_)
                    line(nc.vector.scalar_tensor_tensor(out=hst[c_], in0=hst[c_ - 1],
                                                        scalar=heG[:, (c_ + 1) * P - 1:(c_ + 1) * P],
                                                        in1=B[5][:, c_ * P:(c_ + 1) * P], op0=ALU.mult, op1=ALU.add), st_s)
            finish(HEADS - 1)

        E2 = 24
        U2, PV2 = HEADS * TT, HEADS * TT + HEADS
        M2 = 2 * HEADS
        GATES = ("ggate", "dgate", "pgate")

        def second_pool(pool, line):
            g = nc.gpsimd
            line.settle()
            line(g.memset(w2[:, :, :], 0.0))
            line.settle()
            line(g.memset(poolw[:, :, :], 0.0))
            line.settle()
            line(g.memset(zero2[:, :], 0.0))
            line.settle()
            line(g.memset(reset2[:, :], 1.0))
            line.settle()
            line(g.memset(reset2[:, 0:T:64], 0.0), phase_const)
            for t in range(2):
                for m in range(2):
                    c0 = 2 * GK * t + GK * m
                    pool.dma_start(w2[:, t, 64 * m:64 * m + GK], gla_gate_w2_2[0, :, c0:c0 + GK]).then_inc(small_in, 16)
                    pool.dma_start(poolw[64 * m:64 * m + 64, t, 64 * m:64 * m + 64],
                                   pool_w_2[0, 2 * t + m, :, :]).then_inc(small_in, 16)
            pool.dma_start(poolc[:, :, :], pool_counts).then_inc(small_in, 16)
            for h in range(GH):
                pool.wait_ge(gl_a, h + 1)
                am = at2[:, h % 2, :].rearrange("p (t n) -> p t n", n=P)
                line.settle()
                line(g.affine_select(out=am, in_=am, compare_op=ALU.is_ge, fill=0.0, base=0,
                                     pattern=[[0, TT], [1, P]], channel_multiplier=-1))
                line.settle()
                line(g.memset(am[0:64, :, 64:P], 0.0), gl_m)
            for i in range(1, TT):
                pool.wait_ge(ix_a, IH * i)
                w = (i + 1) * P
                line.settle()
                line(g.affine_select(out=work[:, 4, 0:w], in_=work[:, 4, 0:w], compare_op=ALU.is_ge, fill=LOW,
                                     base=i * P, pattern=[[-1, w]], channel_multiplier=1), ix_c)

        def y_pair(k):
            return (h_hi[:, k, :], h_lo[:, k, :]) if k < KD else (y8_hi[:, :], y8_lo[:, :])

        def y_act(act, line, m, tile, r=P):
            act.wait_ge(y_t, m + 1)
            line(nc.scalar.activation(y_pair(tile)[0][0:r], tmp[0:r, 0, :], ACT.Copy), y_hi)

        def y_dve(dve, line, m, tile, r=P):
            dve.wait_ge(y_hi, m + 1)
            hi, lo = y_pair(tile)
            line(nc.vector.tensor_tensor(lo[0:r], tmp[0:r, 0, :], hi[0:r].bitcast(F32), ALU.subtract), y_ready)

        def values_before(b):
            return HEADS + sum(kind in NATURAL for kind, _, _ in SECOND[:b])

        def second_pe(pe):
            t_ = nc.tensor
            n0 = FIRST["P2"]
            for b, (kind, t, _) in enumerate(SECOND):
                if b >= 4:
                    pe.wait_ge(epi_free, E2 + b - 3)
                if kind == "wi":
                    product_rows(pe, n0 + b, B[b % 4], IH)
                else:
                    product(pe, n0 + b, B[b % 4][:, :], H_TILES, waits=(h_ready, KD * 6 + 1) if b == 0 else None)
                if b and SECOND[b - 1][0] in NATURAL:
                    value_turn(pe, values_before(b - 1), E2 + b)
            pe.wait_ge(epi_free, E2 + len(SECOND))
            pe.wait_ge(vt_out, values_before(len(SECOND)))
            pe.wait_ge(small_in, 16 * 9)
            for t in range(2):
                last = t_.matmul(B[t][:, :], w2[:, t, :], z["gz"][0:16, :], start=True, stop=True)
            last.then_inc(gl_z, 1)
            for t in range(2):
                pe.wait_ge(gl_q, t + 1)
                for c_ in range(TT):
                    s = slice(c_ * P, (c_ + 1) * P)
                    last = t_.transpose(B[4][:, s], work[:, t, s], ident[:, :])
                last.then_inc(gl_T, 1)
                pe.wait_ge(gl_n, t + 1)
                if t:
                    pe.wait_ge(gl_s, t)
                for ch in range(7):
                    r0, bank = 64 * (ch % 2), B[5 + 2 * (ch % 2)]
                    for r in range(2):
                        h = 2 * t + r
                        last = t_.matmul(bank[64 * r:64 * r + 64, (ch // 2) * GV:(ch // 2 + 1) * GV],
                                         work[r0:r0 + 64, 2 + t, (ch // 2) * P + 64 * r:(ch // 2) * P + 64 * r + 64],
                                         z["gv"][r0:r0 + 64, ch // 2, h * GV:(h + 1) * GV], start=True, stop=True)
                last.then_inc(gl_U, 1)
                for r in range(2):
                    h = 2 * t + r
                    rows_ = slice(64 * r, 64 * r + GK)
                    if h >= 2:
                        pe.wait_ge(gl_a, h - 1)
                    for c_ in range(TT):
                        s = slice(c_ * P, (c_ + 1) * P)
                        last = t_.matmul(B[h % 2][:, s], z["gk"][rows_, t, s], z["gq"][rows_, t, s],
                                         start=True, stop=True)
                    last.then_inc(gl_A, 1)
                for r in range(2):
                    h = 2 * t + r
                    rows_ = slice(64 * r, 64 * r + GK)
                    pe.wait_ge(gl_m, h + 1)
                    pe.wait_ge(gl_s, t + 1)
                    if h:
                        pe.wait_ge(o_sq, M2 + h)
                    for c_ in range(TT):
                        s = slice(c_ * P, (c_ + 1) * P)
                        t_.matmul(B[6][0:GV, s], z["gv"][:, c_, h * GV:(h + 1) * GV], at2[:, h % 2, s],
                                  start=True, stop=False)
                        for ch in (2 * c_, 2 * c_ + 1):
                            if ch:
                                last = t_.matmul(B[6][0:GV, ch * 64:(ch + 1) * 64], gst[rows_, ch, :],
                                                 z["gq"][rows_, t, ch * 64:(ch + 1) * 64], start=False,
                                                 stop=(ch % 2 == 1))
                    last.then_inc(pv_done, 1)
                    pe.wait_ge(o_sq, M2 + h + 1)
                    if h:
                        pe.wait_ge(o_rs, M2 + h)
                    t_.matmul(B[3][:, :], ones[0:GV, :], sq[0:GV, :], start=True, stop=True).then_inc(o_ss, 1)
            for t in range(2):
                pe.wait_ge(pl_d, t + 1)
                t_.matmul(B[2][:, :] if t else B[5][:, :], poolw[:, t, :], work[:, 4 + t, :],
                          start=True, stop=True).then_inc(pl_y, 1)
            pe.wait_ge(y_ready, M2 + GH + 2)
            for i in range(1, TT):
                if i > 1:
                    pe.wait_ge(ix_r, IH * (i - 1))
                for h in range(IH):
                    r = slice(32 * h, 32 * h + 32)
                    last = t_.matmul(B[h][:, 0:(i + 1) * P], z["qi"][r, i * P:(i + 1) * P],
                                     z["ki"][r, 0:(i + 1) * P], start=True, stop=True, tile_position=(32 * h, 0))
                last.then_inc(ix_S, 1)
            pe.wait_ge(ix_r, IH * (TT - 1))
            step = rows_pe(pe, U2, DH, 1,
                    lambda h, cc: z["dq"][64 * (h % 2):64 * (h % 2) + 64, h // 2, :],
                    lambda h, cc: z["dk"][64 * (h % 2):64 * (h % 2) + 64, h // 2, :],
                    lambda h, k: z["dv"][:, k, h * HD:(h + 1) * HD],
                    lambda h: slice(64 * (h % 2), 64 * (h % 2) + 64), lambda pe, h: None, ())
            for u in range(DH * TT + DRAIN):
                step(u)

        def second_act(act, line):
            s_ = nc.scalar
            n0 = FIRST["P2"]
            for b, (kind, t, _) in enumerate(SECOND):
                split_hi(act, line, n0 + b + 1)
                if b >= 2 and SECOND[b - 2][0] in NATURAL:
                    last_kind, last_t, _ = SECOND[b - 2]
                    value_out(act, line, values_before(b - 2), z[last_kind][:, :, last_t * P:(last_t + 1) * P])
                act.wait_ge(used, n0 + b + 1)
                bank = B[b % 4]
                if kind == "ggate" and t == 0:
                    nc.scalar.preload_act_table(ACT.Silu)
                if kind == "wi":
                    line(s_.activation(z["wi"][:, :, :], bank[:, 0:TT * IH].rearrange("p (t n) -> p t n", n=IH),
                                       ACT.Copy, scale=IH ** -0.5), epi_free)
                elif kind in NATURAL:
                    value_in(act, line, values_before(b), bank)
                else:
                    dst = z[kind][:, :] if kind in ("qi", "ki", "gz") else z[kind][:, t, :]
                    line(s_.activation(dst, bank[:, :], ACT.Silu if kind in GATES else ACT.Copy), epi_free)
            nc.scalar.preload_act_table_set("natural_log_exp_and_others")
            for t in range(2):
                act.wait_ge(gl_u, t + 1)
                line(s_.activation(tmp[:, 2 + t, :], tmp[:, 2 + t, :], ACT.Exp))
                line.settle()
                line(s_.activation(tmp[:, 2 + t, :], tmp[:, 2 + t, :], ACT.Ln, bias=one_c), gl_l)
            for t in range(2):
                act.wait_ge(gl_b, t + 1)
                if t:
                    act.wait_ge(gl_s, t)
                    act.wait_ge(gl_q, t)
                bt = tmp[:, t, :]
                line(s_.activation(gE[:, 0, :], bt, ACT.Exp, scale=-1.0 / 16))
                line(s_.activation(gE[:, 1, :], bt, ACT.Exp, scale=1.0 / 16))
                for ch in range(8):
                    s = slice(64 * ch, 64 * ch + 64)
                    line(s_.activation(gE[:, 2, s], tmp[:, t, s], ACT.Exp, scale=1.0 / 16,
                                       bias=gend[:, t, ch:ch + 1]), gl_e if ch == 7 else None)
                act.wait_ge(gl_T, t + 1)
                line(s_.activation(work[:, 2 + t, :], B[4][:, :], ACT.Copy), gl_n)
                for r in range(2):
                    h = 2 * t + r
                    act.wait_ge(gl_A, h + 1)
                    if h >= 2:
                        act.wait_ge(pv_done, PV2 + h - 1)
                    line(s_.activation(at2[:, h % 2, :], B[h % 2][:, :], ACT.Copy), gl_a)
                for r in range(2):
                    h = 2 * t + r
                    m = M2 + h
                    act.wait_ge(pv_done, PV2 + h + 1)
                    act.wait_ge(o_ss, m)
                    act.wait_ge(y_t, m)
                    line(s_.activation(o2[0:GV, 0, :], B[6][0:GV, :], ACT.Copy))
                    line(s_.activation(sq[0:GV, :], B[6][0:GV, :], ACT.Square), o_sq)
                    act.wait_ge(o_ss, m + 1)
                    line(s_.activation(lnt[0:GV, :], B[3][0:GV, :], ACT.Ln, bias=eps_c[0:GV], scale=1.0 / GV))
                    line.settle()
                    line(s_.activation(rstd[0:GV, :], lnt[0:GV, :], ACT.Exp, scale=-0.5), o_rs)
                    y_act(act, line, m, h, GV)
            bias_tiles(act, toep2[:, :, :], 1, DH)
            for t in range(2):
                y_act(act, line, M2 + GH + t, 7 + t)
            for i in range(1, TT):
                act.wait_ge(ix_S, i)
                if i > 1:
                    act.wait_ge(ix_a, IH * (i - 1))
                for h in range(IH):
                    line(s_.activation(work[:, h, 0:(i + 1) * P], B[h][:, 0:(i + 1) * P], ACT.Relu,
                                       scale=32.0 ** -0.5), ix_r)

            def out_pair(h):
                if h % 2 == 0:
                    return
                act.wait_ge(pv_done, PV2 + GH + TT * (h + 1))
                act.wait_ge(y_t, M2 + GH + 2 + h // 2)
                line(s_.activation(o2[:, (h // 2) % 2, :], B[6][:, :], ACT.Copy), o_sq)

            def hi_pair(h):
                if h % 2:
                    y_act(act, line, M2 + GH + 2 + h // 2, 4 + h // 2)
            step = rows_act(act, line, U2, PV2 + GH, DH, 1, ((4, out_pair), (7, hi_pair)))
            for u in range(DH * TT + DRAIN):
                step(u)

        def second_dve(dve, line):
            v_ = nc.vector
            n0 = FIRST["P2"]
            for b in range(len(SECOND)):
                split_lo(dve, line, n0 + b + 1)
            dve.wait_ge(gl_z, 1)
            dve.wait_ge(phase_const, 2)
            line.settle()
            for t in range(2):
                gb = cols[:, 0, C_GB + t:C_GB + t + 1]
                line(v_.tensor_scalar(tmp[:, t, :], B[t][:, :], gb, -1.0, ALU.add, ALU.mult))
                line.settle()
                line(v_.tensor_scalar(tmp[:, 2 + t, :], tmp[:, t, :], 40.0, None, ALU.min), gl_u)
            for t in range(2):
                line.settle()
                line(v_.tensor_scalar(work[:, t, :], tmp[:, t, :], -40.0, 0.0, ALU.add, ALU.max))
                line.settle()
                dve.wait_ge(gl_l, t + 1)
                line(v_.tensor_tensor(work[:, t, :], work[:, t, :], tmp[:, 2 + t, :], ALU.add))
                line.settle()
                line(v_.tensor_tensor_scan(tmp[:, t, :], reset2[:, :], work[:, t, :], 0.0, ALU.mult, ALU.add))
                line.settle()
                line(v_.tensor_scalar(gend[:, t, :], tmp[:, t, 63:T:64], -1.0 / 16, None, ALU.mult), gl_b)
            for t in range(2):
                dve.wait_ge(gl_e, t + 1)
                line(v_.scalar_tensor_tensor(out=z["gq"][:, t, :], in0=z["gq"][:, t, :], scalar=GK ** -0.5,
                                             in1=gE[:, 0, :], op0=ALU.mult, op1=ALU.mult))
                line(v_.tensor_tensor(work[:, t, :], z["gk"][:, t, :], gE[:, 2, :], ALU.mult))
                line.settle()
                line(v_.tensor_tensor(z["gk"][:, t, :], z["gk"][:, t, :], gE[:, 1, :], ALU.mult), gl_q)
                dve.wait_ge(gl_U, t + 1)
                if t:
                    dve.wait_ge(pv_done, PV2 + 2)
                line(v_.tensor_copy(gst[:, 1, :], B[5][:, 0:GV]))
                for ch in range(1, 7):
                    line.settle()
                    line(v_.scalar_tensor_tensor(out=gst[:, ch + 1, :], in0=gst[:, ch, :],
                                                 scalar=gE[:, 0, 64 * ch + 63:64 * ch + 64],
                                                 in1=B[5 + 2 * (ch % 2)][:, (ch // 2) * GV:(ch // 2 + 1) * GV],
                                                 op0=ALU.mult, op1=ALU.add), gl_s if ch == 6 else None)
                for r in range(2):
                    h = 2 * t + r
                    m = M2 + h
                    dve.wait_ge(o_rs, m + 1)
                    dve.wait_ge(y_ready, m)
                    gain = cols[0:GV, 0, C_GN:C_GN + 1]
                    line(v_.scalar_tensor_tensor(out=sumsq[0:GV, :], in0=o2[0:GV, 0, :], scalar=gain,
                                                 in1=rstd[0:GV, :], op0=ALU.mult, op1=ALU.mult))
                    line.settle()
                    line(v_.tensor_tensor(tmp[0:GV, 0, :], sumsq[0:GV, :], z["ggate"][0:GV, h, :], ALU.mult), y_t)
                    y_dve(dve, line, m, h, GV)
            for t in range(2):
                u = z["pu"][:, t, :]
                at, src, size = 0, u, 1
                sums = []
                line.settle()
                for _ in range(2 if t == 0 else 4):
                    dst = gE[:, at % 3, :] if at < 3 else o2[:, 1, :]
                    line(v_.tensor_copy(dst[:, 0:size], src[:, 0:size]))
                    line(v_.tensor_tensor(dst[:, size:T], src[:, size:T], src[:, 0:T - size], ALU.add))
                    line.settle()
                    src, size, at = dst, 2 * size, at + 1
                    sums.append((dst, size))
                for r in range(2):
                    s_w, w = sums[-2 + r]
                    p = slice(64 * r, 64 * r + 64)
                    line(v_.scalar_tensor_tensor(out=work[p, 4 + t, 16:T], in0=s_w[p, 16:T], scalar=1.0 / w,
                                                 in1=u[p, 16:T], op0=ALU.mult, op1=ALU.subtract))
                    line(v_.tensor_tensor(work[p, 4 + t, 0:16], s_w[p, 0:16], poolc[p, t, :], ALU.mult))
                    line.settle()
                    line(v_.tensor_tensor(work[p, 4 + t, 0:16], work[p, 4 + t, 0:16], u[p, 0:16], ALU.subtract),
                         pl_d if r else None)
            for t in range(2):
                m = M2 + GH + t
                dve.wait_ge(pl_y, t + 1)
                dve.wait_ge(y_ready, m)
                line(v_.scalar_tensor_tensor(out=tmp[:, 0, :], in0=B[2][:, :] if t else B[5][:, :],
                                             scalar=cols[:, 0, C_PS + t:C_PS + t + 1], in1=z["pgate"][:, t, :],
                                             op0=ALU.mult, op1=ALU.mult), y_t)
                y_dve(dve, line, m, 7 + t)
            line(v_.memset(chosen[:, 0, 0:P], 0.0))
            for i in range(1, TT):
                w = (i + 1) * P
                score = work[:, 4, 0:w]
                for h in range(IH):
                    dve.wait_ge(ix_r, IH * (i - 1) + h + 1)
                    wc = z["wi"][:, i, h:h + 1]
                    line.settle()
                    if h == 0:
                        line(v_.tensor_scalar(score, work[:, 0, 0:w], wc, None, ALU.mult), ix_a)
                    else:
                        line(v_.scalar_tensor_tensor(out=score, in0=work[:, h, 0:w], scalar=wc, in1=score,
                                                     op0=ALU.mult, op1=ALU.add), ix_a)
                dve.wait_ge(ix_c, i)
                src = score
                for r in range(TOPK // 8):
                    line.settle()
                    line(v_.max(eight[:, :], src))
                    if r < TOPK // 8 - 1:
                        line.settle()
                        line(v_.match_replace(work[:, 5, 0:w], eight[:, :], src, -3.3e38))
                        src = work[:, 5, 0:w]
                line.settle()
                line(v_.tensor_scalar(tmp[:, 0, 0:w], score, eight[:, 7:8], None, ALU.is_gt))
                line(v_.tensor_scalar(tmp[:, 1, 0:w], score, eight[:, 7:8], None, ALU.is_equal))
                line.settle()
                line(v_.tensor_reduce(small[:, 57:58], tmp[:, 0, 0:w], AX_X, ALU.add))
                line(v_.tensor_tensor_scan(tmp[:, 2, 0:w], tmp[:, 1, 0:w], zero2[:, 0:w], 0.0, ALU.add, ALU.add))
                line.settle()
                line(v_.tensor_scalar(small[:, 58:59], small[:, 57:58], -1.0, float(TOPK), ALU.mult, ALU.add))
                line.settle()
                line(v_.scalar_tensor_tensor(out=tmp[:, 3, 0:w], in0=tmp[:, 2, 0:w], scalar=small[:, 58:59],
                                             in1=tmp[:, 1, 0:w], op0=ALU.is_le, op1=ALU.mult))
                line.settle()
                line(v_.tensor_tensor(tmp[:, 3, 0:w], tmp[:, 3, 0:w], tmp[:, 0, 0:w], ALU.add))
                line.settle()
                line(v_.tensor_scalar(chosen[:, i, 0:w], tmp[:, 3, 0:w], 1.0, -NEG, ALU.subtract, ALU.mult))
            dve.wait_ge(toep_in, 48)
            line.settle()

            def gate_pair(h):
                if h % 2 == 0:
                    return
                m = M2 + GH + 2 + h // 2
                dve.wait_ge(o_sq, O2 + h // 2 + 1)
                dve.wait_ge(y_ready, m)
                line(v_.tensor_tensor(tmp[:, 0, :], o2[:, (h // 2) % 2, :], z["dgate"][:, h // 2, :], ALU.mult), y_t)

            def lo_pair(h):
                if h % 2:
                    y_dve(dve, line, M2 + GH + 2 + h // 2, 4 + h // 2)
            step = rows_dve(dve, line, U2, DH, 1, ((6, gate_pair), (8, lo_pair)))
            for u in range(DH * TT + DRAIN):
                step(u)

        @block.sync
        def _(sp):
            sp.dma_start(x_rows[:, :, :], x[0].rearrange("(t p) d -> p t d", p=P)).then_inc(setup2, 16)

            def slot(n, k):
                return raw[:, n % 4, 0:k * P].rearrange("p (k n) -> p k n", n=P)

            def load(n, src, i=None, k=KD):
                if n >= 4 or i is not None:
                    sp.wait_ge(lo_ready, plus(i, 4, n - 3))
                sp.dma_start(slot(n, k), src).then_inc(landed[n % 4], 16)

            for q in range(3):
                for kk in range(8):
                    load_ada(sp, q, kk, 0, slice(q * D, (q + 1) * D))

            def feed_forward(name, l, s, q0, parts):
                n0 = FIRST[name]

                def up(n, i, m, with_ada):
                    for b in range(4):
                        col = bass.ds(plus(i, 2 * P, m * 2 * P + (b // 2) * P + (b % 2) * FF), P)
                        load(n + b, up_v[l, s, :, :, col], i)

                k = 0
                if n0 == 0:
                    up(0, None, 0, True)
                    k = 1
                if parts > k:
                    with sp.Fori(0, parts - k) as i:
                        up(n0 + 4 * k, i, k, True)
                    k = parts
                with sp.Fori(0, KF // 2 - k) as i:
                    up(n0 + 4 * k, i, k, False)
                with sp.Fori(0, KD // 2) as i:
                    for b in range(4):
                        load(n0 + UP + b, down_v[l, s, b % 2, :, :, bass.ds(plus(i, 2 * P, (b // 2) * P), P)], i, KH)

            def plain(name, view, count, width=None):
                with sp.Fori(0, count // 4) as i:
                    for b in range(4):
                        load(FIRST[name] + b, view[:, :, bass.ds(plus(i, 4 * P, b * P), P)], i)

            feed_forward(*FFN[0])
            with sp.Fori(0, 2) as i:
                for b in range(12):
                    sp.wait_ge(lo_ready, plus(i, 12, FIRST["QKV"] + b - 3))
                    sp.dma_start(slot(b, KD), qkv_v[0][:, :, bass.ds(plus(i, 4 * P, (b % 3) * D + (b // 3) * P), P)])\
                        .then_inc(landed[b % 4], 16)
            plain("WO", wo_v[0], KD)
            feed_forward(*FFN[1])
            feed_forward(*FFN[2])
            for b, (kind, j) in enumerate(HORDER):
                col = HCOL[kind] * D + j * P
                load(FIRST["HIN"] + b, hin_v[0][:, :, col:col + P])
            plain("HO", ho_v[0], KD)
            feed_forward(*FFN[3])
            extra = 0
            for b, (kind, t, pieces) in enumerate(SECOND):
                n = FIRST["P2"] + b
                sp.wait_ge(lo_ready, n - 3)
                for m, (col, width, at) in enumerate(pieces):
                    sp.dma_start(slot(n, KD)[:, :, at:at + width],
                                 in2_v[0][:, :, col:col + width]).then_inc(landed[n % 4], 16)
            for j in range(KD):
                n = FIRST["OUT"] + j
                sp.wait_ge(lo_ready, n - 3)
                sp.dma_start(slot(n, 9)[0:GV, 0:GH, :],
                             w_out_2[0, 0:GH * GV, j * P:(j + 1) * P].rearrange("(k p) n -> p k n", p=GV))\
                    .then_inc(landed[n % 4], 16)
                sp.dma_start(slot(n, 9)[:, GH:9, :],
                             w_out_2[0, GH * GV:, j * P:(j + 1) * P].rearrange("(k p) n -> p k n", p=P))\
                    .then_inc(landed[n % 4], 16)
            for t in range(TT):
                sp.wait_ge(fin_sb, 2 * (t + 1))
                sp.dma_start(out[0, t * P:(t + 1) * P, :], tmp_out(t)).then_inc(out_done[t % 2], 16)
            for i in range(2):
                sp.wait_ge(out_done[i], 16 * TT // 2)

        @block.gpsimd
        def _(pool):
            line = Line(pool, pool_own)
            g = nc.gpsimd
            line.settle()
            line(g.memset(rows[:, :, :], 0.0))
            line.settle()
            line(g.memset(table[:, :], NEG))
            line.settle()
            line(g.memset(ident[:, :], 0.0))
            line.settle()
            line(g.memset(ones[:, :], 1.0))
            line.settle()
            line(g.memset(halves[:, :], 0.0))
            line.settle()
            line(g.memset(sumsq[:, :], 0.0))
            line.settle()
            line(g.memset(small[:, :], 0.0))
            line.settle()
            line(g.affine_select(out=ident[:, :], in_=ident[:, :], compare_op=ALU.not_equal, fill=1.0, base=0,
                                 pattern=[[-1, P]], channel_multiplier=1))
            line.settle()
            line(g.memset(halves[0:HD, 0:HD], 1.0))
            line.settle()
            line(g.memset(halves[HD:P, HD:P], 1.0))
            line.settle()
            line(g.memset(small[:, 0:1], EPS))
            line.settle()
            line(g.memset(small[:, 1:2], 1.0))
            line.settle()
            line(g.memset(small[:, 7:8], 0.0), const_ready)
            line.settle()
            r = rows[:, 0, :]

            def small_load(dst, src):
                pool.dma_start(dst, src).then_inc(setup, 16)

            small_load(r[0:48, :], norm_g.rearrange("l s (k p) -> (l s k) p", p=P))
            small_load(r[48:56, :], norm_g_2.rearrange("l (k p) -> (l k) p", p=P))
            small_load(r[56:64, :], final_norm_g_2.rearrange("(k p) -> k p", p=P))
            small_load(r[64:72, :], c.rearrange("b (k p) -> (b k) p", p=P))
            small_load(r[72:80, :], hgrn_out_gain.rearrange("b (k p) -> (b k) p", p=P))
            small_load(r[80:88, :], hgrn_lb_logits.rearrange("b (k p) -> (b k) p", p=P))
            small_load(r[88:89, :], attn_subln_gain)
            small_load(r[89:91, :], pool_scale_2.rearrange("b (k p) -> (b k) p", p=P))
            for m in range(2):
                small_load(r[91:92, HD * m:HD * m + HD], attn_q_gain)
                small_load(r[92:93, HD * m:HD * m + HD], attn_k_gain)
                for t in range(2):
                    small_load(r[93 + t:94 + t, 64 * m:64 * m + GK],
                               gla_gate_b_2[:, 2 * GK * t + GK * m:2 * GK * t + GK * m + GK])
            small_load(r[95:96, 0:GV], gla_norm_g_2)
            ada_b_rows = ada_b.rearrange("l (k p) -> (l k) p", p=P)
            small_load(r[96:112, :], ada_b_rows[128:144, :])
            small_load(rows[:, 1, :], ada_b_rows[0:128, :])
            small_load(table[:, 0:640], bucket_rows)
            small_load(table[0:32, 640:648], rel_bias)
            small_load(table[0:32, 648:654], rel_bias_2)
            small_load(lamb[:, :, :], attn_lambda[0].rearrange("(a r) d -> a r d", a=1).broadcast_to((P, 4, HD)))
            ada_loads(pool, 3, 6)
            ada_loads(pool, 9, 9)
            hgrn_pool(pool, line)
            pool.wait_ge(used, FIRST["P2"])
            second_pool(pool, line)

        @block.scalar
        def _(act):
            line = Line(act, act_own)
            s = nc.scalar
            act.wait_ge(const_ready, 1)
            act.wait_ge(cols_ready, 1)
            line(s.activation(cact[:, :], cols[:, 0, C_C:C_C + 8], ACT.Silu), cact_ready)
            act.wait_ge(cols_ready, 2)
            nc.scalar.preload_act_table_set("natural_log_exp_and_others")
            line(s.activation(small[:, 44:46], small[:, 42:44], ACT.Exp), cact_ready)
            line(s.activation(small[:, 48:56], small[:, 8:16], ACT.Exp), cact_ready)
            act.wait_ge(bias_sb, 4)
            for m, heads in ((0, HEADS), (1, DH)):
                act.dma_start(bias_dram.ap()[m, 0:heads, :, :],
                              bias_row[0:heads, m:m + 1, :].broadcast_to((heads, P, 640))).then_inc(bias_out, 16)
            for j in range(KD):
                act.wait_ge(x_ready, j + 1)
                line(s.activation(sq[:, :], xT[:, j, :], ACT.Square), sq_ready)
            split_hi(act, line, 0)
            norm_act(act, line, 0, ACT.Silu)
            act.wait_ge(bias_out, 32)
            ffn_act(act, line, "F0", 0, 6)
            norm_act(act, line, 1, None)
            bias_tiles(act, toep1[:, :, :], 0, HEADS)
            attention_act(act, line)
            back_act(act, line, "WO")
            norm_act(act, line, 2, ACT.Silu)
            ffn_act(act, line, "F1", 1, 9)
            norm_act(act, line, 3, ACT.Silu)
            ffn_act(act, line, "F2", 2, 0)
            norm_act(act, line, 4, None)
            act.dma_start(masks[:, :, :], level_masks.rearrange("p (l t) -> p l t", t=P)).then_inc(toep_in, 16)
            hin_act(act, line)
            hgrn_act(act, line)
            back_act(act, line, "HO")
            norm_act(act, line, 5, ACT.Silu)
            ffn_act(act, line, "F3", 3, 0)
            norm_act(act, line, 6, None)
            second_act(act, line)
            back_act(act, line, "OUT")
            norm_act(act, line, 7, None)
            for t in range(TT):
                act.wait_ge(fin_ps, t + 1)
                if t >= 2:
                    act.wait_ge(out_done[t % 2], 16 * (t // 2))
                for hf in range(2):
                    line(s.activation(tmp[:, 2 * (t % 2) + hf, :], B[2 * (t % 2) + hf][:, :], ACT.Copy), fin_sb)

        @block.vector
        def _(dve):
            line = Line(dve, dve_own)
            v = nc.vector
            dve.wait_ge(turned, 1)
            line(v.tensor_copy(cols[:, :, :], B[7][:, 0:2 * P].rearrange("p (a n) -> p a n", n=P)), cols_ready)
            line.settle()
            for m in range(2):
                line(v.tensor_tensor(lnt[:, m * HD:(m + 1) * HD], lamb[:, 2 * m, :], lamb[:, 2 * m + 1, :], ALU.mult))
            line.settle()
            line(v.tensor_reduce(small[:, 42:44], lnt[:, 0:2 * HD].rearrange("p (a n) -> p a n", n=HD), AX_X, ALU.add))
            line(v.tensor_tensor(lb_c, cols[:, 0, C_LB:C_LB + 8], cols[:, 0, C_LB:C_LB + 8], ALU.subtract))
            line(v.tensor_scalar(qg_c, cols[:, 0, C_QG:C_QG + 1], HD ** -0.5, None, ALU.mult))
            line(v.tensor_scalar(subg_c, cols[:, 0, C_SUB:C_SUB + 1], 1.0 - LAMBDA_INIT, None, ALU.mult))
            for col in (41, 46):
                line(v.memset(small[:, col:col + 1], 0.0), g_ready)
            line.settle()
            line(v.memset(small[:, 47:48], 0.0), cols_ready)
            for m, heads in ((0, HEADS), (1, DH)):
                dve.wait_ge(bias_ps, 2 * m + 1)
                line(v.tensor_copy(bias_row[0:heads, m, 0:T], B[0 + m][0:heads, :]), bias_sb)
                dve.wait_ge(bias_ps, 2 * m + 2)
                line(v.tensor_copy(bias_row[0:heads, m, T:640], B[2 + m][0:heads, 0:P]), bias_sb)
            dve.wait_ge(cact_ready, 3)
            line(v.tensor_tensor(small[:, 56:57], small[:, 45:46], small[:, 44:45], ALU.subtract))
            line(v.reciprocal(small[:, 16:24], small[:, 48:56]))
            line.settle()
            line(v.tensor_scalar(nlam_c, small[:, 56:57], LAMBDA_INIT, None, ALU.subtract))
            line(v.tensor_tensor(small[:, 48:56], small[:, 48:56], small[:, 16:24], ALU.mult))
            line.settle()
            line(v.tensor_tensor(lb_c, small[:, 48:56], small[:, 48:56], ALU.subtract))
            line.settle()
            line(v.tensor_scalar(lb1_c, lb_c, -1.0, 1.0, ALU.mult, ALU.add))
            for j in range(KD):
                dve.wait_ge(x_turned, j + 1)
                line(v.tensor_copy(xT[:, j, :], B[j % 4][:, :]), x_ready)
                ada_dve(dve, line, 0, j)
                dve.wait_ge(sq_ready, j + 1)
                line(v.tensor_tensor(sumsq[:, :], sumsq[:, :], sq[:, :], ALU.add), sum_ready)
            for q in (1, 2):
                for kk in range(8):
                    ada_dve(dve, line, q, kk)
            split_lo(dve, line, 0)
            ada_take(dve, line, 0, 3)
            norm_dve(dve, line, 0)
            dve.wait_ge(bias_out, 32)
            ffn_dve(dve, line, "F0", 0, 3, 6)
            norm_dve(dve, line, 1)
            attention_dve(dve, line)
            back_dve(dve, line, "WO")
            norm_dve(dve, line, 2)
            ffn_dve(dve, line, "F1", 1, 9, 9)
            norm_dve(dve, line, 3)
            ffn_dve(dve, line, "F2", 2, 0, 0)
            norm_dve(dve, line, 4)
            hin_dve(dve, line)
            hgrn_dve(dve, line)
            back_dve(dve, line, "HO")
            norm_dve(dve, line, 5)
            ffn_dve(dve, line, "F3", 3, 0, 0)
            norm_dve(dve, line, 6)
            second_dve(dve, line)
            back_dve(dve, line, "OUT")
            norm_dve(dve, line, 7)
            for j in range(KD):
                line(v.scalar_tensor_tensor(out=xT[:, j, :], in0=xT[:, j, :], scalar=scale_col[:, j:j + 1],
                                            in1=rstd[:, :], op0=ALU.mult, op1=ALU.mult), fin_t)

        @block.tensor
        def _(pe):
            t = nc.tensor
            pe.wait_ge(const_ready, 1)
            pe.wait_ge(setup, 16 * 23)
            t.transpose(B[7][:, 0:P], rows[:, 0, :], ident[:, :])
            t.transpose(B[7][:, P:2 * P], rows[:, 1, :], ident[:, :]).then_inc(turned, 1)
            for m, heads in ((0, HEADS), (1, DH)):
                rb = table[:, 640 + 8 * m:640 + 8 * m + heads]
                t.matmul(B[0 + m][0:heads, :], rb, table[:, 0:T], start=True, stop=True).then_inc(bias_ps, 1)
                t.matmul(B[2 + m][0:heads, 0:P], rb, table[:, T:640], start=True, stop=True).then_inc(bias_ps, 1)
            pe.wait_ge(bias_sb, 4)
            pe.wait_ge(setup2, 16)
            for j in range(KD):
                if j >= 4:
                    pe.wait_ge(x_ready, j - 3)
                for tt in range(TT):
                    last = t.transpose(B[j % 4][:, tt * P:(tt + 1) * P], x_rows[:, tt, j * P:(j + 1) * P], ident[:, :])
                last.then_inc(x_turned, 1)
            for q in range(3):
                ada_pe(pe, q)
            norm_pe(pe, 0)
            ffn_pe(pe, "F0", 0, 3, 6)
            norm_pe(pe, 1)
            attention_pe(pe)
            back_pe(pe, "WO", HEADS, KD, None, lambda k: (y1_hi[:, k, :], y1_lo[:, k, :]))
            norm_pe(pe, 2)
            ffn_pe(pe, "F1", 1, 9, 9)
            norm_pe(pe, 3)
            ffn_pe(pe, "F2", 2, 0, 0)
            norm_pe(pe, 4)
            hin_pe(pe)
            hgrn_pe(pe)
            back_pe(pe, "HO", 2 * HEADS, KD)
            norm_pe(pe, 5)
            ffn_pe(pe, "F3", 3, 0, 0)
            norm_pe(pe, 6)
            second_pe(pe)
            back_pe(pe, "OUT", 2 * HEADS + 9, 9, [GV] * GH + [P] * 5)
            norm_pe(pe, 7)
            pe.wait_ge(fin_t, KD)
            for tt in range(TT):
                if tt >= 2:
                    pe.wait_ge(fin_sb, 2 * (tt - 1))
                for j in range(KD):
                    last = t.transpose(B[2 * (tt % 2) + j // 4][:, (j % 4) * P:(j % 4 + 1) * P],
                                       xT[:, j, tt * P:(tt + 1) * P], ident[:, :])
                last.then_inc(fin_ps, 1)


def bucket_table():
    import math
    import numpy as np
    dist = 511 - np.arange(640)
    d = np.maximum(dist, 0)
    large = 16 + (np.log(np.maximum(d, 1).astype(np.float32) / 16) / math.log(128 / 16) * 16).astype(np.int32)
    bucket = np.where(d < 16, d, np.minimum(large, 31))
    bucket = np.where(dist < 0, 32, bucket)
    return (np.arange(33)[:, None] == bucket[None, :]).astype(np.float32)


def halving_masks():
    import numpy as np
    s, t = np.arange(128)[:, None], np.arange(128)[None, :]
    m = np.zeros((128, 8, 128), np.float32)
    for v in range(7):
        half = 1 << v
        m[:, v, :] = (s // (2 * half) == t // (2 * half)) & (s % (2 * half) < half) & (t % (2 * half) >= half)
    m[:, 7, :] = s == t
    return m.reshape(128, 1024)


def window_counts():
    import numpy as np
    w = np.array([[2, 4], [8, 16]], np.float32)
    out = np.zeros((128, 2, 16), np.float32)
    for t in range(2):
        for g in range(2):
            out[64 * g:64 * g + 64, t, :] = 1.0 / np.minimum(np.arange(16) + 1, w[t, g])
    return out


_INS = ['x', 'c', 'ada_w', 'ada_b', 'norm_g', 'ffn_w_in', 'ffn_w_down', 'attn_w_qkv', 'attn_w_o', 'attn_q_gain',
        'attn_k_gain', 'attn_lambda', 'attn_subln_gain', 'rel_bias', 'hgrn_w_in', 'hgrn_w_o', 'hgrn_out_gain',
        'hgrn_lb_logits', 'norm_g_2', 'w_in_2', 'gla_gate_w2_2', 'gla_gate_b_2', 'gla_norm_g_2', 'rel_bias_2',
        'pool_w_2', 'pool_scale_2', 'w_out_2', 'final_norm_g_2']


def kernel(**inputs):
    import numpy as _np
    import concourse.bacc as _bacc
    from concourse import mybir as _mybir
    from concourse.bass_utils import run_bass_kernel_spmd as _run

    nc = _bacc.Bacc("TRN2", target_bir_lowering=False, num_devices=1, dynamic_dma_scratch_size=2048)
    arrays, args = {}, []
    feeds = [(name, _np.ascontiguousarray(inputs[name])) for name in _INS]
    feeds += [("bucket_rows", bucket_table()), ("level_masks", halving_masks()), ("pool_counts", window_counts())]
    for name, a in feeds:
        arrays[f"in_{name}"] = a
        args.append(nc.dram_tensor(f"in_{name}", a.shape, _mybir.dt.from_np(a.dtype), kind="ExternalInput").ap())
    args.append(nc.dram_tensor("out_0", (1, T, D), F32, kind="ExternalOutput").ap())
    program(nc, *args)
    r = _run(nc, [arrays], core_ids=[0])
    return r.results[0]["out_0"]
```
